# Optimizing a Trainium2 kernel written in Bass

```python
import jax, jax.numpy as jnp
from jax import lax
import numpy as np

D_MODEL = 1024
BATCH = 1
SEQ = 1024
DEPTH = 1

N_MIXERS = 2
MLA_HEADS = 16
Q_LORA = 384
KV_LORA = 256
QK_NOPE = 64
QK_ROPE = 32
V_HEAD = 64
ROPE_THETA = 10000.0
Q_BLOCK = 128
MLA_IN = Q_LORA + KV_LORA + QK_ROPE
POOL_WINDOWS = (2, 4, 8, 16)
POOL_GROUPS = len(POOL_WINDOWS)
POOL_GROUP_DIM = D_MODEL // POOL_GROUPS
MOE_GROUPS = 4
EXPERTS_PER_GROUP = 8
N_EXPERTS = MOE_GROUPS * EXPERTS_PER_GROUP
MOE_TOP_K = 2
EXPERT_FF = D_MODEL // 4
DN_ALPHA = (2.0 * DEPTH) ** 0.25
DN_BETA = (8.0 * DEPTH) ** -0.25
LN_EPS = 1e-5
RMS_EPS = 1e-6
N_MLA_LAYERS = (DEPTH + N_MIXERS - 1) // N_MIXERS
N_POOL_LAYERS = DEPTH // N_MIXERS

kernel_name = 'hybrid_mla_pool_hmoe_deepnorm_adaln'

def _layer_norm(x, g, b):
    xf = x.astype(jnp.float32)
    mu = jnp.mean(xf, axis=-1, keepdims=True)
    var = jnp.mean(jnp.square(xf - mu), axis=-1, keepdims=True)
    return ((xf - mu) * lax.rsqrt(var + LN_EPS) * g + b).astype(x.dtype)

def _rms_norm(x, g):
    xf = x.astype(jnp.float32)
    return (xf * lax.rsqrt(jnp.mean(jnp.square(xf), axis=-1, keepdims=True) + RMS_EPS) * g).astype(x.dtype)

def _rope_angles(positions):
    inv = 1.0 / (ROPE_THETA ** (jnp.arange(0, QK_ROPE, 2, dtype=jnp.float32) / QK_ROPE))
    ang = positions.astype(jnp.float32)[..., None] * inv
    return jnp.cos(ang), jnp.sin(ang)

def _apply_rope(x, cos, sin):
    x1, x2 = jnp.split(x.astype(jnp.float32), 2, axis=-1)
    return jnp.concatenate([x1 * cos - x2 * sin, x1 * sin + x2 * cos], axis=-1).astype(x.dtype)

def _mla(h, positions, w_in, q_norm_g, kv_norm_g, w_uq, w_ukv, w_o):
    B, S, _ = h.shape
    z = h @ w_in
    q_lat = _rms_norm(z[..., :Q_LORA], q_norm_g)
    kv_lat = _rms_norm(z[..., Q_LORA:Q_LORA + KV_LORA], kv_norm_g)
    cos, sin = _rope_angles(positions)
    k_rope = _apply_rope(z[..., Q_LORA + KV_LORA:], cos, sin)
    q = (q_lat @ w_uq).reshape(B, S, MLA_HEADS, QK_NOPE + QK_ROPE)
    q_nope = q[..., :QK_NOPE]
    q_rope = _apply_rope(q[..., QK_NOPE:], cos[:, :, None, :], sin[:, :, None, :])
    kv = (kv_lat @ w_ukv).reshape(B, S, MLA_HEADS, QK_NOPE + V_HEAD)
    k_nope, v = kv[..., :QK_NOPE], kv[..., QK_NOPE:]
    nb = S // Q_BLOCK
    qn_b = q_nope.reshape(B, nb, Q_BLOCK, MLA_HEADS, QK_NOPE).transpose(1, 0, 2, 3, 4)
    qr_b = q_rope.reshape(B, nb, Q_BLOCK, MLA_HEADS, QK_ROPE).transpose(1, 0, 2, 3, 4)
    starts = jnp.arange(nb, dtype=jnp.int32) * Q_BLOCK
    key_pos = jnp.arange(S, dtype=jnp.int32)
    scale = (QK_NOPE + QK_ROPE) ** -0.5

    def block(args):
        qn, qr, start = args
        s = jnp.einsum('bqhd,bkhd->bhqk', qn, k_nope) + jnp.einsum('bqhr,bkr->bhqk', qr, k_rope)
        s = s.astype(jnp.float32) * scale
        q_pos = start + jnp.arange(Q_BLOCK, dtype=jnp.int32)
        s = jnp.where(key_pos[None, :] <= q_pos[:, None], s, -jnp.inf)
        p = jax.nn.softmax(s, axis=-1).astype(v.dtype)
        return jnp.einsum('bhqk,bkhd->bqhd', p, v)

    o = lax.map(block, (qn_b, qr_b, starts))
    o = o.transpose(1, 0, 2, 3, 4).reshape(B, S, MLA_HEADS * V_HEAD)
    return o @ w_o

def _pool_mixer(h, w_pool, pool_scale):
    B, S, D = h.shape
    hf = h.astype(jnp.float32)
    cs = jnp.cumsum(hf, axis=1)
    count = jnp.arange(1, S + 1, dtype=jnp.float32)[None, :, None]
    outs = []
    for gi, w in enumerate(POOL_WINDOWS):
        sl = slice(gi * POOL_GROUP_DIM, (gi + 1) * POOL_GROUP_DIM)
        cg = cs[..., sl]
        shifted = jnp.pad(cg, ((0, 0), (w, 0), (0, 0)))[:, :S]
        mean = (cg - shifted) / jnp.minimum(count, w)
        outs.append(mean - hf[..., sl])
    mixed = jnp.stack(outs, axis=2).astype(h.dtype)
    y = jnp.einsum('bsgc,gcd->bsgd', mixed, w_pool).reshape(B, S, D)
    return y * pool_scale

def _hier_moe(h, w_gr, b_gr, w_er, b_er, w_gate, w_up, w_down):
    B, S, D = h.shape
    N = B * S
    t = h.reshape(N, D)
    g_prob = jax.nn.softmax((t @ w_gr + b_gr).astype(jnp.float32), axis=-1)
    g_p, g_idx = lax.top_k(g_prob, 1)
    e_logits = (t @ w_er + b_er).astype(jnp.float32).reshape(N, MOE_GROUPS, EXPERTS_PER_GROUP)
    sel = jnp.broadcast_to(g_idx[:, :, None], (N, 1, EXPERTS_PER_GROUP))
    e_in_group = jnp.take_along_axis(e_logits, sel, axis=1)[:, 0]
    e_top, e_idx = lax.top_k(e_in_group, MOE_TOP_K)
    e_w = jax.nn.softmax(e_top, axis=-1) * g_p
    expert_id = g_idx * EXPERTS_PER_GROUP + e_idx
    gates = jnp.sum(jax.nn.one_hot(expert_id, N_EXPERTS, dtype=jnp.float32) * e_w[..., None], axis=1)
    out = jnp.zeros((N, D), jnp.float32)
    for e in range(N_EXPERTS):
        he = jax.nn.silu(t @ w_gate[e]) * (t @ w_up[e])
        out = out + gates[:, e:e + 1] * (he @ w_down[e]).astype(jnp.float32)
    return out.astype(h.dtype).reshape(B, S, D)

def setup_inputs(seed: int = 0) -> dict:
    key = jax.random.key(seed)
    ks = jax.random.split(key, 24)
    f32 = jnp.float32

    def nrm(k, shape, scale):
        return jax.random.normal(k, shape, f32) * scale

    offsets = jax.random.randint(ks[2], (BATCH, 1), 0, 1024, dtype=jnp.int32)
    positions = (offsets + jnp.arange(SEQ, dtype=jnp.int32)[None, :]).astype(jnp.int32)
    return {
        'x': nrm(ks[0], (BATCH, SEQ, D_MODEL), 1.0),
        'c': nrm(ks[1], (BATCH, D_MODEL), 1.0),
        'positions': positions,
        'w_mod': nrm(ks[3], (DEPTH, D_MODEL, 6 * D_MODEL), 0.5 * D_MODEL ** -0.5),
        'b_mod': nrm(ks[4], (DEPTH, 6 * D_MODEL), 0.01),
        'ln_g': 1.0 + nrm(ks[5], (DEPTH, 2, D_MODEL), 0.02),
        'ln_b': nrm(ks[6], (DEPTH, 2, D_MODEL), 0.01),
        'w_in': nrm(ks[7], (N_MLA_LAYERS, D_MODEL, MLA_IN), D_MODEL ** -0.5),
        'q_norm_g': 1.0 + nrm(ks[8], (N_MLA_LAYERS, Q_LORA), 0.02),
        'kv_norm_g': 1.0 + nrm(ks[9], (N_MLA_LAYERS, KV_LORA), 0.02),
        'w_uq': nrm(ks[10], (N_MLA_LAYERS, Q_LORA, MLA_HEADS * (QK_NOPE + QK_ROPE)), Q_LORA ** -0.5),
        'w_ukv': nrm(ks[11], (N_MLA_LAYERS, KV_LORA, MLA_HEADS * (QK_NOPE + V_HEAD)), KV_LORA ** -0.5),
        'w_o': nrm(ks[12], (N_MLA_LAYERS, MLA_HEADS * V_HEAD, D_MODEL), DN_BETA * (MLA_HEADS * V_HEAD) ** -0.5),
        'w_pool': nrm(ks[13], (N_POOL_LAYERS, POOL_GROUPS, POOL_GROUP_DIM, POOL_GROUP_DIM), DN_BETA * POOL_GROUP_DIM ** -0.5),
        'pool_scale': 1.0 + nrm(ks[14], (N_POOL_LAYERS, D_MODEL), 0.1),
        'w_group_router': nrm(ks[15], (DEPTH, D_MODEL, MOE_GROUPS), D_MODEL ** -0.5),
        'b_group_router': nrm(ks[16], (DEPTH, MOE_GROUPS), 0.01),
        'w_expert_router': nrm(ks[17], (DEPTH, D_MODEL, N_EXPERTS), D_MODEL ** -0.5),
        'b_expert_router': nrm(ks[18], (DEPTH, N_EXPERTS), 0.01),
        'w_gate': nrm(ks[19], (DEPTH, N_EXPERTS, D_MODEL, EXPERT_FF), D_MODEL ** -0.5),
        'w_up': nrm(ks[20], (DEPTH, N_EXPERTS, D_MODEL, EXPERT_FF), D_MODEL ** -0.5),
        'w_down': nrm(ks[21], (DEPTH, N_EXPERTS, EXPERT_FF, D_MODEL), DN_BETA * EXPERT_FF ** -0.5),
    }

def reference(x, c, positions, w_mod, b_mod, ln_g, ln_b, w_in, q_norm_g, kv_norm_g, w_uq, w_ukv, w_o,
              w_pool, pool_scale, w_group_router, b_group_router, w_expert_router, b_expert_router,
              w_gate, w_up, w_down):
    c_act = jax.nn.silu(c)
    for i in range(DEPTH):
        mod = (c_act @ w_mod[i] + b_mod[i])[:, None, :]
        sh1, sc1, g1, sh2, sc2, g2 = jnp.split(mod, 6, axis=-1)
        j = i // N_MIXERS
        h = x * (1.0 + sc1) + sh1
        if i % N_MIXERS == 0:
            y = _mla(h, positions, w_in[j], q_norm_g[j], kv_norm_g[j], w_uq[j], w_ukv[j], w_o[j])
        else:
            y = _pool_mixer(h, w_pool[j], pool_scale[j])
        x = _layer_norm(DN_ALPHA * x + (1.0 + g1) * y, ln_g[i, 0], ln_b[i, 0])
        h = x * (1.0 + sc2) + sh2
        y = _hier_moe(h, w_group_router[i], b_group_router[i], w_expert_router[i], b_expert_router[i],
                      w_gate[i], w_up[i], w_down[i])
        x = _layer_norm(DN_ALPHA * x + (1.0 + g2) * y, ln_g[i, 1], ln_b[i, 1])
    return x


_drawn_inputs = setup_inputs


def setup_inputs(seed=0):
    import zlib

    import numpy as np

    out = dict(_drawn_inputs(seed))
    spreads = {}
    factors = {'b_mod': 4.036,
     'ln_b': 3.02,
     'q_norm_g': 8.0,
     'kv_norm_g': 6.839,
     'b_group_router': 7.327,
     'b_expert_router': 5.462}
    for name, (base, spread) in spreads.items():
        noise = np.random.default_rng([zlib.crc32(name.encode()), seed]).standard_normal(out[name].shape)
        drawn = base * np.exp(spread * noise) if base else spread * noise
        out[name] = __import__('jax').numpy.asarray(drawn.astype(out[name].dtype))
    for name, factor in factors.items():
        out[name] = (out[name] * factor).astype(out[name].dtype)
    return out
```

```python
from contextlib import ExitStack

import numpy as np
import concourse.bass as bass
from concourse import mybir

F32, BF16, I32, U32 = mybir.dt.float32, mybir.dt.bfloat16, mybir.dt.int32, mybir.dt.uint32
ALU = mybir.AluOpType
ACT = mybir.ActivationFunctionType
AX = mybir.AxisListType

P = 128
D = 1024
S = 1024
T = S // P
KD = D // P
H = 16
QL, KVL, NOPE, ROPE, VH = 384, 256, 64, 32, 64
HR = ROPE // 2
ZW = QL + KVL + ROPE
QH = NOPE + ROPE
KVH = NOPE + VH
G, EPG = 4, 8
E = G * EPG
FF = 256
TOPK = 2
TILES_MAX = E + TOPK * S // P
LOOP_TABLE = TILES_MAX + 4
SCALE = float(QH) ** -0.5
ALPHA = float(2.0 ** 0.25)
LN_EPS, RMS_EPS = 1e-5, 1e-6
BIG = 3.0e38
TWO_PI = 2.0 * np.pi
TWO_PI_HI = 6.28125
TWO_PI_MID = float(np.float32(np.round((TWO_PI - TWO_PI_HI) * 2 ** 21) / 2 ** 21))
TWO_PI_LO = float(np.float32(TWO_PI - TWO_PI_HI - TWO_PI_MID))
ROUND = 1.5 * 2.0 ** 23
PI_F = 3.1415925


def build_trunk(nc, x, c, positions, w_mod, b_mod, ln_g, ln_b, w_in, q_norm_g, kv_norm_g, w_uq, w_ukv, w_o,
                w_gr, b_gr, w_er, b_er, w_gate, w_up, w_down, out):
    inv_freq = (1.0 / np.float32(10000.0) ** (np.arange(0, ROPE, 2, dtype=np.float32) / np.float32(ROPE))).astype(np.float32)
    h2_rows = nc.dram_tensor("h2_rows", [S, D], F32, kind="Internal").ap()
    y_rows = nc.dram_tensor("y_rows", [TOPK * S, D], F32, kind="Internal").ap()

    ctx = ExitStack()
    with ctx:
        def sb(name, shape, dt=F32):
            return ctx.enter_context(nc.sbuf_tensor(name, shape, dt))

        def sem(name):
            return ctx.enter_context(nc.semaphore(name))

        PS = ctx.enter_context(nc.psum_tensor("banks", [P, 8, 512], F32))

        reg_x = sb("reg_x", [P, T * D])
        reg_h = sb("reg_h", [P, T * D])
        reg_mod = sb("reg_mod", [P, 6 * D])
        reg_up = sb("reg_up", [P, 3 * H * QH + 2 * H * KVH])
        reg_lat = sb("reg_lat", [P, 5 * D])
        reg_work = sb("reg_work", [P, 11264])

        x_tok = reg_x[:].rearrange("p (t d) -> p t d", t=T)
        wo_sb = reg_x[:].rearrange("p (k d) -> p k d", k=KD)
        hT = reg_h[:].rearrange("p (k s) -> p k s", k=KD)
        o_tok = reg_h[:].rearrange("p (t d) -> p t d", t=T)
        xa = o_tok
        acc = reg_mod[:]
        wuq_sb = reg_up[:, 0:3 * H * QH].rearrange("p (k n) -> p k n", k=3)
        wukv_sb = reg_up[:, 3 * H * QH:].rearrange("p (k n) -> p k n", k=2)
        qlatT = reg_lat[:, 0:3 * D].rearrange("p (k s) -> p k s", k=3)
        kvlatT = reg_lat[:, 3 * D:5 * D].rearrange("p (k s) -> p k s", k=2)
        g1p, A2, B2, Ga, Ba = (reg_lat[:, i * D:(i + 1) * D] for i in range(5))

        at = [0]

        def work(n):
            at[0] += n
            assert at[0] <= 11264
            return reg_work[:, at[0] - n:at[0]]

        win_sb = work(KD * ZW).rearrange("p (k n) -> p k n", k=KD)
        MOD_BUFS = 4
        mod_w = [reg_up[:, i * 2 * D:(i + 1) * 2 * D] for i in range(MOD_BUFS)]
        zs = [work(ZW) for _ in range(2)]
        sq_junk = work(QL)
        k_rope = work(T * ROPE).rearrange("p (t r) -> p t r", t=T)
        k_rot = work(T * ROPE).rearrange("p (t r) -> p t r", t=T)
        rope_k = work(4 * T * HR).rearrange("p (a t r) -> p a t r", a=4, t=T)
        at[0] = 0
        kT = [work(S) for _ in range(2)]
        qT = [work(S) for _ in range(2)]
        v_h = [work(T * VH).rearrange("p (t d) -> p t d", t=T) for _ in range(2)]
        k_h = work(T * NOPE).rearrange("p (t d) -> p t d", t=T)
        q_h = work(T * QH).rearrange("p (t d) -> p t d", t=T)
        rope_tmp = work(4 * T * HR).rearrange("p (a t r) -> p a t r", a=4, t=T)
        probs = [work(S) for _ in range(2)]
        pT = [work(S).rearrange("p (b q) -> p b q", b=T) for _ in range(2)]
        at[0] = 0
        oT = [work(D).rearrange("p (k q) -> p k q", k=KD) for _ in range(2)]
        h2T = work(D).rearrange("p (k q) -> p k q", k=KD)
        xs = [work(D) for _ in range(2)]
        r_buf = [work(D) for _ in range(2)]
        h2 = [work(D) for _ in range(2)]
        g2p = work(D)
        at[0] = 0
        xg = [work(D) for _ in range(2)]
        xgT = [work(D).rearrange("p (k q) -> p k q", k=KD) for _ in range(2)]
        he = [work(FF) for _ in range(2)]
        heT = [work(FF).rearrange("p (k q) -> p k q", k=2) for _ in range(2)]
        sil = [work(FF) for _ in range(2)]
        y_e = [work(D) for _ in range(2)]
        assert at[0] <= 9 * D
        lng2, lnb2 = reg_lat[:, 0:D], reg_lat[:, D:2 * D]
        te_cmp = reg_lat[0:1, 2 * D:2 * D + LOOP_TABLE * E].rearrange("p (j e) -> p j e", e=E)
        place = reg_lat[:, 4 * D:4 * D + T * E].rearrange("p (t e) -> p t e", e=E)
        picked = reg_lat[:, 4 * D + T * E:4 * D + 3 * T * E].rearrange("p (a t e) -> p a t e", a=TOPK, e=E)
        hot = reg_x[:, 7 * D:7 * D + TOPK * T * E].rearrange("p (a t e) -> p a t e", a=TOPK, t=T)
        over = reg_x[:, 7 * D + TOPK * T * E:7 * D + 3 * T * E].rearrange("p (e t) -> p e t", t=T)
        wgu = [reg_mod[:, 0:KD * 2 * FF].rearrange("p (k n) -> p k n", k=KD),
               reg_up[:, 0:KD * 2 * FF].rearrange("p (k n) -> p k n", k=KD)]
        wdn = [reg_mod[:, KD * 2 * FF:KD * 2 * FF + 2 * D].rearrange("p (k n) -> p k n", k=2),
               reg_up[:, KD * 2 * FF:KD * 2 * FF + 2 * D].rearrange("p (k n) -> p k n", k=2)]
        ya = [reg_x[:, i * D:(i + 1) * D] for i in range(2)]
        yb = [reg_x[:, (2 + i) * D:(3 + i) * D] for i in range(2)]
        yo = [reg_x[:, (4 + i) * D:(5 + i) * D] for i in range(2)]
        r2 = [reg_x[:, (6 + i) * D:(7 + i) * D] for i in range(2)]

        ident = sb("ident", [P, P])
        ones = sb("ones", [P, P])
        ident_bf = sb("ident_bf", [P, P], BF16)
        causal_bf = sb("causal_bf", [P, P], BF16)
        before_bf = sb("before_bf", [P, P], BF16)
        ones_bf = sb("ones_bf", [P, P], BF16)
        iota_row = sb("iota_row", [P, P])
        iota_tiles = sb("iota_tiles", [P, T])
        row_id = sb("row_id", [P, TOPK * T])
        freq = sb("freq", [P, HR])
        c_col = sb("c_col", [P, KD])
        c_act = sb("c_act", [P, KD])
        mod_cols = sb("mod_cols", [P, 2 * KD])
        qg_col = sb("qg_col", [P, 3])
        kvg_col = sb("kvg_col", [P, 2])
        pos_i = sb("pos_i", [P, T], I32)
        pos_f = sb("pos_f", [P, T])
        ang = sb("ang", [P, T, HR])
        turns = sb("turns", [P, T, HR])
        cos_t = sb("cos_t", [P, T, HR])
        sin_t = sb("sin_t", [P, T, HR])
        ms = sb("ms", [P, T, 2])
        rms = sb("rms", [P, T, 2])
        rrms = sb("rrms", [P, T, 2])
        eps_rms = sb("eps_rms", [P, 1])
        eps_ln = sb("eps_ln", [P, 1])
        neg_max = sb("neg_max", [P, T])
        row_sum = sb("row_sum", [P, 2 * T])
        inv_sum = sb("inv_sum", [P, T])
        bn = sb("bn", [P, 2, 6])
        mv = sb("mv", [P, 2 * T, 2])
        std = sb("std", [P, 2 * T])
        rstd = sb("rstd", [P, 2 * T])
        shift = sb("shift", [P, T])
        w_rt = sb("w_rt", [P, KD, G + E])
        b_rt = sb("b_rt", [P, G + E])
        logits = sb("logits", [P, T, G + E])
        gl = sb("gl", [P, T, 8])
        g_top = sb("g_top", [P, T, 8])
        g_idx = sb("g_idx", [P, T, 8], U32)
        g_idf = sb("g_idf", [P, T])
        g_exp = sb("g_exp", [P, T, G])
        g_den = sb("g_den", [P, T])
        g_p = sb("g_p", [P, T])
        g_hot = sb("g_hot", [P, T, G])
        e_sel = sb("e_sel", [P, G, EPG])[:]
        e_in = sb("e_in", [P, T, EPG])
        e_top = sb("e_top", [P, T, 8])
        e_idx = sb("e_idx", [P, T, 8], U32)
        e_idf = sb("e_idf", [P, TOPK, T])
        e_dif = sb("e_dif", [P, T])
        e_exp = sb("e_exp", [P, T])
        e_den = sb("e_den", [P, T])
        wts = sb("wts", [P, TOPK, T])
        member = sb("member", [P, T, E], BF16)
        count = sb("count", [P, E])
        n_tiles = sb("n_tiles", [P, E])
        tile_end = sb("tile_end", [P, E])
        base = sb("base", [P, E])
        slot = sb("slot", [P, TOPK, T])
        row_f = sb("row_f", [P, LOOP_TABLE])
        pad = sb("pad", [P, LOOP_TABLE])
        slot_w = sb("slot_w", [P, LOOP_TABLE])
        past = sb("past", [P, LOOP_TABLE])
        slot_in = sb("slot_in", [P, TOPK, T])
        slot_dv = sb("slot_dv", [P, TOPK, T])
        hot_in = [sb(f"hot_in{i}", [P, P]) for i in range(2)]
        hot_dv = [sb(f"hot_dv{i}", [P, 2, TILES_MAX]) for i in range(2)]
        idx_f = sb("idx_f", [P, LOOP_TABLE])
        idx_u = sb("idx_u", [P, LOOP_TABLE], U32)
        dst_u = sb("dst_u", [P, LOOP_TABLE], U32)
        idx_now = [sb(f"idx_now{i}", [P, 1], U32) for i in range(2)]
        dst_now = [sb(f"dst_now{i}", [P, 1], U32) for i in range(2)]
        te_f = sb("te_f", [1, LOOP_TABLE])
        te_i = sb("te_i", [1, LOOP_TABLE], I32)
        rounds_f = sb("rounds_f", [1, 2])
        rounds_i = sb("rounds_i", [1, 1], I32)

        consts = sem("consts")
        ld_x = sem("ld_x")
        ld_small = sem("ld_small")
        ld_bmod = sem("ld_bmod")
        acc_zero = sem("acc_zero")
        ld_mod = [sem(f"ld_mod{i}") for i in range(MOD_BUFS)]
        mod_done = sem("mod_done")
        c_ready = sem("c_ready")
        ld_win = sem("ld_win")
        ld_up = sem("ld_up")
        ld_wo = sem("ld_wo")
        xT_done = sem("xT_done")
        xT_out = sem("xT_out")
        cols_done = sem("cols_done")
        cols_out = sem("cols_out")
        z_done = sem("z_done")
        z_out = sem("z_out")
        ms_done = sem("ms_done")
        rms_done = sem("rms_done")
        rrms_done = sem("rrms_done")
        zn_done = sem("zn_done")
        znT_done = sem("znT_done")
        znT_out = sem("znT_out")
        ang_done = sem("ang_done")
        trig_done = sem("trig_done")
        krot_done = sem("krot_done")
        krT_done = sem("krT_done")
        krT_out = sem("krT_out")
        proj_done = sem("proj_done")
        proj_out = sem("proj_out")
        q_rot = sem("q_rot")
        s_done = sem("s_done")
        max_done = sem("max_done")
        exp_done = sem("exp_done")
        inv_done = sem("inv_done")
        pT_done = sem("pT_done")
        pT_out = sem("pT_out")
        o_done = sem("o_done")
        o_out = sem("o_out")
        bc_done = sem("bc_done")
        bc_out = sem("bc_out")
        ld_ln = sem("ld_ln")
        ld_ln2 = sem("ld_ln2")
        ld_xs = [sem(f"ld_xs{i}") for i in range(2)]
        oT_done = sem("oT_done")
        oT_out = sem("oT_out")
        yo_done = sem("yo_done")
        yo_used = sem("yo_used")
        std_in = sem("std_in")
        std_done = sem("std_done")
        xa_done = sem("xa_done")
        h2_done = sem("h2_done")
        h2_stored = [sem(f"h2_stored{i}") for i in range(2)]
        h2T_done = sem("h2T_done")
        h2T_out = sem("h2T_out")
        lg_done = sem("lg_done")
        lg_out = sem("lg_out")
        rt_exp_in = sem("rt_exp_in")
        rt_exp = sem("rt_exp")
        member_done = sem("member_done")
        rank_done = sem("rank_done")
        rank_out = sem("rank_out")
        hot_done = sem("hot_done")
        idx_acc = sem("idx_acc")
        tiles_known = sem("tiles_known")
        table_done = sem("table_done")
        ld_gu = [sem(f"ld_gu{i}") for i in range(2)]
        ld_dn = [sem(f"ld_dn{i}") for i in range(2)]
        idx_set = sem("idx_set")
        gathered = [sem(f"gathered{i}") for i in range(2)]
        xgT_done = sem("xgT_done")
        xgT_outA = sem("xgT_outA")
        xgT_outV = sem("xgT_outV")
        hid_done = sem("hid_done")
        silu_done = sem("silu_done")
        he_done = sem("he_done")
        heT_done = sem("heT_done")
        heT_out = sem("heT_out")
        ye_done = sem("ye_done")
        ye_out = sem("ye_out")
        y_stored = [sem(f"y_stored{i}") for i in range(2)]
        y_all = sem("y_all")
        ld_y = [sem(f"ld_y{i}") for i in range(2)]
        comb_done = sem("comb_done")
        out_done = sem("out_done")
        stored = [sem(f"stored{i}") for i in range(2)]
        rot_half = sem("rot_half")
        k_turn = sem("k_turn")
        idx_seen = sem("idx_seen")
        y_free = sem("y_free")
        shift_done = sem("shift_done")
        norm_done = sem("norm_done")
        scaled = sem("scaled")
        vec = sem("vec")
        pol = sem("pol")

        block = ctx.enter_context(nc.Block())
        MOD_STEPS = 3 * KD
        PROJ = 8

        @block.sync
        def _(sp):
            with nc.allow_non_contiguous_dma(reason="four vectors of at most 1024 elements"):
                sp.dma_start(c_col[:], c.rearrange("o (k p) -> p (o k)", p=P)).then_inc(ld_small, 16)
                sp.dma_start(qg_col[:], q_norm_g.rearrange("o (k p) -> p (o k)", p=P)).then_inc(ld_small, 16)
                sp.dma_start(kvg_col[:], kv_norm_g.rearrange("o (k p) -> p (o k)", p=P)).then_inc(ld_small, 16)
                sp.dma_start(pos_i[:], positions.rearrange("o (t p) -> p (o t)", p=P)).then_inc(ld_small, 16)
            sp.dma_start(w_rt[:, :, 0:G], w_gr[0].rearrange("(k p) n -> p k n", p=P)).then_inc(ld_small, 16)
            sp.dma_start(w_rt[:, :, G:], w_er[0].rearrange("(k p) n -> p k n", p=P)).then_inc(ld_small, 16)
            sp.dma_start(b_rt[:, 0:G], b_gr.broadcast_to([P, G])).then_inc(ld_small, 16)
            sp.dma_start(b_rt[:, G:], b_er.broadcast_to([P, E])).then_inc(ld_small, 16)
            x_t = x[0].rearrange("(t p) d -> p t d", p=P)
            wm = w_mod[0].rearrange("(k p) n -> p k n", p=P)

            def load_mod(n):
                if n >= MOD_BUFS:
                    sp.wait_ge(mod_done, n - MOD_BUFS + 1)
                sec, k = n // KD, n % KD
                sp.dma_start(mod_w[n % MOD_BUFS], wm[:, k, sec * 2 * D:(sec + 1) * 2 * D]).then_inc(ld_mod[n % MOD_BUFS], 16)

            for n in range(MOD_BUFS):
                load_mod(n)
            sp.wait_ge(acc_zero, 1)
            sp.dma_start(acc[0:1, :], b_mod).then_inc(ld_bmod, 16)
            for half in range(2):
                sp.dma_start(x_tok[:, half * 4:half * 4 + 4, :], x_t[:, half * 4:half * 4 + 4, :]).then_inc(ld_x, 16)
            for n in range(MOD_BUFS, KD):
                load_mod(n)
            sp.dma_start(win_sb, w_in[0].rearrange("(k p) n -> p k n", p=P)).then_inc(ld_win, 16)
            for n in range(KD, MOD_STEPS):
                load_mod(n)
            sp.wait_ge(mod_done, MOD_STEPS)
            sp.dma_start(wuq_sb, w_uq[0].rearrange("(k p) n -> p k n", p=P)).then_inc(ld_up, 16)
            sp.dma_start(wukv_sb, w_ukv[0].rearrange("(k p) n -> p k n", p=P)).then_inc(ld_up, 16)
            sp.wait_ge(xT_done, 16)
            sp.dma_start(wo_sb, w_o[0].rearrange("(k p) n -> p k n", p=P)).then_inc(ld_wo, 16)

            sp.wait_ge(o_done, H * T)
            sp.dma_start(Ga, ln_g[0, 0:1, :].broadcast_to([P, D])).then_inc(ld_ln, 16)
            sp.dma_start(Ba, ln_b[0, 0:1, :].broadcast_to([P, D])).then_inc(ld_ln, 16)
            for t in range(T):
                if t >= 2:
                    sp.wait_ge(std_in, t - 1)
                sp.dma_start(xs[t % 2], x_t[:, t, :]).then_inc(ld_xs[t % 2], 16)
                if t >= 1:
                    sp.wait_ge(h2_done, t)
                    sp.dma_start(h2_rows[(t - 1) * P:t * P, :], h2[(t - 1) % 2]).then_inc(h2_stored[(t - 1) % 2], 16)
            sp.wait_ge(h2_done, T)
            sp.dma_start(h2_rows[(T - 1) * P:, :], h2[(T - 1) % 2]).then_inc(h2_stored[(T - 1) % 2], 16)

            sp.wait_ge(tiles_known, 1)
            sp.wait_ge(xa_done, T)
            sp.dma_start(lng2, ln_g[0, 1:2, :].broadcast_to([P, D])).then_inc(ld_ln2, 16)
            sp.dma_start(lnb2, ln_b[0, 1:2, :].broadcast_to([P, D])).then_inc(ld_ln2, 16)
            rounds = sp.value_load(rounds_i[0:1, 0:1], min_val=T - 1, max_val=TILES_MAX // 2 - 1)

            def load_weights(j, b):
                e = sp.value_load(te_i[0:1, bass.ds(j, 1)], min_val=0, max_val=E - 1)
                for w, at0 in ((w_gate, 0), (w_up, FF)):
                    sp.dma_start(wgu[b][:, :, at0:at0 + FF],
                                 w[0, bass.ds(e, 1)].rearrange("o (p k) n -> p (o k) n", p=P)).then_inc(ld_gu[b], 16)
                return e

            def load_down(e, b):
                sp.dma_start(wdn[b], w_down[0, bass.ds(e, 1)].rearrange("o (p k) n -> p (o k) n", p=P)).then_inc(ld_dn[b], 16)

            for b in range(2):
                load_down(load_weights(b, b), b)
            with sp.Fori(0, rounds) as i:
                for b in range(2):
                    nxt = i * 2 + (b + 2)
                    sp.wait_ge(hid_done, i * 2 + (b + 1))
                    e = load_weights(nxt, b)
                    sp.wait_ge(ye_done, i * 2 + (b + 1))
                    load_down(e, b)

            sp.wait_ge(y_all, 1)

            def load_pair(t):
                if t >= 2:
                    sp.wait_ge(comb_done, t - 1)
                for a, dst in ((0, ya), (1, yb)):
                    sp.dma_start(dst[t % 2], y_rows[a * S + t * P:a * S + (t + 1) * P, :]).then_inc(ld_y[t % 2], 16)

            load_pair(0)
            load_pair(1)
            for t in range(T):
                if t >= 2:
                    load_pair(t)
                if t >= 1:
                    sp.wait_ge(out_done, t)
                    sp.dma_start(out[0, (t - 1) * P:t * P, :], yo[(t - 1) % 2]).then_inc(stored[(t - 1) % 2], 16)
            sp.wait_ge(out_done, T)
            sp.dma_start(out[0, (T - 1) * P:, :], yo[(T - 1) % 2]).then_inc(stored[(T - 1) % 2], 16)
            for b in range(2):
                sp.wait_ge(stored[b], 16 * (T // 2))

        @block.tensor
        def _(pe):
            def mm(o, a, b, start, stop):
                return nc.tensor.matmul(o, a, b, start=start, stop=stop, skip_group_check=True)

            pe.wait_ge(consts, 1)
            def xT_group(g):
                k, half = g // 2, g % 2
                pe.wait_ge(ld_x, 16 * 2)
                if g >= 4:
                    pe.wait_ge(xT_out, g - 3)
                for t in range(4):
                    ins = nc.tensor.transpose(PS[:, g % 4, t * P:(t + 1) * P],
                                              x_tok[:, half * 4 + t, k * P:(k + 1) * P], ident[:])
                ins.then_inc(xT_done, 1)

            for g in range(4):
                xT_group(g)
            pe.wait_ge(mod_done, KD)
            for j in range(2 * KD):
                ins = mm(PS[:, 7, j:j + 1], acc[:, j * P:(j + 1) * P], ones[:, 0:1], True, True)
            ins.then_inc(cols_done, 1)
            for g in range(4, 16):
                xT_group(g)

            pe.wait_ge(ld_win, 16)
            pe.wait_ge(xT_out, 16)

            def z_tile(t):
                b = 2 * (t % 2)
                if t >= 2:
                    pe.wait_ge(z_out, t - 1)
                for lo, hi in ((0, 512), (512, ZW)):
                    for k in range(KD):
                        ins = mm(PS[:, b + lo // 512, 0:hi - lo], hT[:, k, t * P:(t + 1) * P],
                                 win_sb[:, k, lo:hi], k == 0, k == KD - 1)
                ins.then_inc(z_done, 1)

            def zn_tile(t):
                pe.wait_ge(zn_done, t + 1)
                if t >= 1:
                    pe.wait_ge(znT_out, t)
                for j in range(5):
                    bank, off = (4, j) if j < 3 else (5, j - 3)
                    ins = nc.tensor.transpose(PS[:, bank, off * P:(off + 1) * P], zs[t % 2][:, j * P:(j + 1) * P], ident[:])
                ins.then_inc(znT_done, 1)

            z_tile(0)
            for t in range(T):
                if t + 1 < T:
                    z_tile(t + 1)
                zn_tile(t)
            pe.wait_ge(krot_done, 1)
            for half in range(2):
                for t in range(4):
                    ins = nc.tensor.transpose(PS[0:ROPE, 6 + half, t * P:(t + 1) * P], k_rot[:, half * 4 + t, :], ident[:])
            ins.then_inc(krT_done, 1)

            pe.wait_ge(ld_up, 32)
            pe.wait_ge(znT_out, T)

            def project(m, hn, hp):
                pe.wait_ge(proj_out, hn * PROJ + m)
                half = m % 2
                if m < 2:
                    for t in range(4):
                        for k in range(3):
                            ins = mm(PS[:, 6, t * QH:(t + 1) * QH], qlatT[:, k, (half * 4 + t) * P:(half * 4 + t + 1) * P],
                                     wuq_sb[:, k, bass.ds(hn * QH, QH)], k == 0, k == 2)
                elif m < 4:
                    for t in range(4):
                        for k in range(2):
                            ins = mm(PS[:, 6, t * KVH:(t + 1) * KVH], kvlatT[:, k, (half * 4 + t) * P:(half * 4 + t + 1) * P],
                                     wukv_sb[:, k, bass.ds(hn * KVH, KVH)], k == 0, k == 1)
                elif m < 6:
                    pe.sem_inc(k_turn, 1)
                    for t in range(4):
                        ins = nc.tensor.transpose(PS[0:NOPE, 6, t * P:(t + 1) * P], k_h[:, half * 4 + t, :], ident[:])
                else:
                    if m == 6:
                        pe.wait_ge(q_rot, hn + 1)
                    for t in range(4):
                        ins = nc.tensor.transpose(PS[0:QH, 6, t * P:(t + 1) * P], q_h[:, half * 4 + t, :], ident[:])
                ins.then_inc(proj_done, 1)

            def scores(h, hp, i):
                b, w = 2 * (i % 2), (i + 1) * P
                if not (isinstance(h, int) and h == 0 and i < 2):
                    pe.wait_ge(exp_done, h * T + (i - 1))
                if i == 0:
                    pe.wait_ge(proj_out, h * PROJ + PROJ)
                q = qT[hp][0:QH, i * P:(i + 1) * P]
                for lo in range(0, w, 512):
                    hi = min(w, lo + 512)
                    lastc = hi == w
                    mm(PS[:, b + lo // 512, 0:hi - lo], q, kT[hp][0:QH, lo:hi], True, not lastc)
                    if lastc:
                        ins = mm(PS[:, b + lo // 512, hi - lo - P:hi - lo], ident_bf[:], causal_bf[:], False, True)
                ins.then_inc(s_done, 1)

            def turn(h, i):
                pe.wait_ge(exp_done, h * T + (i + 1))
                for g in range(1 if i < 4 else 2):
                    n = group_at(i) + g
                    if not (isinstance(h, int) and h == 0 and n < 2):
                        pe.wait_ge(pT_out, h * 12 + (n - 1))
                    for k in range(4 * g, min(4 * g + 4, i + 1)):
                        ins = nc.tensor.transpose(PS[:, 4 + n % 2, (k % 4) * P:(k % 4 + 1) * P],
                                                  probs[i % 2][:, k * P:(k + 1) * P], ident[:])
                    ins.then_inc(pT_done, 1)

            def values(h, hp, i):
                pe.wait_ge(pT_out, h * 12 + (group_at(i) + (1 if i < 4 else 2)))
                if not (isinstance(h, int) and h == 0 and i == 0):
                    pe.wait_ge(o_out, h * T + i)
                for k in range(i + 1):
                    ins = mm(PS[:, 7, 0:VH], pT[i % 2][:, k, :], v_h[hp][:, k, :], k == 0, k == i)
                ins.then_inc(o_done, 1)

            def head(h, hp, first, nxt):
                for i in range(T):
                    if nxt and i == 7:
                        project(i, h + 1, 1 - hp)
                    scores(h, hp, i)
                    if nxt and i < 7:
                        project(i, h + 1, 1 - hp)
                    if i >= 1:
                        turn(h, i - 1)
                    elif not first:
                        turn(h - 1, T - 1)
                    if i >= 2:
                        values(h, hp, i - 2)
                    elif not first:
                        values(h - 1, 1 - hp, T - 2 + i)

            pe.wait_ge(krT_out, 1)
            for m in range(PROJ):
                project(m, 0, 0)
            head(0, 0, True, True)
            with pe.Fori(0, (H - 2) // 2) as hh:
                for q in range(2):
                    head(hh * 2 + (1 + q), 1 - q, False, True)
            head(H - 1, 1, False, False)
            turn(H - 1, T - 1)
            values(H - 1, 1, T - 2)
            values(H - 1, 1, T - 1)

            pe.wait_ge(o_out, H * T)
            pe.wait_ge(mod_done, MOD_STEPS)
            for n, sec in enumerate((2, 4, 3, 5)):
                for half in range(2):
                    m = 2 * n + half
                    if m >= 2:
                        pe.wait_ge(bc_out, m - 1)
                    mm(PS[:, 6 + m % 2, :], ones[:], acc[:, sec * D + half * 512:sec * D + half * 512 + 512],
                       True, True).then_inc(bc_done, 1)

            pe.wait_ge(ld_wo, 16)

            def turn_o(t):
                if t >= 1:
                    pe.wait_ge(oT_out, 2 * t)
                for half in range(2):
                    for k in range(4):
                        ins = nc.tensor.transpose(PS[:, half, k * P:(k + 1) * P],
                                                  o_tok[:, t, (half * 4 + k) * P:(half * 4 + k + 1) * P], ident[:])
                    ins.then_inc(oT_done, 1)

            def out_proj(t):
                pe.wait_ge(oT_out, 2 * t + 2)
                if t >= 2:
                    pe.wait_ge(yo_used, t - 1)
                for half in range(2):
                    for k in range(KD):
                        ins = mm(PS[:, 2 + 2 * (t % 2) + half, :], oT[t % 2][:, k, :],
                                 wo_sb[:, k, half * 512:(half + 1) * 512], k == 0, k == KD - 1)
                ins.then_inc(yo_done, 1)

            def route(t):
                pe.wait_ge(h2_done, t + 1)
                for half in range(2):
                    if t >= 1 or half == 1:
                        pe.wait_ge(h2T_out, 2 * t + half)
                    else:
                        pe.wait_ge(bc_out, 8)
                    for k in range(4):
                        ins = nc.tensor.transpose(PS[:, 6, k * P:(k + 1) * P],
                                                  h2[t % 2][:, (half * 4 + k) * P:(half * 4 + k + 1) * P], ident[:])
                    ins.then_inc(h2T_done, 1)
                pe.wait_ge(h2T_out, 2 * t + 2)
                if t >= 1:
                    pe.wait_ge(lg_out, t)
                for k in range(KD):
                    ins = mm(PS[:, 7, 0:G + E], h2T[:, k, :], w_rt[:, k, :], k == 0, k == KD - 1)
                ins.then_inc(lg_done, 1)

            turn_o(0)
            for t in range(T):
                if t + 1 < T:
                    turn_o(t + 1)
                out_proj(t)
                if t >= 1:
                    route(t - 1)
            route(T - 1)

            pe.wait_ge(member_done, 1)
            for t in range(T):
                for u in range(t + 1):
                    mm(PS[:, 0, t * E:(t + 1) * E], before_bf[:] if u == t else ones_bf[:], member[:, u, :], u == 0, u == t)
            for u in range(T):
                ins = mm(PS[:, 1, 0:E], ones_bf[:], member[:, u, :], u == 0, u == T - 1)
            ins.then_inc(rank_done, 1)
            for n in range(TOPK * T):
                pe.wait_ge(hot_done, n + 1)
                mm(PS[:, 2, 0:2 * TILES_MAX], hot_in[n % 2][:], hot_dv[n % 2][:].rearrange("p a j -> p (a j)"), n == 0, n == TOPK * T - 1).then_inc(idx_acc, 1)

            pe.wait_ge(table_done, 1)
            rounds = pe.value_load(rounds_i[0:1, 0:1], min_val=T - 1, max_val=TILES_MAX // 2 - 1)

            def turn_rows(i, b):
                pe.wait_ge(gathered[b], i * 16 + 16)
                if not (isinstance(i, int) and i == 0 and b == 0):
                    pe.wait_ge(xgT_outA, i * 2 + b)
                    pe.wait_ge(xgT_outV, i * 2 + b)
                rows = xg[b].rearrange("p (q k) -> p k q", k=KD)
                for half in range(2):
                    for k in range(4):
                        ins = nc.tensor.transpose(PS[:, half, k * P:(k + 1) * P], rows[:, half * 4 + k, :], ident[:])
                ins.then_inc(xgT_done, 1)

            def hidden(i, b):
                pe.wait_ge(ld_gu[b], i * 32 + 32)
                pe.wait_ge(xgT_outA, i * 2 + (b + 1))
                pe.wait_ge(xgT_outV, i * 2 + (b + 1))
                for k in range(KD):
                    ins = mm(PS[:, 2 + b, :], xgT[b][:, k, :], wgu[b][:, k, :], k == 0, k == KD - 1)
                ins.then_inc(hid_done, 1)

            def turn_hidden(i, b):
                pe.wait_ge(he_done, i * 2 + (b + 1))
                for k in range(2):
                    ins = nc.tensor.transpose(PS[:, 4, k * P:(k + 1) * P], he[b].rearrange("p (q k) -> p k q", k=2)[:, k, :], ident[:])
                ins.then_inc(heT_done, 1)

            def down(i, b):
                pe.wait_ge(heT_out, i * 2 + (b + 1))
                pe.wait_ge(ld_dn[b], i * 16 + 16)
                pe.wait_ge(ye_out, i * 2 + (b + 1))
                for half in range(2):
                    for k in range(2):
                        ins = mm(PS[:, 6 + half, :], heT[b][:, k, :], wdn[b][:, k, half * 512:(half + 1) * 512], k == 0, k == 1)
                ins.then_inc(ye_done, 1)

            turn_rows(0, 0)
            hidden(0, 0)
            turn_rows(0, 1)
            with pe.Fori(0, rounds) as i:
                for b in range(2):
                    turn_hidden(i, b)
                    hidden(i + b, 1 - b)
                    turn_rows(i + 1, b)
                    down(i, b)
            turn_hidden(rounds, 0)
            hidden(rounds, 1)
            down(rounds, 0)
            turn_hidden(rounds, 1)
            down(rounds, 1)

        @block.scalar
        def _(act):
            act.wait_ge(ld_small, 16 * 8)
            nc.scalar.activation(c_act[:], c_col[:], ACT.Silu).then_inc(c_ready, 1)
            act.wait_ge(cols_out, 1)
            for g in range(16):
                k, half = g // 2, g % 2
                act.wait_ge(xT_done, g + 1)
                nc.scalar.activation(hT[:, k, half * 512:(half + 1) * 512], PS[:, g % 4, :], ACT.Identity,
                                     bias=mod_cols[:, k:k + 1], scale=mod_cols[:, KD + k:KD + k + 1]).then_inc(xT_out, 1)
            act.wait_ge(ang_done, 1)
            nc.scalar.activation(sin_t[:], ang[:], ACT.Sin)
            nc.scalar.activation(cos_t[:], turns[:], ACT.Sin).then_inc(trig_done, 1)
            for t in range(T):
                act.wait_ge(z_out, t + 1)
                nc.scalar.activation(sq_junk, zs[t % 2][:, 0:QL], ACT.Square, scale=QL ** -0.5, accum_out=ms[:, t, 0:1]).then_inc(ms_done, 1)
                act.wait_ge(ms_done, 2 * t + 1)
                nc.scalar.activation(sq_junk[:, 0:KVL], zs[t % 2][:, QL:QL + KVL], ACT.Square, scale=KVL ** -0.5,
                                     accum_out=ms[:, t, 1:2]).then_inc(ms_done, 1)
                act.wait_ge(ms_done, 2 * t + 2)
                nc.scalar.activation(rms[:, t, :], ms[:, t, :], ACT.Sqrt, bias=eps_rms[:]).then_inc(rms_done, 1)
                act.wait_ge(znT_done, t + 1)
                for j in range(5):
                    src = PS[:, 4, j * P:(j + 1) * P] if j < 3 else PS[:, 5, (j - 3) * P:(j - 2) * P]
                    dst = qlatT[:, j, t * P:(t + 1) * P] if j < 3 else kvlatT[:, j - 3, t * P:(t + 1) * P]
                    gw = qg_col[:, j:j + 1] if j < 3 else kvg_col[:, j - 3:j - 2]
                    ins = nc.scalar.activation(dst, src, ACT.Copy, scale=gw)
                ins.then_inc(znT_out, 1)
            act.wait_ge(krT_done, 1)
            for q in range(2):
                for half in range(2):
                    ins = nc.scalar.activation(kT[q][NOPE:QH, half * 512:(half + 1) * 512], PS[0:ROPE, 6 + half, :], ACT.Copy)
            ins.then_inc(krT_out, 1)

            def copy_out(m, hn, hp):
                act.wait_ge(proj_done, hn * PROJ + (m + 1))
                half = m % 2
                ts = slice(half * 4, half * 4 + 4)
                if m < 2:
                    ins = nc.scalar.activation(q_h[:, ts, :], PS[:, 6, 0:4 * QH].rearrange("p (t d) -> p t d", t=4), ACT.Copy)
                elif m < 4:
                    src = PS[:, 6, :].rearrange("p (t d) -> p t d", t=4)
                    nc.scalar.activation(k_h[:, ts, :], src[:, :, 0:NOPE], ACT.Copy)
                    ins = nc.scalar.activation(v_h[hp][:, ts, :], src[:, :, NOPE:], ACT.Copy)
                elif m < 6:
                    ins = nc.scalar.activation(kT[hp][0:NOPE, half * 512:(half + 1) * 512], PS[0:NOPE, 6, :], ACT.Copy)
                else:
                    ins = nc.scalar.activation(qT[hp][0:QH, half * 512:(half + 1) * 512], PS[0:QH, 6, :], ACT.Copy, scale=SCALE)
                ins.then_inc(proj_out, 1)

            def softmax(h, hp, i):
                act.wait_ge(max_done, h * T + (i + 1))
                if not (isinstance(h, int) and h == 0 and i < 2):
                    act.wait_ge(pT_done, h * 12 + (group_at(i - 2) + (1 if 0 <= i - 2 < 4 else 2)))
                b, w = 2 * (i % 2), (i + 1) * P
                nc.scalar.activation(probs[i % 2][:, 0:w], PS[:, b:b + 2, :].rearrange("p a n -> p (a n)")[:, 0:w], ACT.Exp,
                                     bias=neg_max[:, i:i + 1], accum_out=row_sum[:, hp * T + i:hp * T + i + 1]).then_inc(exp_done, 1)

            def head(h, hp, nxt):
                for i in range(T):
                    if nxt and i == 7:
                        copy_out(i, h + 1, 1 - hp)
                    softmax(h, hp, i)
                    if nxt and i < 7:
                        copy_out(i, h + 1, 1 - hp)

            for m in range(PROJ):
                copy_out(m, 0, 0)
            head(0, 0, True)
            with act.Fori(0, (H - 2) // 2) as hh:
                for q in range(2):
                    head(hh * 2 + (1 + q), 1 - q, True)
            head(H - 1, 1, False)

            act.wait_ge(o_done, H * T)
            for t in range(T):
                def oT_copy(t):
                    if t >= 2:
                        act.wait_ge(yo_done, t - 1)
                    for half in range(2):
                        act.wait_ge(oT_done, 2 * t + half + 1)
                        nc.scalar.activation(oT[t % 2][:, half * 4:half * 4 + 4, :],
                                             PS[:, half, :].rearrange("p (k q) -> p k q", k=4), ACT.Copy).then_inc(oT_out, 1)

                if t == 0:
                    oT_copy(0)
                if t + 1 < T:
                    oT_copy(t + 1)
                act.wait_ge(std_in, t + 1)
                nc.scalar.activation(std[:, t:t + 1], mv[:, t, 1:2], ACT.Sqrt, bias=eps_ln[:]).then_inc(std_done, 1)
                for half in range(2):
                    act.wait_ge(h2T_done, 2 * t + half + 1)
                    if half == 0 and t >= 1:
                        act.wait_ge(lg_done, t)
                    nc.scalar.activation(h2T[:, half * 4:half * 4 + 4, :],
                                         PS[:, 6, :].rearrange("p (k q) -> p k q", k=4), ACT.Copy).then_inc(h2T_out, 1)

            act.wait_ge(rt_exp_in, 1)
            nc.scalar.activation(g_exp[:], g_exp[:], ACT.Exp)
            nc.scalar.activation(e_exp[:], e_dif[:], ACT.Exp).then_inc(rt_exp, 1)

            act.wait_ge(table_done, 1)
            rounds = act.value_load(rounds_i[0:1, 0:1], min_val=T - 1, max_val=TILES_MAX // 2 - 1)

            def rows_out(i, b):
                act.wait_ge(xgT_done, i * 2 + (b + 1))
                nc.scalar.activation(xgT[b][:, 0:4, :], PS[:, 0, :].rearrange("p (k q) -> p k q", k=4), ACT.Copy).then_inc(xgT_outA, 1)

            def silu(i, b):
                act.wait_ge(hid_done, i * 2 + (b + 1))
                nc.scalar.activation(sil[b], PS[:, 2 + b, 0:FF], ACT.Silu).then_inc(silu_done, 1)

            rows_out(0, 0)
            silu(0, 0)
            rows_out(0, 1)
            with act.Fori(0, rounds) as i:
                for b in range(2):
                    silu(i + b, 1 - b)
                    rows_out(i + 1, b)
            silu(rounds, 1)

            for t in range(T):
                act.wait_ge(std_in, T + t + 1)
                nc.scalar.activation(std[:, T + t:T + t + 1], mv[:, T + t, 1:2], ACT.Sqrt, bias=eps_ln[:]).then_inc(std_done, 1)
                act.wait_ge(shift_done, t + 1)
                nc.scalar.activation(r2[t % 2], r2[t % 2], ACT.Identity, bias=shift[:, t:t + 1],
                                     scale=rstd[:, T + t:T + t + 1]).then_inc(norm_done, 1)

        @block.vector
        def _(dve):
            links = [0]

            def then(ins):
                links[0] += 1
                ins.then_inc(vec, 1)
                dve.wait_ge(vec, links[0])

            dve_ = nc.vector
            dve_.memset(acc, 0.0).then_inc(acc_zero, 1)
            dve_.memset(eps_rms[:], RMS_EPS)
            then(dve_.memset(eps_ln[:], LN_EPS))
            dve.wait_ge(c_ready, 1)
            dve.wait_ge(ld_bmod, 16)
            dve.wait_ge(acc_zero, 1)

            def mod_step(n):
                sec, k = n // KD, n % KD
                a = acc[:, sec * 2 * D:(sec + 1) * 2 * D]
                dve.wait_ge(ld_mod[n % MOD_BUFS], 16 * (n // MOD_BUFS + 1))
                if n >= 1:
                    dve.wait_ge(mod_done, n)
                dve_.scalar_tensor_tensor(out=a, in0=mod_w[n % MOD_BUFS], scalar=c_act[:, k:k + 1], in1=a,
                                          op0=ALU.mult, op1=ALU.add).then_inc(mod_done, 1)

            for n in range(KD):
                mod_step(n)
            dve.wait_ge(cols_done, 1)
            dve_.tensor_copy(mod_cols[:, 0:KD], PS[:, 7, 0:KD])
            dve_.tensor_scalar(mod_cols[:, KD:], PS[:, 7, KD:2 * KD], 1.0, None, ALU.add).then_inc(cols_out, 1)

            for n in range(KD, KD + 6):
                mod_step(n)
            dve.wait_ge(consts, 1)
            then(dve_.tensor_copy(pos_f[:], pos_i[:]))
            then(dve_.tensor_tensor(ang[:], pos_f[:].unsqueeze(2).broadcast_to([P, T, HR]),
                                    freq[:].unsqueeze(1).broadcast_to([P, T, HR]), ALU.mult))
            then(dve_.tensor_scalar(turns[:], ang[:], float(1.0 / TWO_PI), ROUND, ALU.mult, ALU.add))
            then(dve_.tensor_scalar(turns[:], turns[:], -ROUND, None, ALU.add))
            for part in (TWO_PI_HI, TWO_PI_MID, TWO_PI_LO):
                then(dve_.scalar_tensor_tensor(out=ang[:], in0=turns[:], scalar=-part, in1=ang[:], op0=ALU.mult, op1=ALU.add))
            then(dve_.tensor_scalar(turns[:], ang[:], float(np.pi / 2), None, ALU.add))
            then(dve_.tensor_scalar(cos_t[:], turns[:], float(np.pi), -TWO_PI, ALU.is_gt, ALU.mult))
            then(dve_.tensor_tensor(turns[:], turns[:], cos_t[:], ALU.add))
            then(dve_.tensor_scalar(turns[:], turns[:], PI_F, -PI_F, ALU.min, ALU.max))
            dve_.tensor_scalar(ang[:], ang[:], PI_F, -PI_F, ALU.min, ALU.max).then_inc(ang_done, 1)

            for t in range(T):
                dve.wait_ge(z_done, t + 1)
                if t >= 2:
                    dve.wait_ge(znT_done, t - 1)
                b = 2 * (t % 2)
                z_flat = PS[:, b:b + 2, :].rearrange("p a n -> p (a n)")
                dve_.tensor_copy(k_rope[:, t, :], z_flat[:, QL + KVL:ZW])
                dve_.tensor_copy(zs[t % 2][:, 0:QL + KVL], z_flat[:, 0:QL + KVL]).then_inc(z_out, 1)
                for n in range(KD + 6 + 2 * t, min(KD + 8 + 2 * t, MOD_STEPS)):
                    mod_step(n)
                dve.wait_ge(rms_done, t + 1)
                then(dve_.reciprocal(rrms[:, t, :], rms[:, t, :]))
                dve_.tensor_scalar(zs[t % 2][:, 0:QL], zs[t % 2][:, 0:QL], rrms[:, t, 0:1], None, ALU.mult)
                dve_.tensor_scalar(zs[t % 2][:, QL:QL + KVL], zs[t % 2][:, QL:QL + KVL], rrms[:, t, 1:2], None,
                                   ALU.mult).then_inc(zn_done, 1)

            def row_max(h, i):
                dve.wait_ge(s_done, h * T + (i + 1))
                b, w = 2 * (i % 2), (i + 1) * P
                dve_.tensor_reduce(neg_max[:, i:i + 1], PS[:, b:b + 2, :].rearrange("p a n -> p (a n)")[:, 0:w], AX.X, ALU.max,
                                   negate=True).then_inc(max_done, 1)

            def turned(h, i):
                for g in range(1 if i < 4 else 2):
                    n = group_at(i) + g
                    dve.wait_ge(pT_done, h * 12 + (n + 1))
                    if g == 0 and not (isinstance(h, int) and h == 0 and i < 2):
                        dve.wait_ge(o_done, h * T + (i - 1))
                    k0, k1 = 4 * g, min(4 * g + 4, i + 1)
                    dve_.tensor_copy(pT[i % 2][:, k0:k1, :],
                                     PS[:, 4 + n % 2, 0:(k1 - k0) * P].rearrange("p (k q) -> p k q", k=k1 - k0)).then_inc(pT_out, 1)

            def finish(h, hp, i):
                dve.wait_ge(exp_done, h * T + (i + 1))
                dve_.reciprocal(inv_sum[:, i:i + 1], row_sum[:, hp * T + i:hp * T + i + 1]).then_inc(inv_done, 1)
                dve.wait_ge(o_done, h * T + (i + 1))
                dve.wait_ge(inv_done, h * T + (i + 1))
                dve_.tensor_scalar(o_tok[:, i, bass.ds(h * VH, VH)], PS[:, 7, 0:VH], inv_sum[:, i:i + 1], None,
                                   ALU.mult).then_inc(o_out, 1)

            def head(h, hp, first):
                for i in range(T):
                    row_max(h, i)
                    if i >= 1:
                        turned(h, i - 1)
                    elif not first:
                        turned(h - 1, T - 1)
                    if i >= 2:
                        finish(h, hp, i - 2)
                    elif not first:
                        finish(h - 1, 1 - hp, T - 2 + i)

            head(0, 0, True)
            with dve.Fori(0, (H - 2) // 2) as hh:
                for q in range(2):
                    head(hh * 2 + (1 + q), 1 - q, False)
            head(H - 1, 1, False)
            turned(H - 1, T - 1)
            finish(H - 1, 1, T - 2)
            finish(H - 1, 1, T - 1)

            dve.wait_ge(ld_ln, 32)
            for m in range(8):
                half = slice((m % 2) * 512, (m % 2) * 512 + 512)
                src = PS[:, 6 + m % 2, :]
                dve.wait_ge(bc_done, m + 1)
                if m < 2:
                    ins = dve_.tensor_scalar(g1p[:, half], src, 1.0, None, ALU.add)
                elif m < 4:
                    dve_.scalar_tensor_tensor(out=A2[:, half], in0=src, scalar=1.0, in1=Ga[:, half], op0=ALU.add, op1=ALU.mult)
                    ins = dve_.scalar_tensor_tensor(out=B2[:, half], in0=src, scalar=1.0, in1=Ba[:, half], op0=ALU.add, op1=ALU.mult)
                elif m < 6:
                    dve.wait_ge(bc_out, m - 1)
                    ins = dve_.tensor_tensor(B2[:, half], src, B2[:, half], ALU.add)
                else:
                    ins = dve_.tensor_scalar(g2p[:, half], src, 1.0, None, ALU.add)
                ins.then_inc(bc_out, 1)
            dve.wait_ge(bc_out, 8)
            then(dve_.tensor_scalar(Ga, Ga, ALPHA, None, ALU.mult))
            then(dve_.tensor_scalar(Ba, Ba, ALPHA, None, ALU.mult))

            def normalise(t, r):
                dve_.bn_stats(bn[:, 0, :], r[:, 0:512])
                then(dve_.bn_stats(bn[:, 1, :], r[:, 512:D]))
                dve_.bn_aggr(mv[:, t, :], bn[:].rearrange("p a b -> p (a b)")).then_inc(std_in, 1)
                dve.wait_ge(std_done, t + 1)
                then(dve_.reciprocal(rstd[:, t:t + 1], std[:, t:t + 1]))
                then(dve_.tensor_scalar(r, r, mv[:, t, 0:1], rstd[:, t:t + 1], ALU.subtract, ALU.mult))

            def choose(t):
                dve.wait_ge(lg_done, t + 1)
                dve_.tensor_tensor(logits[:, t, :], PS[:, 7, 0:G + E], b_rt[:], ALU.add).then_inc(lg_out, 1)
                dve.wait_ge(lg_out, t + 1)
                then(dve_.tensor_copy(gl[:, t, 0:G], logits[:, t, 0:G]))
                then(dve_.max(g_top[:, t, :], gl[:, t, :]))
                then(dve_.max_index(g_idx[:, t, :], g_top[:, t, :], gl[:, t, :]))
                then(dve_.tensor_copy(g_idf[:, t:t + 1], g_idx[:, t, 0:1]))
                then(dve_.tensor_scalar(g_hot[:, t, :], iota_row[:, 0:G], g_idf[:, t:t + 1], None, ALU.is_equal))
                then(dve_.tensor_tensor(e_sel, logits[:, t, G:].rearrange("p (g e) -> p g e", g=G),
                                        g_hot[:, t, :].unsqueeze(2).broadcast_to([P, G, EPG]), ALU.mult))
                then(dve_.tensor_reduce(e_in[:, t, :], e_sel.rearrange("p g e -> p e g"), AX.X, ALU.add))
                then(dve_.max(e_top[:, t, :], e_in[:, t, :]))
                dve_.max_index(e_idx[:, t, :], e_top[:, t, :], e_in[:, t, :])

            then(dve_.memset(gl[:], -BIG))
            for t in range(T):
                r = r_buf[t % 2]
                dve.wait_ge(yo_done, t + 1)
                b = 2 + 2 * (t % 2)
                y = PS[:, b:b + 2, :].rearrange("p a n -> p (a n)")
                dve.wait_ge(ld_xs[t % 2], 16 * (t // 2 + 1))
                if t >= 2:
                    dve.wait_ge(xa_done, t - 1)
                dve_.tensor_tensor(r, y, g1p, ALU.mult).then_inc(yo_used, 1)
                dve.wait_ge(yo_used, t + 1)
                then(dve_.scalar_tensor_tensor(out=r, in0=xs[t % 2], scalar=ALPHA, in1=r, op0=ALU.mult, op1=ALU.add))
                normalise(t, r)
                if t >= 2:
                    dve.wait_ge(h2_stored[t % 2], 16 * (t // 2))
                    dve.wait_ge(h2T_done, 2 * (t - 1))
                then(dve_.tensor_tensor(h2[t % 2], r, A2, ALU.mult))
                dve_.tensor_tensor(h2[t % 2], h2[t % 2], B2, ALU.add).then_inc(h2_done, 1)
                if t >= 1:
                    choose(t - 1)
            choose(T - 1)

            dve.wait_ge(xa_done, T)
            then(dve_.memset(idx_f[:], 0.0))
            dve_.tensor_tensor(g_exp[:], logits[:, :, 0:G], g_top[:, :, 0:1].broadcast_to([P, T, G]), ALU.subtract)
            dve_.tensor_tensor(e_dif[:], e_top[:, :, 1], e_top[:, :, 0], ALU.subtract).then_inc(rt_exp_in, 1)
            for a in range(TOPK):
                then(dve_.tensor_copy(e_idf[:, a, :], e_idx[:, :, a]))
                then(dve_.scalar_tensor_tensor(out=e_idf[:, a, :], in0=g_idf[:], scalar=float(EPG), in1=e_idf[:, a, :],
                                               op0=ALU.mult, op1=ALU.add))
                then(dve_.tensor_tensor(hot[:, a], iota_row[:, 0:E].unsqueeze(1).broadcast_to([P, T, E]),
                                        e_idf[:, a, :].unsqueeze(2).broadcast_to([P, T, E]), ALU.is_equal))
            dve_.tensor_tensor(member[:], hot[:, 0], hot[:, 1], ALU.add).then_inc(member_done, 1)
            dve.wait_ge(rt_exp, 1)
            then(dve_.tensor_reduce(g_den[:], g_exp[:], AX.X, ALU.add))
            then(dve_.reciprocal(g_p[:], g_den[:]))
            then(dve_.tensor_scalar(e_den[:], e_exp[:], 1.0, None, ALU.add))
            then(dve_.reciprocal(e_den[:], e_den[:]))
            then(dve_.tensor_tensor(wts[:, 0, :], e_den[:], g_p[:], ALU.mult))
            then(dve_.tensor_tensor(wts[:, 1, :], wts[:, 0, :], e_exp[:], ALU.mult))
            dve.wait_ge(rank_done, 1)
            then(dve_.tensor_copy(count[:], PS[:, 1, 0:E]))
            then(dve_.tensor_tensor(over, count[:].unsqueeze(2).broadcast_to([P, E, T]),
                                    iota_tiles[:].unsqueeze(1).broadcast_to([P, E, T]), ALU.is_gt))
            then(dve_.tensor_reduce(n_tiles[:], over, AX.X, ALU.add))
            then(dve_.tensor_tensor_scan(tile_end[:], ones[:, 0:E], n_tiles[:], 0.0, ALU.mult, ALU.add))
            then(dve_.tensor_tensor(te_cmp, iota_row[0:1, 0:LOOP_TABLE].unsqueeze(2).broadcast_to([1, LOOP_TABLE, E]),
                                    tile_end[0:1, :].unsqueeze(1).broadcast_to([1, LOOP_TABLE, E]), ALU.is_ge))
            then(dve_.tensor_reduce(te_f[:], te_cmp, AX.X, ALU.add))
            then(dve_.tensor_scalar(te_f[:], te_f[:], float(E - 1), None, ALU.min))
            then(dve_.tensor_copy(te_i[:], te_f[:]))
            then(dve_.tensor_scalar(rounds_f[:, 0:1], tile_end[0:1, E - 1:E], 0.5, 0.25, ALU.mult, ALU.add))
            then(dve_.tensor_scalar(rounds_f[:, 0:1], rounds_f[:, 0:1], ROUND, -ROUND - 1.0, ALU.add, ALU.add))
            dve_.tensor_copy(rounds_i[:], rounds_f[:, 0:1]).then_inc(tiles_known, 1)
            then(dve_.tensor_tensor(base[:], tile_end[:], n_tiles[:], ALU.subtract))
            then(dve_.scalar_tensor_tensor(out=place, in0=base[:].unsqueeze(1).broadcast_to([P, T, E]), scalar=float(P),
                                           in1=PS[:, 0, 0:T * E].rearrange("p (t e) -> p t e", t=T), op0=ALU.mult, op1=ALU.add))
            for a in range(TOPK):
                then(dve_.tensor_tensor(picked[:, a], hot[:, a], place, ALU.mult))
            then(dve_.tensor_reduce(slot[:], picked, AX.X, ALU.add))
            then(dve_.tensor_scalar(slot_dv[:], slot[:], 1.0 / P, -0.5 + 0.5 / P, ALU.mult, ALU.add))
            then(dve_.tensor_scalar(slot_dv[:], slot_dv[:], ROUND, None, ALU.add))
            then(dve_.tensor_scalar(slot_dv[:], slot_dv[:], -ROUND, None, ALU.add))
            then(dve_.scalar_tensor_tensor(out=slot_in[:], in0=slot_dv[:], scalar=-float(P), in1=slot[:], op0=ALU.mult, op1=ALU.add))
            for n in range(TOPK * T):
                a, t = n // T, n % T
                if n >= 2:
                    dve.wait_ge(idx_acc, n - 1)
                dve_.tensor_scalar(hot_in[n % 2][:], iota_row[:], slot_in[:, a, t:t + 1], None, ALU.is_equal)
                dve_.tensor_scalar(hot_dv[n % 2][:, 1, :], iota_row[:, 0:TILES_MAX], slot_dv[:, a, t:t + 1], wts[:, a, t:t + 1],
                                   ALU.is_equal, ALU.mult)
                dve_.tensor_scalar(hot_dv[n % 2][:, 0, :], iota_row[:, 0:TILES_MAX], slot_dv[:, a, t:t + 1], row_id[:, a * T + t:a * T + t + 1],
                                   ALU.is_equal, ALU.mult).then_inc(hot_done, 1)
            for b in range(2):
                ins = dve_.memset(xg[b], 0.0)
            then(ins)
            dve.wait_ge(idx_acc, TOPK * T)
            dve_.tensor_copy(slot_w[:, 0:TILES_MAX], PS[:, 2, TILES_MAX:2 * TILES_MAX])
            then(dve_.tensor_copy(idx_f[:, 0:TILES_MAX], PS[:, 2, 0:TILES_MAX]))
            then(dve_.tensor_scalar(pad[:], idx_f[:], 0.0, 4.0 * S, ALU.is_equal, ALU.mult))
            then(dve_.scalar_tensor_tensor(out=row_f[:], in0=idx_f[:], scalar=-1.0, in1=pad[:], op0=ALU.add, op1=ALU.add))
            then(dve_.tensor_copy(dst_u[:], row_f[:]))
            then(dve_.tensor_scalar(past[:], row_f[:], float(S) - 0.5, -float(S), ALU.is_gt, ALU.mult))
            then(dve_.tensor_tensor(row_f[:], row_f[:], past[:], ALU.add))
            dve_.tensor_copy(idx_u[:], row_f[:]).then_inc(table_done, 1)

            dve.wait_ge(table_done, 1)
            rounds = dve.value_load(rounds_i[0:1, 0:1], min_val=T - 1, max_val=TILES_MAX // 2 - 1)

            def rows_out(i, b):
                dve.wait_ge(xgT_done, i * 2 + (b + 1))
                dve_.tensor_copy(xgT[b][:, 4:8, :], PS[:, 1, :].rearrange("p (k q) -> p k q", k=4)).then_inc(xgT_outV, 1)

            def gated(i, b):
                dve.wait_ge(silu_done, i * 2 + (b + 1))
                dve_.tensor_tensor(he[b], PS[:, 2 + b, FF:], sil[b], ALU.mult).then_inc(he_done, 1)

            def hidden_out(i, b):
                dve.wait_ge(heT_done, i * 2 + (b + 1))
                dve_.tensor_copy(heT[b], PS[:, 4, 0:2 * P].rearrange("p (k q) -> p k q", k=2)).then_inc(heT_out, 1)

            def result_out(i, b):
                dve.wait_ge(ye_done, i * 2 + (b + 1))
                dve.wait_ge(y_free, i * 2 + (b + 1))
                dve_.scalar_tensor_tensor(out=y_e[b], in0=PS[:, 6:8, :].rearrange("p a n -> p (a n)"),
                                          scalar=slot_w[:, bass.ds(i * 2 + b, 1)], in1=g2p, op0=ALU.mult, op1=ALU.mult).then_inc(ye_out, 1)

            dve.sem_inc(ye_out, 1)
            rows_out(0, 0)
            gated(0, 0)
            rows_out(0, 1)
            with dve.Fori(0, rounds) as i:
                for b in range(2):
                    hidden_out(i, b)
                    gated(i + b, 1 - b)
                    rows_out(i + 1, b)
                    result_out(i, b)
            hidden_out(rounds, 0)
            gated(rounds, 1)
            result_out(rounds, 0)
            hidden_out(rounds, 1)
            result_out(rounds, 1)

            dve.wait_ge(ld_ln2, 32)

            def last_part(t):
                dve.wait_ge(norm_done, t + 1)
                dve_.tensor_tensor(r2[t % 2], r2[t % 2], lng2, ALU.mult).then_inc(scaled, 1)

            for t in range(T):
                b = t % 2
                dve.wait_ge(ld_y[b], 32 * (t // 2 + 1))
                then(dve_.tensor_tensor(ya[b], ya[b], yb[b], ALU.add))
                if t >= 2:
                    dve.wait_ge(out_done, t - 1)
                dve_.tensor_tensor(r2[b], ya[b], xa[:, t, :], ALU.add).then_inc(comb_done, 1)
                dve.wait_ge(comb_done, t + 1)
                dve_.bn_stats(bn[:, 0, :], r2[b][:, 0:512])
                then(dve_.bn_stats(bn[:, 1, :], r2[b][:, 512:D]))
                dve_.bn_aggr(mv[:, T + t, :], bn[:].rearrange("p a b -> p (a b)")).then_inc(std_in, 1)
                dve.wait_ge(std_done, T + t + 1)
                then(dve_.reciprocal(rstd[:, T + t:T + t + 1], std[:, T + t:T + t + 1]))
                dve_.scalar_tensor_tensor(out=shift[:, t:t + 1], in0=mv[:, T + t, 0:1], scalar=-1.0, in1=rstd[:, T + t:T + t + 1],
                                          op0=ALU.mult, op1=ALU.mult).then_inc(shift_done, 1)
                if t >= 1:
                    last_part(t - 1)
            last_part(T - 1)

        @block.gpsimd
        def _(pool):
            links = [0]

            def then(ins):
                links[0] += 1
                ins.then_inc(pol, 1)
                pool.wait_ge(pol, links[0])

            g_ = nc.gpsimd
            g_.memset(ident[:], 0.0)
            g_.memset(ones[:], 1.0)
            g_.memset(causal_bf[:], 0.0)
            g_.memset(ident_bf[:], 0.0)
            then(g_.memset(ones_bf[:], 1.0))
            for m in (ident, ident_bf):
                then(g_.affine_select(out=m[:], in_=m[:], compare_op=ALU.not_equal, fill=1.0, base=0,
                                      pattern=[[-1, P]], channel_multiplier=1))
            then(g_.affine_select(out=causal_bf[:], in_=causal_bf[:], compare_op=ALU.is_ge, fill=-BIG, base=0,
                                  pattern=[[-1, P]], channel_multiplier=1))
            then(g_.affine_select(out=before_bf[:], in_=ones_bf[:], compare_op=ALU.is_gt, fill=0.0, base=0,
                                  pattern=[[1, P]], channel_multiplier=-1))
            then(g_.iota(iota_row[:], [[1, P]], base=0, channel_multiplier=0, allow_small_or_imprecise_dtypes=True))
            then(g_.iota(iota_tiles[:], [[P, T]], base=0, channel_multiplier=0, allow_small_or_imprecise_dtypes=True))
            then(g_.iota(row_id[:], [[P, TOPK * T]], base=1, channel_multiplier=1, allow_small_or_imprecise_dtypes=True))
            for r in range(HR):
                ins = g_.memset(freq[:, r:r + 1], float(inv_freq[r]))
            then(ins)
            pool.sem_inc(consts, 1)

            pool.wait_ge(trig_done, 1)
            pool.wait_ge(z_out, T)
            x1, x2 = k_rope[:, :, 0:HR], k_rope[:, :, HR:ROPE]
            g_.tensor_tensor(rope_k[:, 0], x1, cos_t[:], ALU.mult)
            g_.tensor_tensor(rope_k[:, 1], x2, sin_t[:], ALU.mult)
            g_.tensor_tensor(rope_k[:, 2], x1, sin_t[:], ALU.mult)
            then(g_.tensor_tensor(rope_k[:, 3], x2, cos_t[:], ALU.mult))
            g_.tensor_tensor(k_rot[:, :, 0:HR], rope_k[:, 0], rope_k[:, 1], ALU.subtract)
            g_.tensor_tensor(k_rot[:, :, HR:ROPE], rope_k[:, 2], rope_k[:, 3], ALU.add).then_inc(krot_done, 1)

            def rotate(h):
                pool.wait_ge(proj_out, h * PROJ + 2)
                q1, q2 = q_h[:, :, NOPE:NOPE + HR], q_h[:, :, NOPE + HR:QH]
                g_.tensor_tensor(rope_tmp[:, 0], q1, cos_t[:], ALU.mult)
                g_.tensor_tensor(rope_tmp[:, 1], q2, sin_t[:], ALU.mult)
                g_.tensor_tensor(rope_tmp[:, 2], q1, sin_t[:], ALU.mult)
                g_.tensor_tensor(rope_tmp[:, 3], q2, cos_t[:], ALU.mult).then_inc(rot_half, 1)
                pool.wait_ge(rot_half, h + 1)
                g_.tensor_tensor(q1, rope_tmp[:, 0], rope_tmp[:, 1], ALU.subtract)
                g_.tensor_tensor(q2, rope_tmp[:, 2], rope_tmp[:, 3], ALU.add).then_inc(q_rot, 1)

            with pool.Fori(0, H) as h:
                rotate(h)

            for t in range(T):
                pool.wait_ge(h2_done, t + 1)
                pool.wait_ge(oT_done, 2 * t + 2)
                then(g_.tensor_tensor(xa[:, t, :], r_buf[t % 2], Ga, ALU.mult))
                g_.tensor_tensor(xa[:, t, :], xa[:, t, :], Ba, ALU.add).then_inc(xa_done, 1)

            pool.wait_ge(xa_done, T)
            pool.wait_ge(h2_stored[0], 16 * (T // 2))
            pool.wait_ge(h2_stored[1], 16 * (T // 2))
            pool.wait_ge(h2T_done, 2 * T)
            pool.wait_ge(table_done, 1)
            rounds = pool.value_load(rounds_i[0:1, 0:1], min_val=T - 1, max_val=TILES_MAX // 2 - 1)
            last = pool.snap(rounds * 16 + 32)

            def gather(b):
                g_.indirect_dma_start(xg[b], None, h2_rows, bass.IndirectOffsetOnAxis(idx_now[b][:, 0:1], 0),
                                      bounds_check=S - 1, oob_is_err=False).then_inc(gathered[b], 16)

            def scatter(i, b, ahead):
                n = i * 2 + b
                if ahead:
                    pool.wait_ge(xgT_done, n + 2)
                    g_.tensor_copy(idx_now[1 - b][:], idx_u[:, bass.ds(n + 3, 1)])
                g_.tensor_copy(dst_now[b][:], dst_u[:, bass.ds(n, 1)]).then_inc(idx_set, 1)
                pool.wait_ge(idx_set, n + 2)
                if ahead:
                    pool.sem_inc(idx_seen, 1)
                    gather(1 - b)
                pool.wait_ge(ye_out, n + 2)
                pool.sem_inc(idx_seen, 1)
                g_.indirect_dma_start(y_rows, bass.IndirectOffsetOnAxis(dst_now[b][:, 0:1], 0), y_e[b], None,
                                      bounds_check=TOPK * S - 1, oob_is_err=False).then_inc(y_stored[b], 16)
                pool.wait_ge(y_stored[b], i * 16 + 16)
                pool.sem_inc(y_free, 1)

            pool.sem_inc(y_free, 2)
            g_.tensor_copy(idx_now[0][:], idx_u[:, 0:1])
            g_.tensor_copy(idx_now[1][:], idx_u[:, 1:2]).then_inc(idx_set, 1)
            pool.wait_ge(idx_set, 1)
            gather(0)
            gather(1)
            pool.wait_ge(xgT_done, 1)
            then(g_.tensor_copy(idx_now[0][:], idx_u[:, 2:3]))
            gather(0)
            with pool.Fori(0, rounds) as i:
                for b in range(2):
                    scatter(i, b, True)
            scatter(rounds, 0, False)
            scatter(rounds, 1, False)
            pool.wait_ge(gathered[0], last)
            pool.sem_inc(y_all, 1)

            for t in range(T):
                pool.wait_ge(scaled, t + 1)
                if t >= 2:
                    pool.wait_ge(stored[t % 2], 16 * (t // 2))
                g_.tensor_tensor(yo[t % 2], r2[t % 2], lnb2, ALU.add).then_inc(out_done, 1)


def group_at(i):
    return sum(1 if j < 4 else 2 for j in range(i)) if i >= 0 else -sum(1 if j % T < 4 else 2 for j in range(i, 0))


_INS = ["x", "c", "positions", "w_mod", "b_mod", "ln_g", "ln_b", "w_in", "q_norm_g", "kv_norm_g", "w_uq", "w_ukv", "w_o",
        "w_group_router", "b_group_router", "w_expert_router", "b_expert_router", "w_gate", "w_up", "w_down"]


def kernel(**inputs):
    import concourse.bacc as _bacc
    from concourse.bass_utils import run_bass_kernel_spmd as _run

    nc = _bacc.Bacc("TRN2", target_bir_lowering=False, num_devices=1)
    arrays, args = {}, []
    for name in _INS:
        a = np.ascontiguousarray(inputs[name])
        arrays[f"in_{name}_dram"] = a
        args.append(nc.dram_tensor(f"in_{name}_dram", a.shape, mybir.dt.from_np(a.dtype), kind="ExternalInput").ap())
    args.append(nc.dram_tensor("out_dram", (1, S, D), F32, kind="ExternalOutput").ap())
    build_trunk(nc, *args)
    r = _run(nc, [arrays], core_ids=[0])
    return r.results[0]["out_dram"]
```

```python
from contextlib import ExitStack

import numpy as np
import concourse.bass as bass
from concourse import mybir

F32, BF16, I32, U32 = mybir.dt.float32, mybir.dt.bfloat16, mybir.dt.int32, mybir.dt.uint32
ALU = mybir.AluOpType
ACT = mybir.ActivationFunctionType
AX = mybir.AxisListType

P = 128
D = 1024
S = 1024
T = S // P
KD = D // P
H = 16
QL, KVL, NOPE, ROPE, VH = 384, 256, 64, 32, 64
HR = ROPE // 2
ZW = QL + KVL + ROPE
QH = NOPE + ROPE
KVH = NOPE + VH
G, EPG = 4, 8
E = G * EPG
FF = 256
TOPK = 2
TILES_MAX = E + TOPK * S // P
LOOP_TABLE = TILES_MAX + 4
SCALE = float(QH) ** -0.5
ALPHA = float(2.0 ** 0.25)
LN_EPS, RMS_EPS = 1e-5, 1e-6
BIG = 3.0e38
TWO_PI = 2.0 * np.pi
TWO_PI_HI = 6.28125
TWO_PI_MID = float(np.float32(np.round((TWO_PI - TWO_PI_HI) * 2 ** 21) / 2 ** 21))
TWO_PI_LO = float(np.float32(TWO_PI - TWO_PI_HI - TWO_PI_MID))
ROUND = 1.5 * 2.0 ** 23
PI_F = 3.1415925


def build_trunk(nc, x, c, positions, w_mod, b_mod, ln_g, ln_b, w_in, q_norm_g, kv_norm_g, w_uq, w_ukv, w_o,
                w_gr, b_gr, w_er, b_er, w_gate, w_up, w_down, out):
    inv_freq = (1.0 / np.float32(10000.0) ** (np.arange(0, ROPE, 2, dtype=np.float32) / np.float32(ROPE))).astype(np.float32)
    h2_rows = nc.dram_tensor("h2_rows", [S, D], F32, kind="Internal").ap()
    y_rows = nc.dram_tensor("y_rows", [TOPK * S, D], F32, kind="Internal").ap()

    ctx = ExitStack()
    with ctx:
        def sb(name, shape, dt=F32):
            return ctx.enter_context(nc.sbuf_tensor(name, shape, dt))

        def sem(name):
            return ctx.enter_context(nc.semaphore(name))

        PS = ctx.enter_context(nc.psum_tensor("banks", [P, 8, 512], F32))

        reg_x = sb("reg_x", [P, T * D])
        reg_h = sb("reg_h", [P, T * D])
        reg_mod = sb("reg_mod", [P, 6 * D])
        reg_up = sb("reg_up", [P, 3 * H * QH + 2 * H * KVH])
        reg_lat = sb("reg_lat", [P, 5 * D])
        reg_work = sb("reg_work", [P, 11264])

        x_tok = reg_x[:].rearrange("p (t d) -> p t d", t=T)
        wo_sb = reg_x[:].rearrange("p (k d) -> p k d", k=KD)
        hT = reg_h[:].rearrange("p (k s) -> p k s", k=KD)
        o_tok = reg_h[:].rearrange("p (t d) -> p t d", t=T)
        xa = o_tok
        acc = reg_mod[:]
        wuq_sb = reg_up[:, 0:3 * H * QH].rearrange("p (k n) -> p k n", k=3)
        wukv_sb = reg_up[:, 3 * H * QH:].rearrange("p (k n) -> p k n", k=2)
        qlatT = reg_lat[:, 0:3 * D].rearrange("p (k s) -> p k s", k=3)
        kvlatT = reg_lat[:, 3 * D:5 * D].rearrange("p (k s) -> p k s", k=2)
        g1p, A2, B2, Ga, Ba = (reg_lat[:, i * D:(i + 1) * D] for i in range(5))

        at = [0]

        def work(n):
            at[0] += n
            assert at[0] <= 11264
            return reg_work[:, at[0] - n:at[0]]

        win_sb = work(KD * ZW).rearrange("p (k n) -> p k n", k=KD)
        MOD_BUFS = 4
        mod_w = [reg_up[:, i * 2 * D:(i + 1) * 2 * D] for i in range(MOD_BUFS)]
        zs = [work(ZW) for _ in range(2)]
        sq_junk = work(QL)
        k_rope = work(T * ROPE).rearrange("p (t r) -> p t r", t=T)
        k_rot = work(T * ROPE).rearrange("p (t r) -> p t r", t=T)
        rope_k = work(4 * T * HR).rearrange("p (a t r) -> p a t r", a=4, t=T)
        at[0] = 0
        kT = [work(S) for _ in range(2)]
        qT = [work(S) for _ in range(2)]
        v_h = [work(T * VH).rearrange("p (t d) -> p t d", t=T) for _ in range(2)]
        k_h = work(T * NOPE).rearrange("p (t d) -> p t d", t=T)
        q_h = work(T * QH).rearrange("p (t d) -> p t d", t=T)
        rope_tmp = work(4 * T * HR).rearrange("p (a t r) -> p a t r", a=4, t=T)
        probs = [work(S) for _ in range(2)]
        pT = [work(S).rearrange("p (b q) -> p b q", b=T) for _ in range(2)]
        at[0] = 0
        oT = [work(D).rearrange("p (k q) -> p k q", k=KD) for _ in range(2)]
        h2T = work(D).rearrange("p (k q) -> p k q", k=KD)
        xs = [work(D) for _ in range(2)]
        r_buf = [work(D) for _ in range(2)]
        h2 = [work(D) for _ in range(2)]
        g2p = work(D)
        at[0] = 0
        xg = [work(D) for _ in range(2)]
        xgT = [work(D).rearrange("p (k q) -> p k q", k=KD) for _ in range(2)]
        he = [work(FF) for _ in range(2)]
        heT = [work(FF).rearrange("p (k q) -> p k q", k=2) for _ in range(2)]
        sil = [work(FF) for _ in range(2)]
        y_e = [work(D) for _ in range(2)]
        assert at[0] <= 9 * D
        lng2, lnb2 = reg_lat[:, 0:D], reg_lat[:, D:2 * D]
        te_cmp = reg_lat[0:1, 2 * D:2 * D + LOOP_TABLE * E].rearrange("p (j e) -> p j e", e=E)
        place = reg_lat[:, 4 * D:4 * D + T * E].rearrange("p (t e) -> p t e", e=E)
        picked = reg_lat[:, 4 * D + T * E:4 * D + 3 * T * E].rearrange("p (a t e) -> p a t e", a=TOPK, e=E)
        hot = reg_x[:, 7 * D:7 * D + TOPK * T * E].rearrange("p (a t e) -> p a t e", a=TOPK, t=T)
        hot_in = reg_x[:, 0:TOPK * T * P].rearrange("p (a t j) -> p a t j", a=TOPK, t=T)
        hot_dv = reg_x[:, 2 * D:2 * D + TOPK * T * 2 * TILES_MAX].rearrange("p (n a j) -> p n a j", n=TOPK * T, a=2)
        over = reg_x[:, 7 * D + TOPK * T * E:7 * D + 3 * T * E].rearrange("p (e t) -> p e t", t=T)
        wgu = [reg_mod[:, 0:KD * 2 * FF].rearrange("p (k n) -> p k n", k=KD),
               reg_up[:, 0:KD * 2 * FF].rearrange("p (k n) -> p k n", k=KD)]
        wdn = [reg_mod[:, KD * 2 * FF:KD * 2 * FF + 2 * D].rearrange("p (k n) -> p k n", k=2),
               reg_up[:, KD * 2 * FF:KD * 2 * FF + 2 * D].rearrange("p (k n) -> p k n", k=2)]
        y_at = [reg_x[:, i * D:(i + 1) * D] for i in range(8)] + [reg_up[:, i * D:(i + 1) * D] for i in range(8)]
        ya, yb = y_at[0::2], y_at[1::2]

        ident = sb("ident", [P, P])
        ones = sb("ones", [P, P])
        ident_bf = sb("ident_bf", [P, P], BF16)
        causal_bf = sb("causal_bf", [P, P], BF16)
        before_bf = sb("before_bf", [P, P], BF16)
        ones_bf = sb("ones_bf", [P, P], BF16)
        iota_row = sb("iota_row", [P, P])
        iota_tiles = sb("iota_tiles", [P, T])
        row_id = sb("row_id", [P, TOPK * T])
        freq = sb("freq", [P, HR])
        c_col = sb("c_col", [P, KD])
        c_act = sb("c_act", [P, KD])
        mod_cols = sb("mod_cols", [P, 2 * KD])
        qg_col = sb("qg_col", [P, 3])
        kvg_col = sb("kvg_col", [P, 2])
        pos_i = sb("pos_i", [P, T], I32)
        pos_f = sb("pos_f", [P, T])
        ang = sb("ang", [P, T, HR])
        turns = sb("turns", [P, T, HR])
        cos_t = sb("cos_t", [P, T, HR])
        sin_t = sb("sin_t", [P, T, HR])
        ms = sb("ms", [P, T, 2])
        rms = sb("rms", [P, T, 2])
        rrms = sb("rrms", [P, T, 2])
        eps_rms = sb("eps_rms", [P, 1])
        eps_ln = sb("eps_ln", [P, 1])
        neg_max = sb("neg_max", [P, T])
        row_sum = sb("row_sum", [P, 2 * T])
        inv_sum = sb("inv_sum", [P, T])
        bn = sb("bn", [P, 2, 6])
        mv = sb("mv", [P, 2 * T, 2])
        std = sb("std", [P, 2 * T])
        rstd = sb("rstd", [P, 2 * T])
        shift = sb("shift", [P, T])
        w_rt = sb("w_rt", [P, KD, G + E])
        b_rt = sb("b_rt", [P, G + E])
        logits = sb("logits", [P, T, G + E])
        gl = sb("gl", [P, T, 8])
        g_top = sb("g_top", [P, T, 8])
        g_idx = sb("g_idx", [P, T, 8], U32)
        g_idf = sb("g_idf", [P, T])
        g_exp = sb("g_exp", [P, T, G])
        g_den = sb("g_den", [P, T])
        g_p = sb("g_p", [P, T])
        g_hot = sb("g_hot", [P, T, G])
        e_sel = sb("e_sel", [P, G, EPG])[:]
        e_in = sb("e_in", [P, T, EPG])
        e_top = sb("e_top", [P, T, 8])
        e_idx = sb("e_idx", [P, T, 8], U32)
        e_idf = sb("e_idf", [P, TOPK, T])
        e_dif = sb("e_dif", [P, T])
        e_exp = sb("e_exp", [P, T])
        e_den = sb("e_den", [P, T])
        wts = sb("wts", [P, TOPK, T])
        member = sb("member", [P, T, E], BF16)
        count = sb("count", [P, E])
        n_tiles = sb("n_tiles", [P, E])
        tile_end = sb("tile_end", [P, E])
        base = sb("base", [P, E])
        slot = sb("slot", [P, TOPK, T])
        row_f = sb("row_f", [P, LOOP_TABLE])
        pad = sb("pad", [P, LOOP_TABLE])
        slot_w = sb("slot_w", [P, LOOP_TABLE])
        past = sb("past", [P, LOOP_TABLE])
        slot_in = sb("slot_in", [P, TOPK, T])
        slot_dv = sb("slot_dv", [P, TOPK, T])
        idx_f = sb("idx_f", [P, LOOP_TABLE])
        idx_u = sb("idx_u", [P, LOOP_TABLE], U32)
        dst_u = sb("dst_u", [P, LOOP_TABLE], U32)
        idx_now = [sb(f"idx_now{i}", [P, 1], U32) for i in range(2)]
        dst_now = [sb(f"dst_now{i}", [P, 1], U32) for i in range(2)]
        te_f = sb("te_f", [1, LOOP_TABLE])
        te_i = sb("te_i", [1, LOOP_TABLE], I32)
        rounds_f = sb("rounds_f", [1, 2])
        rounds_i = sb("rounds_i", [1, 2], I32)

        consts = sem("consts")
        ld_x = [sem(f"ld_x{i}") for i in range(2)]
        ld_small = sem("ld_small")
        ld_bmod = sem("ld_bmod")
        acc_zero = sem("acc_zero")
        ld_mod = [sem(f"ld_mod{i}") for i in range(MOD_BUFS)]
        mod_done = sem("mod_done")
        c_ready = sem("c_ready")
        ld_win = sem("ld_win")
        ld_up = sem("ld_up")
        ld_wo = sem("ld_wo")
        xT_done = sem("xT_done")
        xT_out = sem("xT_out")
        cols_done = sem("cols_done")
        cols_out = sem("cols_out")
        z_done = sem("z_done")
        z_out = sem("z_out")
        ms_done = sem("ms_done")
        rms_done = sem("rms_done")
        rrms_done = sem("rrms_done")
        zn_done = sem("zn_done")
        znT_done = sem("znT_done")
        znT_out = sem("znT_out")
        ang_done = sem("ang_done")
        trig_done = sem("trig_done")
        krot_done = sem("krot_done")
        krT_done = sem("krT_done")
        krT_out = sem("krT_out")
        proj_done = sem("proj_done")
        proj_out = sem("proj_out")
        q_rot = sem("q_rot")
        s_done = sem("s_done")
        max_done = sem("max_done")
        exp_done = sem("exp_done")
        inv_done = sem("inv_done")
        pT_done = sem("pT_done")
        pT_out = sem("pT_out")
        o_done = sem("o_done")
        o_out = sem("o_out")
        bc_done = sem("bc_done")
        bc_out = sem("bc_out")
        ld_ln = sem("ld_ln")
        ld_ln2 = sem("ld_ln2")
        ld_xs = [sem(f"ld_xs{i}") for i in range(2)]
        oT_done = sem("oT_done")
        oT_out = sem("oT_out")
        yo_done = sem("yo_done")
        yo_used = sem("yo_used")
        std_in = sem("std_in")
        std_done = sem("std_done")
        xa_done = sem("xa_done")
        h2_done = sem("h2_done")
        h2_stored = [sem(f"h2_stored{i}") for i in range(2)]
        h2T_done = sem("h2T_done")
        h2T_out = sem("h2T_out")
        lg_done = sem("lg_done")
        lg_out = sem("lg_out")
        rt_exp_in = sem("rt_exp_in")
        rt_exp = sem("rt_exp")
        member_done = sem("member_done")
        rank_done = sem("rank_done")
        rank_out = sem("rank_out")
        place_known = sem("place_known")
        hot_done = sem("hot_done")
        idx_acc = sem("idx_acc")
        tiles_known = sem("tiles_known")
        table_done = sem("table_done")
        ld_gu = [sem(f"ld_gu{i}") for i in range(2)]
        ld_dn = [sem(f"ld_dn{i}") for i in range(2)]
        idx_set = sem("idx_set")
        gathered = [sem(f"gathered{i}") for i in range(2)]
        xgT_done = sem("xgT_done")
        xgT_outA = sem("xgT_outA")
        xgT_outV = sem("xgT_outV")
        hid_done = sem("hid_done")
        silu_done = sem("silu_done")
        he_done = sem("he_done")
        heT_done = sem("heT_done")
        heT_out = sem("heT_out")
        ye_done = sem("ye_done")
        ye_out = sem("ye_out")
        y_stored = [sem(f"y_stored{i}") for i in range(2)]
        y_all = sem("y_all")
        ld_y = [sem(f"ld_y{i}") for i in range(T)]
        added = sem("added")
        out_done = sem("out_done")
        stored = sem("stored")
        rot_half = sem("rot_half")
        k_turn = sem("k_turn")
        idx_seen = sem("idx_seen")
        y_free = sem("y_free")
        shift_done = sem("shift_done")
        norm_done = sem("norm_done")
        scaled = sem("scaled")
        vec = sem("vec")
        pol = sem("pol")

        block = ctx.enter_context(nc.Block())
        MOD_STEPS = 3 * KD
        PROJ = 8
        POOL_ADDS = 2

        @block.sync
        def _(sp):
            with nc.allow_non_contiguous_dma(reason="four vectors of at most 1024 elements"):
                sp.dma_start(c_col[:], c.rearrange("o (k p) -> p (o k)", p=P)).then_inc(ld_small, 16)
                sp.dma_start(qg_col[:], q_norm_g.rearrange("o (k p) -> p (o k)", p=P)).then_inc(ld_small, 16)
                sp.dma_start(kvg_col[:], kv_norm_g.rearrange("o (k p) -> p (o k)", p=P)).then_inc(ld_small, 16)
                sp.dma_start(pos_i[:], positions.rearrange("o (t p) -> p (o t)", p=P)).then_inc(ld_small, 16)
            sp.dma_start(w_rt[:, :, 0:G], w_gr[0].rearrange("(k p) n -> p k n", p=P)).then_inc(ld_small, 16)
            sp.dma_start(w_rt[:, :, G:], w_er[0].rearrange("(k p) n -> p k n", p=P)).then_inc(ld_small, 16)
            sp.dma_start(b_rt[:, 0:G], b_gr.broadcast_to([P, G])).then_inc(ld_small, 16)
            sp.dma_start(b_rt[:, G:], b_er.broadcast_to([P, E])).then_inc(ld_small, 16)
            x_t = x[0].rearrange("(t p) d -> p t d", p=P)
            wm = w_mod[0].rearrange("(k p) n -> p k n", p=P)

            def load_mod(n):
                if n >= MOD_BUFS:
                    sp.wait_ge(mod_done, n - MOD_BUFS + 1)
                sec, k = n // KD, n % KD
                sp.dma_start(mod_w[n % MOD_BUFS], wm[:, k, sec * 2 * D:(sec + 1) * 2 * D]).then_inc(ld_mod[n % MOD_BUFS], 16)

            for n in range(MOD_BUFS):
                load_mod(n)
            sp.wait_ge(acc_zero, 1)
            sp.dma_start(acc[0:1, :], b_mod).then_inc(ld_bmod, 16)
            for half in range(2):
                sp.dma_start(x_tok[:, half * 4:half * 4 + 4, :], x_t[:, half * 4:half * 4 + 4, :]).then_inc(ld_x[half], 16)
            for n in range(MOD_BUFS, KD):
                load_mod(n)
            sp.dma_start(win_sb, w_in[0].rearrange("(k p) n -> p k n", p=P)).then_inc(ld_win, 16)
            for n in range(KD, MOD_STEPS):
                load_mod(n)
            sp.wait_ge(mod_done, MOD_STEPS)
            sp.dma_start(wuq_sb, w_uq[0].rearrange("(k p) n -> p k n", p=P)).then_inc(ld_up, 16)
            sp.dma_start(wukv_sb, w_ukv[0].rearrange("(k p) n -> p k n", p=P)).then_inc(ld_up, 16)
            sp.wait_ge(xT_done, 16)
            sp.dma_start(wo_sb, w_o[0].rearrange("(k p) n -> p k n", p=P)).then_inc(ld_wo, 16)

            sp.wait_ge(o_done, H * T)
            sp.dma_start(Ga, ln_g[0, 0:1, :].broadcast_to([P, D])).then_inc(ld_ln, 16)
            sp.dma_start(Ba, ln_b[0, 0:1, :].broadcast_to([P, D])).then_inc(ld_ln, 16)
            for t in range(T):
                if t >= 2:
                    sp.wait_ge(std_in, t - 1)
                sp.dma_start(xs[t % 2], x_t[:, t, :]).then_inc(ld_xs[t % 2], 16)
                if t >= 1:
                    sp.wait_ge(h2_done, t)
                    sp.dma_start(h2_rows[(t - 1) * P:t * P, :], h2[(t - 1) % 2]).then_inc(h2_stored[(t - 1) % 2], 16)
            sp.wait_ge(h2_done, T)
            sp.dma_start(h2_rows[(T - 1) * P:, :], h2[(T - 1) % 2]).then_inc(h2_stored[(T - 1) % 2], 16)

            sp.wait_ge(tiles_known, 1)
            rounds_less = sp.value_load(rounds_i[0:1, 1:2], min_val=T - 2, max_val=TILES_MAX // 2 - 2)

            def expert(j):
                return sp.value_load(te_i[0:1, bass.ds(j, 1)], min_val=0, max_val=E - 1)

            def load_gate_up(e, b):
                for w, at0 in ((w_gate, 0), (w_up, FF)):
                    sp.dma_start(wgu[b][:, :, at0:at0 + FF],
                                 w[0, bass.ds(e, 1)].rearrange("o (p k) n -> p (o k) n", p=P)).then_inc(ld_gu[b], 16)

            def load_down(e, b):
                sp.dma_start(wdn[b], w_down[0, bass.ds(e, 1)].rearrange("o (p k) n -> p (o k) n", p=P)).then_inc(ld_dn[b], 16)

            def refill(i, b, both):
                e_down = expert(i * 2 + (b + 2))
                if both:
                    e_gu = expert(i * 2 + (b + 3))
                    sp.wait_ge(hid_done, i * 2 + (b + 2))
                    load_gate_up(e_gu, 1 - b)
                sp.wait_ge(ye_done, i * 2 + (b + 1))
                load_down(e_down, b)

            for b in range(2):
                e_b = expert(b)
                load_gate_up(e_b, b)
                load_down(e_b, b)
            sp.dma_start(lng2, ln_g[0, 1:2, :].broadcast_to([P, D])).then_inc(ld_ln2, 16)
            sp.dma_start(lnb2, ln_b[0, 1:2, :].broadcast_to([P, D])).then_inc(ld_ln2, 16)
            e_2 = expert(2)
            sp.wait_ge(hid_done, 1)
            load_gate_up(e_2, 0)
            with sp.Fori(0, rounds_less) as i:
                for b in range(2):
                    refill(i, b, True)
            refill(rounds_less, 0, True)
            refill(rounds_less, 1, False)

            sp.wait_ge(y_all, 1)

            for t in range(T):
                for a, dst in ((0, ya), (1, yb)):
                    sp.dma_start(dst[t], y_rows[a * S + t * P:a * S + (t + 1) * P, :]).then_inc(ld_y[t], 16)
            for t in range(T):
                sp.wait_ge(out_done, t + 1)
                sp.dma_start(out[0, t * P:(t + 1) * P, :], yb[t]).then_inc(stored, 16)
            sp.wait_ge(stored, 16 * T)

        @block.tensor
        def _(pe):
            def mm(o, a, b, start, stop):
                return nc.tensor.matmul(o, a, b, start=start, stop=stop, skip_group_check=True)

            pe.wait_ge(consts, 1)
            def xT_group(g):
                half, k = g // KD, g % KD
                pe.wait_ge(ld_x[half], 16)
                if g >= 4:
                    pe.wait_ge(xT_out, g - 3)
                for t in range(4):
                    ins = nc.tensor.transpose(PS[:, 4 + g % 4, t * P:(t + 1) * P],
                                              x_tok[:, half * 4 + t, k * P:(k + 1) * P], ident[:])
                ins.then_inc(xT_done, 1)

            for g in range(4):
                xT_group(g)
            pe.wait_ge(mod_done, KD)
            for j in range(2 * KD):
                ins = mm(PS[:, 0, j:j + 1], acc[:, j * P:(j + 1) * P], ones[:, 0:1], True, True)
            ins.then_inc(cols_done, 1)
            for g in range(4, KD):
                xT_group(g)

            pe.wait_ge(ld_win, 16)
            pe.wait_ge(xT_out, KD)

            def z_tile(t):
                b = 2 * (t % 2)
                if t >= 2:
                    pe.wait_ge(z_out, t - 1)
                for lo, hi in ((0, 512), (512, ZW)):
                    for k in range(KD):
                        ins = mm(PS[:, b + lo // 512, 0:hi - lo], hT[:, k, t * P:(t + 1) * P],
                                 win_sb[:, k, lo:hi], k == 0, k == KD - 1)
                ins.then_inc(z_done, 1)

            def zn_tile(t):
                pe.wait_ge(zn_done, t + 1)
                if t >= 1:
                    pe.wait_ge(znT_out, t)
                for j in range(5):
                    bank, off = (4, j) if j < 3 else (5, j - 3)
                    ins = nc.tensor.transpose(PS[:, bank, off * P:(off + 1) * P], zs[t % 2][:, j * P:(j + 1) * P], ident[:])
                ins.then_inc(znT_done, 1)

            z_tile(0)
            for g in range(KD, 2 * KD):
                xT_group(g)
            pe.wait_ge(xT_out, 2 * KD)
            for t in range(T):
                if t + 1 < T:
                    z_tile(t + 1)
                zn_tile(t)
            pe.wait_ge(krot_done, 1)
            for half in range(2):
                for t in range(4):
                    ins = nc.tensor.transpose(PS[0:ROPE, 6 + half, t * P:(t + 1) * P], k_rot[:, half * 4 + t, :], ident[:])
            ins.then_inc(krT_done, 1)

            pe.wait_ge(ld_up, 32)
            pe.wait_ge(znT_out, T)

            def project(m, hn, hp):
                bank = proj_bank(hn, m)
                if isinstance(hn, int) and hn == 0:
                    if m >= 4:
                        pe.wait_ge(proj_out, m - 1 if m < 6 else m - 3)
                else:
                    pe.wait_ge(proj_out, hn * PROJ + m)
                half = m % 2
                if m < 2:
                    for t in range(4):
                        for k in range(3):
                            ins = mm(PS[:, bank, t * QH:(t + 1) * QH], qlatT[:, k, (half * 4 + t) * P:(half * 4 + t + 1) * P],
                                     wuq_sb[:, k, bass.ds(hn * QH, QH)], k == 0, k == 2)
                elif m < 4:
                    for t in range(4):
                        for k in range(2):
                            ins = mm(PS[:, bank, t * KVH:(t + 1) * KVH], kvlatT[:, k, (half * 4 + t) * P:(half * 4 + t + 1) * P],
                                     wukv_sb[:, k, bass.ds(hn * KVH, KVH)], k == 0, k == 1)
                elif m < 6:
                    pe.sem_inc(k_turn, 1)
                    for t in range(4):
                        ins = nc.tensor.transpose(PS[0:NOPE, bank, t * P:(t + 1) * P], k_h[:, half * 4 + t, :], ident[:])
                else:
                    if m == 6:
                        pe.wait_ge(q_rot, hn + 1)
                    for t in range(4):
                        ins = nc.tensor.transpose(PS[0:QH, bank, t * P:(t + 1) * P], q_h[:, half * 4 + t, :], ident[:])
                ins.then_inc(proj_done, 1)

            def scores(h, hp, i):
                b, w = 2 * (i % 2), (i + 1) * P
                if not (isinstance(h, int) and h == 0 and i < 2):
                    pe.wait_ge(exp_done, h * T + (i - 1))
                if i == 0:
                    pe.wait_ge(proj_out, h * PROJ + PROJ)
                q = qT[hp][0:QH, i * P:(i + 1) * P]
                for lo in range(0, w, 512):
                    hi = min(w, lo + 512)
                    lastc = hi == w
                    mm(PS[:, b + lo // 512, 0:hi - lo], q, kT[hp][0:QH, lo:hi], True, not lastc)
                    if lastc:
                        ins = mm(PS[:, b + lo // 512, hi - lo - P:hi - lo], ident_bf[:], causal_bf[:], False, True)
                ins.then_inc(s_done, 1)

            def turn(h, i):
                pe.wait_ge(exp_done, h * T + (i + 1))
                for g in range(1 if i < 4 else 2):
                    n = group_at(i) + g
                    if not (isinstance(h, int) and h == 0 and n < 2):
                        pe.wait_ge(pT_out, h * 12 + (n - 1))
                    for k in range(4 * g, min(4 * g + 4, i + 1)):
                        ins = nc.tensor.transpose(PS[:, 4 + n % 2, (k % 4) * P:(k % 4 + 1) * P],
                                                  probs[i % 2][:, k * P:(k + 1) * P], ident[:])
                    ins.then_inc(pT_done, 1)

            def values(h, hp, i):
                pe.wait_ge(pT_out, h * 12 + (group_at(i) + (1 if i < 4 else 2)))
                if not (isinstance(h, int) and h == 0 and i == 0):
                    pe.wait_ge(o_out, h * T + i)
                for k in range(i + 1):
                    ins = mm(PS[:, 7, 0:VH], pT[i % 2][:, k, :], v_h[hp][:, k, :], k == 0, k == i)
                ins.then_inc(o_done, 1)

            def head(h, hp, first, nxt):
                for i in range(T):
                    if nxt and i == 7:
                        project(i, h + 1, 1 - hp)
                    scores(h, hp, i)
                    if nxt and i < 7:
                        project(i, h + 1, 1 - hp)
                    if i >= 1:
                        turn(h, i - 1)
                    elif not first:
                        turn(h - 1, T - 1)
                    if i >= 2:
                        values(h, hp, i - 2)
                    elif not first:
                        values(h - 1, 1 - hp, T - 2 + i)

            pe.wait_ge(krT_out, 1)
            for m in range(PROJ):
                project(m, 0, 0)
            head(0, 0, True, True)
            with pe.Fori(0, (H - 2) // 2) as hh:
                for q in range(2):
                    head(hh * 2 + (1 + q), 1 - q, False, True)
            head(H - 1, 1, False, False)
            turn(H - 1, T - 1)
            values(H - 1, 1, T - 2)
            values(H - 1, 1, T - 1)

            pe.wait_ge(o_out, H * T)
            pe.wait_ge(mod_done, MOD_STEPS)
            def mod_row(m):
                sec, half = (2, 4, 3, 5)[m // 2], m % 2
                if m >= 2:
                    pe.wait_ge(bc_out, m - 1)
                mm(PS[:, 6 + m % 2, :], ones[:], acc[:, sec * D + half * 512:sec * D + half * 512 + 512],
                   True, True).then_inc(bc_done, 1)

            mod_row(0)
            mod_row(1)

            pe.wait_ge(ld_wo, 16)

            def turn_o(t):
                if t >= 1:
                    pe.wait_ge(oT_out, 2 * t)
                for half in range(2):
                    for k in range(4):
                        ins = nc.tensor.transpose(PS[:, half, k * P:(k + 1) * P],
                                                  o_tok[:, t, (half * 4 + k) * P:(half * 4 + k + 1) * P], ident[:])
                    ins.then_inc(oT_done, 1)

            def out_proj(t):
                pe.wait_ge(oT_out, 2 * t + 2)
                if t >= 2:
                    pe.wait_ge(yo_used, t - 1)
                for half in range(2):
                    for k in range(KD):
                        ins = mm(PS[:, 2 + 2 * (t % 2) + half, :], oT[t % 2][:, k, :],
                                 wo_sb[:, k, half * 512:(half + 1) * 512], k == 0, k == KD - 1)
                ins.then_inc(yo_done, 1)

            def route(t):
                pe.wait_ge(h2_done, t + 1)
                for half in range(2):
                    if t >= 1 or half == 1:
                        pe.wait_ge(h2T_out, 2 * t + half)
                    else:
                        pe.wait_ge(bc_out, 8)
                    for k in range(4):
                        ins = nc.tensor.transpose(PS[:, 6, k * P:(k + 1) * P],
                                                  h2[t % 2][:, (half * 4 + k) * P:(half * 4 + k + 1) * P], ident[:])
                    ins.then_inc(h2T_done, 1)
                pe.wait_ge(h2T_out, 2 * t + 2)
                if t >= 1:
                    pe.wait_ge(lg_out, t)
                for k in range(KD):
                    ins = mm(PS[:, 7, 0:G + E], h2T[:, k, :], w_rt[:, k, :], k == 0, k == KD - 1)
                ins.then_inc(lg_done, 1)

            turn_o(0)
            for t in range(T):
                if t + 1 < T:
                    turn_o(t + 1)
                out_proj(t)
                if t == 0:
                    for m in range(2, 8):
                        mod_row(m)
                else:
                    route(t - 1)
            route(T - 1)

            pe.wait_ge(member_done, 1)
            for t in range(T):
                for u in range(t + 1):
                    mm(PS[:, 0, t * E:(t + 1) * E], before_bf[:] if u == t else ones_bf[:], member[:, u, :], u == 0, u == t)
            for u in range(T):
                ins = mm(PS[:, 1, 0:E], ones_bf[:], member[:, u, :], u == 0, u == T - 1)
            ins.then_inc(rank_done, 1)
            for n in range(TOPK * T):
                if n % 4 == 0:
                    pe.wait_ge(hot_done, n // 4 + 1)
                ins = mm(PS[:, 2, 0:2 * TILES_MAX], hot_in[:, n // T, n % T, :], hot_dv[:, n].rearrange("p a j -> p (a j)"),
                         n == 0, n == TOPK * T - 1)
            ins.then_inc(idx_acc, 1)

            pe.wait_ge(table_done, 1)
            rounds = pe.value_load(rounds_i[0:1, 0:1], min_val=T - 1, max_val=TILES_MAX // 2 - 1)

            def turn_rows(i, b):
                pe.wait_ge(gathered[b], i * 16 + 16)
                if not (isinstance(i, int) and i == 0 and b == 0):
                    pe.wait_ge(xgT_outA, i * 2 + b)
                    pe.wait_ge(xgT_outV, i * 2 + b)
                rows = xg[b].rearrange("p (q k) -> p k q", k=KD)
                for half in range(2):
                    for k in range(4):
                        ins = nc.tensor.transpose(PS[:, half, k * P:(k + 1) * P], rows[:, half * 4 + k, :], ident[:])
                ins.then_inc(xgT_done, 1)

            def hidden(i, b):
                pe.wait_ge(ld_gu[b], i * 32 + 32)
                pe.wait_ge(xgT_outA, i * 2 + (b + 1))
                pe.wait_ge(xgT_outV, i * 2 + (b + 1))
                for k in range(KD):
                    ins = mm(PS[:, 2 + b, :], xgT[b][:, k, :], wgu[b][:, k, :], k == 0, k == KD - 1)
                ins.then_inc(hid_done, 1)

            def turn_hidden(i, b):
                pe.wait_ge(he_done, i * 2 + (b + 1))
                for k in range(2):
                    ins = nc.tensor.transpose(PS[:, 4, k * P:(k + 1) * P], he[b].rearrange("p (q k) -> p k q", k=2)[:, k, :], ident[:])
                ins.then_inc(heT_done, 1)

            def down(i, b):
                pe.wait_ge(heT_out, i * 2 + (b + 1))
                pe.wait_ge(ld_dn[b], i * 16 + 16)
                pe.wait_ge(ye_out, i * 2 + (b + 1))
                for half in range(2):
                    for k in range(2):
                        ins = mm(PS[:, 6 + half, :], heT[b][:, k, :], wdn[b][:, k, half * 512:(half + 1) * 512], k == 0, k == 1)
                ins.then_inc(ye_done, 1)

            turn_rows(0, 0)
            hidden(0, 0)
            turn_rows(0, 1)
            with pe.Fori(0, rounds) as i:
                for b in range(2):
                    turn_hidden(i, b)
                    hidden(i + b, 1 - b)
                    turn_rows(i + 1, b)
                    down(i, b)
            turn_hidden(rounds, 0)
            hidden(rounds, 1)
            down(rounds, 0)
            turn_hidden(rounds, 1)
            down(rounds, 1)

        @block.scalar
        def _(act):
            act.wait_ge(ld_small, 16 * 8)
            nc.scalar.activation(c_act[:], c_col[:], ACT.Silu).then_inc(c_ready, 1)
            act.wait_ge(cols_out, 1)
            for g in range(16):
                half, k = g // KD, g % KD
                act.wait_ge(xT_done, g + 1)
                nc.scalar.activation(hT[:, k, half * 512:(half + 1) * 512], PS[:, 4 + g % 4, :], ACT.Identity,
                                     bias=mod_cols[:, k:k + 1], scale=mod_cols[:, KD + k:KD + k + 1]).then_inc(xT_out, 1)
            act.wait_ge(ang_done, 1)
            nc.scalar.activation(sin_t[:], ang[:], ACT.Sin)
            nc.scalar.activation(cos_t[:], turns[:], ACT.Sin).then_inc(trig_done, 1)
            for t in range(T):
                act.wait_ge(z_out, t + 1)
                nc.scalar.activation(sq_junk, zs[t % 2][:, 0:QL], ACT.Square, scale=QL ** -0.5, accum_out=ms[:, t, 0:1]).then_inc(ms_done, 1)
                act.wait_ge(ms_done, 2 * t + 1)
                nc.scalar.activation(sq_junk[:, 0:KVL], zs[t % 2][:, QL:QL + KVL], ACT.Square, scale=KVL ** -0.5,
                                     accum_out=ms[:, t, 1:2]).then_inc(ms_done, 1)
                act.wait_ge(ms_done, 2 * t + 2)
                nc.scalar.activation(rms[:, t, :], ms[:, t, :], ACT.Sqrt, bias=eps_rms[:]).then_inc(rms_done, 1)
                act.wait_ge(znT_done, t + 1)
                for j in range(5):
                    src = PS[:, 4, j * P:(j + 1) * P] if j < 3 else PS[:, 5, (j - 3) * P:(j - 2) * P]
                    dst = qlatT[:, j, t * P:(t + 1) * P] if j < 3 else kvlatT[:, j - 3, t * P:(t + 1) * P]
                    gw = qg_col[:, j:j + 1] if j < 3 else kvg_col[:, j - 3:j - 2]
                    ins = nc.scalar.activation(dst, src, ACT.Copy, scale=gw)
                ins.then_inc(znT_out, 1)
            act.wait_ge(krT_done, 1)
            for q in range(2):
                for half in range(2):
                    ins = nc.scalar.activation(kT[q][NOPE:QH, half * 512:(half + 1) * 512], PS[0:ROPE, 6 + half, :], ACT.Copy)
            ins.then_inc(krT_out, 1)

            def copy_out(m, hn, hp):
                act.wait_ge(proj_done, hn * PROJ + (m + 1))
                half, bank = m % 2, proj_bank(hn, m)
                ts = slice(half * 4, half * 4 + 4)
                if m < 2:
                    ins = nc.scalar.activation(q_h[:, ts, :], PS[:, bank, 0:4 * QH].rearrange("p (t d) -> p t d", t=4), ACT.Copy)
                elif m < 4:
                    src = PS[:, bank, :].rearrange("p (t d) -> p t d", t=4)
                    nc.scalar.activation(k_h[:, ts, :], src[:, :, 0:NOPE], ACT.Copy)
                    ins = nc.scalar.activation(v_h[hp][:, ts, :], src[:, :, NOPE:], ACT.Copy)
                elif m < 6:
                    ins = nc.scalar.activation(kT[hp][0:NOPE, half * 512:(half + 1) * 512], PS[0:NOPE, bank, :], ACT.Copy)
                else:
                    ins = nc.scalar.activation(qT[hp][0:QH, half * 512:(half + 1) * 512], PS[0:QH, bank, :], ACT.Copy, scale=SCALE)
                ins.then_inc(proj_out, 1)

            def softmax(h, hp, i):
                act.wait_ge(max_done, h * T + (i + 1))
                if not (isinstance(h, int) and h == 0 and i < 2):
                    act.wait_ge(pT_done, h * 12 + (group_at(i - 2) + (1 if 0 <= i - 2 < 4 else 2)))
                b, w = 2 * (i % 2), (i + 1) * P
                nc.scalar.activation(probs[i % 2][:, 0:w], PS[:, b:b + 2, :].rearrange("p a n -> p (a n)")[:, 0:w], ACT.Exp,
                                     bias=neg_max[:, i:i + 1], accum_out=row_sum[:, hp * T + i:hp * T + i + 1]).then_inc(exp_done, 1)

            def head(h, hp, nxt):
                for i in range(T):
                    if nxt and i == 7:
                        copy_out(i, h + 1, 1 - hp)
                    softmax(h, hp, i)
                    if nxt and i < 7:
                        copy_out(i, h + 1, 1 - hp)

            for m in range(PROJ):
                copy_out(m, 0, 0)
            head(0, 0, True)
            with act.Fori(0, (H - 2) // 2) as hh:
                for q in range(2):
                    head(hh * 2 + (1 + q), 1 - q, True)
            head(H - 1, 1, False)

            act.wait_ge(o_done, H * T)
            for t in range(T):
                def oT_copy(t):
                    if t >= 2:
                        act.wait_ge(yo_done, t - 1)
                    for half in range(2):
                        act.wait_ge(oT_done, 2 * t + half + 1)
                        nc.scalar.activation(oT[t % 2][:, half * 4:half * 4 + 4, :],
                                             PS[:, half, :].rearrange("p (k q) -> p k q", k=4), ACT.Copy).then_inc(oT_out, 1)

                if t == 0:
                    oT_copy(0)
                if t + 1 < T:
                    oT_copy(t + 1)
                act.wait_ge(std_in, t + 1)
                nc.scalar.activation(std[:, t:t + 1], mv[:, t, 1:2], ACT.Sqrt, bias=eps_ln[:]).then_inc(std_done, 1)
                for half in range(2):
                    act.wait_ge(h2T_done, 2 * t + half + 1)
                    if half == 0 and t >= 1:
                        act.wait_ge(lg_done, t)
                    nc.scalar.activation(h2T[:, half * 4:half * 4 + 4, :],
                                         PS[:, 6, :].rearrange("p (k q) -> p k q", k=4), ACT.Copy).then_inc(h2T_out, 1)

            act.wait_ge(rt_exp_in, 1)
            nc.scalar.activation(g_exp[:], g_exp[:], ACT.Exp)
            nc.scalar.activation(e_exp[:], e_dif[:], ACT.Exp).then_inc(rt_exp, 1)

            act.wait_ge(table_done, 1)
            rounds = act.value_load(rounds_i[0:1, 0:1], min_val=T - 1, max_val=TILES_MAX // 2 - 1)

            def rows_out(i, b):
                act.wait_ge(xgT_done, i * 2 + (b + 1))
                nc.scalar.activation(xgT[b][:, 0:4, :], PS[:, 0, :].rearrange("p (k q) -> p k q", k=4), ACT.Copy).then_inc(xgT_outA, 1)

            def silu(i, b):
                act.wait_ge(hid_done, i * 2 + (b + 1))
                nc.scalar.activation(sil[b], PS[:, 2 + b, 0:FF], ACT.Silu).then_inc(silu_done, 1)

            rows_out(0, 0)
            silu(0, 0)
            rows_out(0, 1)
            with act.Fori(0, rounds) as i:
                for b in range(2):
                    silu(i + b, 1 - b)
                    rows_out(i + 1, b)
            silu(rounds, 1)

            for t in range(T):
                act.wait_ge(std_in, T + t + 1)
                nc.scalar.activation(std[:, T + t:T + t + 1], mv[:, T + t, 1:2], ACT.Sqrt, bias=eps_ln[:]).then_inc(std_done, 1)
                act.wait_ge(shift_done, t + 1)
                nc.scalar.activation(ya[t], ya[t], ACT.Identity, bias=shift[:, t:t + 1],
                                     scale=rstd[:, T + t:T + t + 1]).then_inc(norm_done, 1)

        @block.vector
        def _(dve):
            links = [0]

            def then(ins):
                links[0] += 1
                ins.then_inc(vec, 1)
                dve.wait_ge(vec, links[0])

            dve_ = nc.vector
            dve_.memset(acc, 0.0).then_inc(acc_zero, 1)
            dve_.memset(eps_rms[:], RMS_EPS)
            then(dve_.memset(eps_ln[:], LN_EPS))
            dve.wait_ge(c_ready, 1)
            dve.wait_ge(ld_bmod, 16)
            dve.wait_ge(acc_zero, 1)

            def mod_step(n):
                sec, k = n // KD, n % KD
                a = acc[:, sec * 2 * D:(sec + 1) * 2 * D]
                dve.wait_ge(ld_mod[n % MOD_BUFS], 16 * (n // MOD_BUFS + 1))
                if n >= 1:
                    dve.wait_ge(mod_done, n)
                dve_.scalar_tensor_tensor(out=a, in0=mod_w[n % MOD_BUFS], scalar=c_act[:, k:k + 1], in1=a,
                                          op0=ALU.mult, op1=ALU.add).then_inc(mod_done, 1)

            for n in range(KD):
                mod_step(n)
            dve.wait_ge(cols_done, 1)
            dve_.tensor_copy(mod_cols[:, 0:KD], PS[:, 0, 0:KD])
            dve_.tensor_scalar(mod_cols[:, KD:], PS[:, 0, KD:2 * KD], 1.0, None, ALU.add).then_inc(cols_out, 1)

            for n in range(KD, KD + 6):
                mod_step(n)
            dve.wait_ge(consts, 1)
            then(dve_.tensor_copy(pos_f[:], pos_i[:]))
            then(dve_.tensor_tensor(ang[:], pos_f[:].unsqueeze(2).broadcast_to([P, T, HR]),
                                    freq[:].unsqueeze(1).broadcast_to([P, T, HR]), ALU.mult))
            then(dve_.tensor_scalar(turns[:], ang[:], float(1.0 / TWO_PI), ROUND, ALU.mult, ALU.add))
            then(dve_.tensor_scalar(turns[:], turns[:], -ROUND, None, ALU.add))
            for part in (TWO_PI_HI, TWO_PI_MID, TWO_PI_LO):
                then(dve_.scalar_tensor_tensor(out=ang[:], in0=turns[:], scalar=-part, in1=ang[:], op0=ALU.mult, op1=ALU.add))
            then(dve_.tensor_scalar(turns[:], ang[:], float(np.pi / 2), None, ALU.add))
            then(dve_.tensor_scalar(cos_t[:], turns[:], float(np.pi), -TWO_PI, ALU.is_gt, ALU.mult))
            then(dve_.tensor_tensor(turns[:], turns[:], cos_t[:], ALU.add))
            then(dve_.tensor_scalar(turns[:], turns[:], PI_F, -PI_F, ALU.min, ALU.max))
            dve_.tensor_scalar(ang[:], ang[:], PI_F, -PI_F, ALU.min, ALU.max).then_inc(ang_done, 1)

            for t in range(T):
                dve.wait_ge(z_done, t + 1)
                if t >= 2:
                    dve.wait_ge(znT_done, t - 1)
                b = 2 * (t % 2)
                z_flat = PS[:, b:b + 2, :].rearrange("p a n -> p (a n)")
                dve_.tensor_copy(k_rope[:, t, :], z_flat[:, QL + KVL:ZW])
                dve_.tensor_copy(zs[t % 2][:, 0:QL + KVL], z_flat[:, 0:QL + KVL]).then_inc(z_out, 1)
                for n in range(KD + 6 + 2 * t, min(KD + 8 + 2 * t, MOD_STEPS)):
                    mod_step(n)
                dve.wait_ge(rms_done, t + 1)
                then(dve_.reciprocal(rrms[:, t, :], rms[:, t, :]))
                dve_.tensor_scalar(zs[t % 2][:, 0:QL], zs[t % 2][:, 0:QL], rrms[:, t, 0:1], None, ALU.mult)
                dve_.tensor_scalar(zs[t % 2][:, QL:QL + KVL], zs[t % 2][:, QL:QL + KVL], rrms[:, t, 1:2], None,
                                   ALU.mult).then_inc(zn_done, 1)

            def row_max(h, i):
                dve.wait_ge(s_done, h * T + (i + 1))
                b, w = 2 * (i % 2), (i + 1) * P
                dve_.tensor_reduce(neg_max[:, i:i + 1], PS[:, b:b + 2, :].rearrange("p a n -> p (a n)")[:, 0:w], AX.X, ALU.max,
                                   negate=True).then_inc(max_done, 1)

            def turned(h, i):
                for g in range(1 if i < 4 else 2):
                    n = group_at(i) + g
                    dve.wait_ge(pT_done, h * 12 + (n + 1))
                    if g == 0 and not (isinstance(h, int) and h == 0 and i < 2):
                        dve.wait_ge(o_done, h * T + (i - 1))
                    k0, k1 = 4 * g, min(4 * g + 4, i + 1)
                    dve_.tensor_copy(pT[i % 2][:, k0:k1, :],
                                     PS[:, 4 + n % 2, 0:(k1 - k0) * P].rearrange("p (k q) -> p k q", k=k1 - k0)).then_inc(pT_out, 1)

            def finish(h, hp, i):
                dve.wait_ge(exp_done, h * T + (i + 1))
                dve_.reciprocal(inv_sum[:, i:i + 1], row_sum[:, hp * T + i:hp * T + i + 1]).then_inc(inv_done, 1)
                dve.wait_ge(o_done, h * T + (i + 1))
                dve.wait_ge(inv_done, h * T + (i + 1))
                dve_.tensor_scalar(o_tok[:, i, bass.ds(h * VH, VH)], PS[:, 7, 0:VH], inv_sum[:, i:i + 1], None,
                                   ALU.mult).then_inc(o_out, 1)

            def head(h, hp, first):
                for i in range(T):
                    row_max(h, i)
                    if i >= 1:
                        turned(h, i - 1)
                    elif not first:
                        turned(h - 1, T - 1)
                    if i >= 2:
                        finish(h, hp, i - 2)
                    elif not first:
                        finish(h - 1, 1 - hp, T - 2 + i)

            head(0, 0, True)
            with dve.Fori(0, (H - 2) // 2) as hh:
                for q in range(2):
                    head(hh * 2 + (1 + q), 1 - q, False)
            head(H - 1, 1, False)
            turned(H - 1, T - 1)
            finish(H - 1, 1, T - 2)
            finish(H - 1, 1, T - 1)

            dve.wait_ge(ld_ln, 32)
            for m in range(8):
                half = slice((m % 2) * 512, (m % 2) * 512 + 512)
                src = PS[:, 6 + m % 2, :]
                dve.wait_ge(bc_done, m + 1)
                if m < 2:
                    ins = dve_.tensor_scalar(g1p[:, half], src, 1.0, None, ALU.add)
                elif m < 4:
                    dve_.scalar_tensor_tensor(out=A2[:, half], in0=src, scalar=1.0, in1=Ga[:, half], op0=ALU.add, op1=ALU.mult)
                    ins = dve_.scalar_tensor_tensor(out=B2[:, half], in0=src, scalar=1.0, in1=Ba[:, half], op0=ALU.add, op1=ALU.mult)
                elif m < 6:
                    dve.wait_ge(bc_out, m - 1)
                    ins = dve_.tensor_tensor(B2[:, half], src, B2[:, half], ALU.add)
                else:
                    ins = dve_.tensor_scalar(g2p[:, half], src, 1.0, None, ALU.add)
                ins.then_inc(bc_out, 1)
            dve.wait_ge(bc_out, 8)
            then(dve_.tensor_scalar(Ga, Ga, ALPHA, None, ALU.mult))
            then(dve_.tensor_scalar(Ba, Ba, ALPHA, None, ALU.mult))

            def normalise(t, r):
                dve_.bn_stats(bn[:, 0, :], r[:, 0:512])
                then(dve_.bn_stats(bn[:, 1, :], r[:, 512:D]))
                dve_.bn_aggr(mv[:, t, :], bn[:].rearrange("p a b -> p (a b)")).then_inc(std_in, 1)
                dve.wait_ge(std_done, t + 1)
                then(dve_.reciprocal(rstd[:, t:t + 1], std[:, t:t + 1]))
                then(dve_.tensor_scalar(r, r, mv[:, t, 0:1], rstd[:, t:t + 1], ALU.subtract, ALU.mult))

            def choose(t):
                dve.wait_ge(lg_done, t + 1)
                dve_.tensor_tensor(logits[:, t, :], PS[:, 7, 0:G + E], b_rt[:], ALU.add).then_inc(lg_out, 1)
                dve.wait_ge(lg_out, t + 1)
                then(dve_.tensor_copy(gl[:, t, 0:G], logits[:, t, 0:G]))
                then(dve_.max(g_top[:, t, :], gl[:, t, :]))
                then(dve_.max_index(g_idx[:, t, :], g_top[:, t, :], gl[:, t, :]))
                then(dve_.tensor_copy(g_idf[:, t:t + 1], g_idx[:, t, 0:1]))
                then(dve_.tensor_scalar(g_hot[:, t, :], iota_row[:, 0:G], g_idf[:, t:t + 1], None, ALU.is_equal))
                then(dve_.tensor_tensor(e_sel, logits[:, t, G:].rearrange("p (g e) -> p g e", g=G),
                                        g_hot[:, t, :].unsqueeze(2).broadcast_to([P, G, EPG]), ALU.mult))
                then(dve_.tensor_reduce(e_in[:, t, :], e_sel.rearrange("p g e -> p e g"), AX.X, ALU.add))
                then(dve_.max(e_top[:, t, :], e_in[:, t, :]))
                dve_.max_index(e_idx[:, t, :], e_top[:, t, :], e_in[:, t, :])

            then(dve_.memset(gl[:], -BIG))
            for t in range(T):
                r = r_buf[t % 2]
                dve.wait_ge(yo_done, t + 1)
                b = 2 + 2 * (t % 2)
                y = PS[:, b:b + 2, :].rearrange("p a n -> p (a n)")
                dve.wait_ge(ld_xs[t % 2], 16 * (t // 2 + 1))
                if t >= 2:
                    dve.wait_ge(xa_done, t - 1)
                dve_.tensor_tensor(r, y, g1p, ALU.mult).then_inc(yo_used, 1)
                dve.wait_ge(yo_used, t + 1)
                then(dve_.scalar_tensor_tensor(out=r, in0=xs[t % 2], scalar=ALPHA, in1=r, op0=ALU.mult, op1=ALU.add))
                normalise(t, r)
                if t >= 2:
                    dve.wait_ge(h2_stored[t % 2], 16 * (t // 2))
                    dve.wait_ge(h2T_done, 2 * (t - 1))
                then(dve_.tensor_tensor(h2[t % 2], r, A2, ALU.mult))
                dve_.tensor_tensor(h2[t % 2], h2[t % 2], B2, ALU.add).then_inc(h2_done, 1)
                if t >= 1:
                    choose(t - 1)
            for b in range(2):
                ins = dve_.memset(xg[b], 0.0)
            then(ins)
            choose(T - 1)

            dve.wait_ge(xa_done, T)
            then(dve_.memset(idx_f[:], 0.0))
            dve_.tensor_tensor(g_exp[:], logits[:, :, 0:G], g_top[:, :, 0:1].broadcast_to([P, T, G]), ALU.subtract)
            dve_.tensor_tensor(e_dif[:], e_top[:, :, 1], e_top[:, :, 0], ALU.subtract).then_inc(rt_exp_in, 1)
            for a in range(TOPK):
                then(dve_.tensor_copy(e_idf[:, a, :], e_idx[:, :, a]))
                then(dve_.scalar_tensor_tensor(out=e_idf[:, a, :], in0=g_idf[:], scalar=float(EPG), in1=e_idf[:, a, :],
                                               op0=ALU.mult, op1=ALU.add))
                then(dve_.tensor_tensor(hot[:, a], iota_row[:, 0:E].unsqueeze(1).broadcast_to([P, T, E]),
                                        e_idf[:, a, :].unsqueeze(2).broadcast_to([P, T, E]), ALU.is_equal))
            dve_.tensor_tensor(member[:], hot[:, 0], hot[:, 1], ALU.add).then_inc(member_done, 1)
            dve.wait_ge(rt_exp, 1)
            then(dve_.tensor_reduce(g_den[:], g_exp[:], AX.X, ALU.add))
            then(dve_.reciprocal(g_p[:], g_den[:]))
            then(dve_.tensor_scalar(e_den[:], e_exp[:], 1.0, None, ALU.add))
            then(dve_.reciprocal(e_den[:], e_den[:]))
            then(dve_.tensor_tensor(wts[:, 0, :], e_den[:], g_p[:], ALU.mult))
            then(dve_.tensor_tensor(wts[:, 1, :], wts[:, 0, :], e_exp[:], ALU.mult))
            dve.wait_ge(rank_done, 1)
            then(dve_.tensor_copy(count[:], PS[:, 1, 0:E]))
            then(dve_.tensor_tensor(over, count[:].unsqueeze(2).broadcast_to([P, E, T]),
                                    iota_tiles[:].unsqueeze(1).broadcast_to([P, E, T]), ALU.is_gt))
            then(dve_.tensor_reduce(n_tiles[:], over, AX.X, ALU.add))
            then(dve_.tensor_tensor_scan(tile_end[:], ones[:, 0:E], n_tiles[:], 0.0, ALU.mult, ALU.add))
            then(dve_.tensor_tensor(te_cmp, iota_row[0:1, 0:LOOP_TABLE].unsqueeze(2).broadcast_to([1, LOOP_TABLE, E]),
                                    tile_end[0:1, :].unsqueeze(1).broadcast_to([1, LOOP_TABLE, E]), ALU.is_ge))
            then(dve_.tensor_reduce(te_f[:], te_cmp, AX.X, ALU.add))
            then(dve_.tensor_scalar(te_f[:], te_f[:], float(E - 1), None, ALU.min))
            then(dve_.tensor_copy(te_i[:], te_f[:]))
            then(dve_.tensor_scalar(rounds_f[:, 0:1], tile_end[0:1, E - 1:E], 0.5, 0.25, ALU.mult, ALU.add))
            then(dve_.tensor_scalar(rounds_f[:, 0:1], rounds_f[:, 0:1], ROUND, -ROUND - 1.0, ALU.add, ALU.add))
            then(dve_.tensor_scalar(rounds_f[:, 1:2], rounds_f[:, 0:1], -1.0, None, ALU.add))
            dve_.tensor_copy(rounds_i[:], rounds_f[:]).then_inc(tiles_known, 1)
            then(dve_.tensor_tensor(base[:], tile_end[:], n_tiles[:], ALU.subtract))
            then(dve_.scalar_tensor_tensor(out=place, in0=base[:].unsqueeze(1).broadcast_to([P, T, E]), scalar=float(P),
                                           in1=PS[:, 0, 0:T * E].rearrange("p (t e) -> p t e", t=T), op0=ALU.mult, op1=ALU.add))
            for a in range(TOPK):
                then(dve_.tensor_tensor(picked[:, a], hot[:, a], place, ALU.mult))
            then(dve_.tensor_reduce(slot[:], picked, AX.X, ALU.add))
            then(dve_.tensor_scalar(slot_dv[:], slot[:], 1.0 / P, -0.5 + 0.5 / P, ALU.mult, ALU.add))
            then(dve_.tensor_scalar(slot_dv[:], slot_dv[:], ROUND, None, ALU.add))
            then(dve_.tensor_scalar(slot_dv[:], slot_dv[:], -ROUND, None, ALU.add))
            dve_.scalar_tensor_tensor(out=slot_in[:], in0=slot_dv[:], scalar=-float(P), in1=slot[:], op0=ALU.mult,
                                      op1=ALU.add).then_inc(place_known, 1)
            then(dve_.tensor_tensor(hot_dv[:, :, 1, :], iota_row[:, 0:TILES_MAX].unsqueeze(1).broadcast_to([P, TOPK * T, TILES_MAX]),
                                    slot_dv[:].rearrange("p a t -> p (a t)").unsqueeze(2).broadcast_to([P, TOPK * T, TILES_MAX]),
                                    ALU.is_equal))
            then(dve_.tensor_tensor(hot_dv[:, :, 0, :], hot_dv[:, :, 1, :],
                                    row_id[:].unsqueeze(2).broadcast_to([P, TOPK * T, TILES_MAX]), ALU.mult))
            dve_.tensor_tensor(hot_dv[:, :, 1, :], hot_dv[:, :, 1, :],
                               wts[:].rearrange("p a t -> p (a t)").unsqueeze(2).broadcast_to([P, TOPK * T, TILES_MAX]), ALU.mult)
            dve.wait_ge(place_known, 1)
            for n in range(0, TOPK * T, 4):
                a, ts = n // T, slice(n % T, n % T + 4)
                dve_.tensor_tensor(hot_in[:, a, ts, :], iota_row[:].unsqueeze(1).broadcast_to([P, 4, P]),
                                   slot_in[:, a, ts].unsqueeze(2).broadcast_to([P, 4, P]), ALU.is_equal).then_inc(hot_done, 1)
            dve.wait_ge(idx_acc, 1)
            dve_.tensor_copy(slot_w[:, 0:TILES_MAX], PS[:, 2, TILES_MAX:2 * TILES_MAX])
            then(dve_.tensor_copy(idx_f[:, 0:TILES_MAX], PS[:, 2, 0:TILES_MAX]))
            then(dve_.tensor_scalar(pad[:], idx_f[:], 0.0, 4.0 * S, ALU.is_equal, ALU.mult))
            then(dve_.scalar_tensor_tensor(out=row_f[:], in0=idx_f[:], scalar=-1.0, in1=pad[:], op0=ALU.add, op1=ALU.add))
            then(dve_.tensor_copy(dst_u[:], row_f[:]))
            then(dve_.tensor_scalar(past[:], row_f[:], float(S) - 0.5, -float(S), ALU.is_gt, ALU.mult))
            then(dve_.tensor_tensor(row_f[:], row_f[:], past[:], ALU.add))
            dve_.tensor_copy(idx_u[:], row_f[:]).then_inc(table_done, 1)

            dve.wait_ge(table_done, 1)
            rounds = dve.value_load(rounds_i[0:1, 0:1], min_val=T - 1, max_val=TILES_MAX // 2 - 1)

            def rows_out(i, b):
                dve.wait_ge(xgT_done, i * 2 + (b + 1))
                dve_.tensor_copy(xgT[b][:, 4:8, :], PS[:, 1, :].rearrange("p (k q) -> p k q", k=4)).then_inc(xgT_outV, 1)

            def gated(i, b):
                dve.wait_ge(silu_done, i * 2 + (b + 1))
                dve_.tensor_tensor(he[b], PS[:, 2 + b, FF:], sil[b], ALU.mult).then_inc(he_done, 1)

            def hidden_out(i, b):
                dve.wait_ge(heT_done, i * 2 + (b + 1))
                dve_.tensor_copy(heT[b], PS[:, 4, 0:2 * P].rearrange("p (k q) -> p k q", k=2)).then_inc(heT_out, 1)

            def result_out(i, b):
                dve.wait_ge(ye_done, i * 2 + (b + 1))
                dve.wait_ge(y_free, i * 2 + (b + 1))
                dve_.scalar_tensor_tensor(out=y_e[b], in0=PS[:, 6:8, :].rearrange("p a n -> p (a n)"),
                                          scalar=slot_w[:, bass.ds(i * 2 + b, 1)], in1=g2p, op0=ALU.mult, op1=ALU.mult).then_inc(ye_out, 1)

            dve.sem_inc(ye_out, 1)
            rows_out(0, 0)
            gated(0, 0)
            rows_out(0, 1)
            with dve.Fori(0, rounds) as i:
                for b in range(2):
                    hidden_out(i, b)
                    gated(i + b, 1 - b)
                    rows_out(i + 1, b)
                    result_out(i, b)
            hidden_out(rounds, 0)
            gated(rounds, 1)
            result_out(rounds, 0)
            hidden_out(rounds, 1)
            result_out(rounds, 1)

            dve.wait_ge(ld_ln2, 32)

            def residual(t):
                dve.wait_ge(ld_y[t], 32)
                if t % POOL_ADDS == POOL_ADDS - 1:
                    dve.wait_ge(added, t // POOL_ADDS + 1)
                else:
                    then(dve_.tensor_tensor(ya[t], ya[t], yb[t], ALU.add))
                then(dve_.tensor_tensor(ya[t], ya[t], xa[:, t, :], ALU.add))
                dve_.bn_stats(bn[:, 0, :], ya[t][:, 0:512])
                then(dve_.bn_stats(bn[:, 1, :], ya[t][:, 512:D]))
                dve_.bn_aggr(mv[:, T + t, :], bn[:].rearrange("p a b -> p (a b)")).then_inc(std_in, 1)

            def shifts(t):
                dve.wait_ge(std_done, T + t + 1)
                then(dve_.reciprocal(rstd[:, T + t:T + t + 1], std[:, T + t:T + t + 1]))
                dve_.scalar_tensor_tensor(out=shift[:, t:t + 1], in0=mv[:, T + t, 0:1], scalar=-1.0, in1=rstd[:, T + t:T + t + 1],
                                          op0=ALU.mult, op1=ALU.mult).then_inc(shift_done, 1)

            def weigh(t):
                dve.wait_ge(norm_done, t + 1)
                dve_.tensor_tensor(ya[t], ya[t], lng2, ALU.mult).then_inc(scaled, 1)

            for t in range(T + 2):
                if t < T:
                    residual(t)
                if 1 <= t <= T:
                    shifts(t - 1)
                if t >= 2:
                    weigh(t - 2)

        @block.gpsimd
        def _(pool):
            links = [0]

            def then(ins):
                links[0] += 1
                ins.then_inc(pol, 1)
                pool.wait_ge(pol, links[0])

            g_ = nc.gpsimd
            g_.memset(ident[:], 0.0)
            g_.memset(ones[:], 1.0)
            g_.memset(causal_bf[:], 0.0)
            g_.memset(ident_bf[:], 0.0)
            then(g_.memset(ones_bf[:], 1.0))
            for m in (ident, ident_bf):
                then(g_.affine_select(out=m[:], in_=m[:], compare_op=ALU.not_equal, fill=1.0, base=0,
                                      pattern=[[-1, P]], channel_multiplier=1))
            then(g_.affine_select(out=causal_bf[:], in_=causal_bf[:], compare_op=ALU.is_ge, fill=-BIG, base=0,
                                  pattern=[[-1, P]], channel_multiplier=1))
            then(g_.affine_select(out=before_bf[:], in_=ones_bf[:], compare_op=ALU.is_gt, fill=0.0, base=0,
                                  pattern=[[1, P]], channel_multiplier=-1))
            then(g_.iota(iota_row[:], [[1, P]], base=0, channel_multiplier=0, allow_small_or_imprecise_dtypes=True))
            then(g_.iota(iota_tiles[:], [[P, T]], base=0, channel_multiplier=0, allow_small_or_imprecise_dtypes=True))
            then(g_.iota(row_id[:], [[P, TOPK * T]], base=1, channel_multiplier=1, allow_small_or_imprecise_dtypes=True))
            for r in range(HR):
                ins = g_.memset(freq[:, r:r + 1], float(inv_freq[r]))
            then(ins)
            pool.sem_inc(consts, 1)

            pool.wait_ge(trig_done, 1)
            pool.wait_ge(z_out, T)
            x1, x2 = k_rope[:, :, 0:HR], k_rope[:, :, HR:ROPE]
            g_.tensor_tensor(rope_k[:, 0], x1, cos_t[:], ALU.mult)
            g_.tensor_tensor(rope_k[:, 1], x2, sin_t[:], ALU.mult)
            g_.tensor_tensor(rope_k[:, 2], x1, sin_t[:], ALU.mult)
            then(g_.tensor_tensor(rope_k[:, 3], x2, cos_t[:], ALU.mult))
            g_.tensor_tensor(k_rot[:, :, 0:HR], rope_k[:, 0], rope_k[:, 1], ALU.subtract)
            g_.tensor_tensor(k_rot[:, :, HR:ROPE], rope_k[:, 2], rope_k[:, 3], ALU.add).then_inc(krot_done, 1)

            def rotate(h):
                pool.wait_ge(proj_out, h * PROJ + 2)
                q1, q2 = q_h[:, :, NOPE:NOPE + HR], q_h[:, :, NOPE + HR:QH]
                g_.tensor_tensor(rope_tmp[:, 0], q1, cos_t[:], ALU.mult)
                g_.tensor_tensor(rope_tmp[:, 1], q2, sin_t[:], ALU.mult)
                g_.tensor_tensor(rope_tmp[:, 2], q1, sin_t[:], ALU.mult)
                g_.tensor_tensor(rope_tmp[:, 3], q2, cos_t[:], ALU.mult).then_inc(rot_half, 1)
                pool.wait_ge(rot_half, h + 1)
                g_.tensor_tensor(q1, rope_tmp[:, 0], rope_tmp[:, 1], ALU.subtract)
                g_.tensor_tensor(q2, rope_tmp[:, 2], rope_tmp[:, 3], ALU.add).then_inc(q_rot, 1)

            with pool.Fori(0, H) as h:
                rotate(h)

            for t in range(T):
                pool.wait_ge(h2_done, t + 1)
                pool.wait_ge(oT_done, 2 * t + 2)
                then(g_.tensor_tensor(xa[:, t, :], r_buf[t % 2], Ga, ALU.mult))
                g_.tensor_tensor(xa[:, t, :], xa[:, t, :], Ba, ALU.add).then_inc(xa_done, 1)

            pool.wait_ge(xa_done, T)
            pool.wait_ge(h2_stored[0], 16 * (T // 2))
            pool.wait_ge(h2_stored[1], 16 * (T // 2))
            pool.wait_ge(h2T_done, 2 * T)
            pool.wait_ge(table_done, 1)
            rounds = pool.value_load(rounds_i[0:1, 0:1], min_val=T - 1, max_val=TILES_MAX // 2 - 1)
            rows_all = pool.snap(rounds * 16 + 32)
            y_both = pool.snap(rounds * 16 + 16)

            def gather(b):
                g_.indirect_dma_start(xg[b], None, h2_rows, bass.IndirectOffsetOnAxis(idx_now[b][:, 0:1], 0),
                                      bounds_check=S - 1, oob_is_err=False).then_inc(gathered[b], 16)

            def scatter(i, c, ahead):
                n, b = i * 2 + c, c % 2
                if ahead:
                    pool.wait_ge(xgT_done, n + 2)
                    g_.tensor_copy(idx_now[1 - b][:], idx_u[:, bass.ds(n + 3, 1)])
                g_.tensor_copy(dst_now[b][:], dst_u[:, bass.ds(n, 1)]).then_inc(idx_set, 1)
                pool.wait_ge(idx_set, n + 2)
                if ahead:
                    pool.sem_inc(idx_seen, 1)
                    gather(1 - b)
                pool.wait_ge(ye_out, n + 2)
                pool.sem_inc(idx_seen, 1)
                g_.indirect_dma_start(y_rows, bass.IndirectOffsetOnAxis(dst_now[b][:, 0:1], 0), y_e[b], None,
                                      bounds_check=TOPK * S - 1, oob_is_err=False).then_inc(y_stored[b], 16)
                if c >= 1:
                    pool.wait_ge(y_stored[1 - b], i * 16 + 16)
                    pool.sem_inc(y_free, 1)

            pool.sem_inc(y_free, 2)
            g_.tensor_copy(idx_now[0][:], idx_u[:, 0:1])
            g_.tensor_copy(idx_now[1][:], idx_u[:, 1:2]).then_inc(idx_set, 1)
            pool.wait_ge(idx_set, 1)
            gather(0)
            gather(1)
            pool.wait_ge(xgT_done, 1)
            then(g_.tensor_copy(idx_now[0][:], idx_u[:, 2:3]))
            gather(0)
            scatter(0, 0, True)
            with pool.Fori(0, rounds) as i:
                for c in (1, 2):
                    scatter(i, c, True)
            scatter(rounds, 1, False)
            pool.wait_ge(y_stored[1], y_both)
            pool.wait_ge(gathered[0], rows_all)
            pool.wait_ge(gathered[1], rows_all)
            pool.sem_inc(y_all, 1)

            def add_bias(t):
                pool.wait_ge(scaled, t + 1)
                g_.tensor_tensor(yb[t], ya[t], lnb2, ALU.add).then_inc(out_done, 1)

            pool.wait_ge(ld_ln2, 32)
            for t in range(POOL_ADDS - 1, T, POOL_ADDS):
                pool.wait_ge(ld_y[t], 32)
                g_.tensor_tensor(ya[t], ya[t], yb[t], ALU.add).then_inc(added, 1)
                for u in range(max(0, t - 3), t - 1):
                    add_bias(u)
            for u in range(T - 2, T):
                add_bias(u)


def proj_bank(h, m):
    return (6, 7, 4, 5)[m % 4] if isinstance(h, int) and h == 0 else 6


def group_at(i):
    return sum(1 if j < 4 else 2 for j in range(i)) if i >= 0 else -sum(1 if j % T < 4 else 2 for j in range(i, 0))


_INS = ["x", "c", "positions", "w_mod", "b_mod", "ln_g", "ln_b", "w_in", "q_norm_g", "kv_norm_g", "w_uq", "w_ukv", "w_o",
        "w_group_router", "b_group_router", "w_expert_router", "b_expert_router", "w_gate", "w_up", "w_down"]


def kernel(**inputs):
    import concourse.bacc as _bacc
    from concourse.bass_utils import run_bass_kernel_spmd as _run

    nc = _bacc.Bacc("TRN2", target_bir_lowering=False, num_devices=1)
    arrays, args = {}, []
    for name in _INS:
        a = np.ascontiguousarray(inputs[name])
        arrays[f"in_{name}_dram"] = a
        args.append(nc.dram_tensor(f"in_{name}_dram", a.shape, mybir.dt.from_np(a.dtype), kind="ExternalInput").ap())
    args.append(nc.dram_tensor("out_dram", (1, S, D), F32, kind="ExternalOutput").ap())
    build_trunk(nc, *args)
    r = _run(nc, [arrays], core_ids=[0])
    return r.results[0]["out_dram"]
```

```python
from contextlib import ExitStack

import numpy as np
import concourse.bass as bass
from concourse import mybir

F32, F32R, BF16, I32, U32 = mybir.dt.float32, mybir.dt.float32r, mybir.dt.bfloat16, mybir.dt.int32, mybir.dt.uint32
ALU = mybir.AluOpType
ACT = mybir.ActivationFunctionType
AX = mybir.AxisListType

P = 128
D = 1024
S = 1024
T = S // P
KD = D // P
H = 16
QL, KVL, NOPE, ROPE, VH = 384, 256, 64, 32, 64
HR = ROPE // 2
ZW = QL + KVL + ROPE
QH = NOPE + ROPE
KVH = NOPE + VH
G, EPG = 4, 8
E = G * EPG
FF = 256
TOPK = 2
TILES_MAX = E + TOPK * S // P
LOOP_TABLE = TILES_MAX + 4
SCALE = float(QH) ** -0.5
ALPHA = float(2.0 ** 0.25)
LN_EPS, RMS_EPS = 1e-5, 1e-6
BIG = 3.0e38
TWO_PI = 2.0 * np.pi
TWO_PI_HI = 6.28125
TWO_PI_MID = float(np.float32(np.round((TWO_PI - TWO_PI_HI) * 2 ** 21) / 2 ** 21))
TWO_PI_LO = float(np.float32(TWO_PI - TWO_PI_HI - TWO_PI_MID))
ROUND = 1.5 * 2.0 ** 23
PI_F = 3.1415925


def build_trunk(nc, x, c, positions, w_mod, b_mod, ln_g, ln_b, w_in, q_norm_g, kv_norm_g, w_uq, w_ukv, w_o,
                w_gr, b_gr, w_er, b_er, w_gate, w_up, w_down, out):
    inv_freq = (1.0 / np.float32(10000.0) ** (np.arange(0, ROPE, 2, dtype=np.float32) / np.float32(ROPE))).astype(np.float32)
    h2_rows = nc.dram_tensor("h2_rows", [S, D], F32, kind="Internal").ap()
    y_rows = nc.dram_tensor("y_rows", [TOPK * S, D], F32, kind="Internal").ap()

    ctx = ExitStack()
    with ctx:
        def sb(name, shape, dt=F32):
            return ctx.enter_context(nc.sbuf_tensor(name, shape, dt))

        def sem(name):
            return ctx.enter_context(nc.semaphore(name))

        PS = ctx.enter_context(nc.psum_tensor("banks", [P, 8, 512], F32))

        start_of = {}

        def region(name, words):
            start_of[name] = (nc.sbuf_base + 31) // 32 * 32
            reg = sb(name, [P, words])
            assert nc.sbuf_base == start_of[name] + 4 * words
            return reg

        def parts_at(name, region_name, word, shape):
            return nc.alloc_sbuf_tensor_at(name, shape, F32R, offset=start_of[region_name] + 4 * word)

        reg_x = region("reg_x", T * D)
        reg_h = region("reg_h", T * D)
        reg_mod = region("reg_mod", 6 * D)
        reg_up = region("reg_up", 3 * H * QH + 2 * H * KVH)
        reg_lat = region("reg_lat", 5 * D)
        reg_work = region("reg_work", 11264)
        reg_klo = region("reg_klo", 2 * S)

        x_tok = reg_x[:].rearrange("p (t d) -> p t d", t=T)
        wo_sb = reg_x[:].rearrange("p (k d) -> p k d", k=KD)
        hT = reg_h[:].rearrange("p (k s) -> p k s", k=KD)
        o_tok = reg_h[:].rearrange("p (t d) -> p t d", t=T)
        xa = o_tok
        acc = reg_mod[:]
        qlat_lo = parts_at("qlat_lo", "reg_up", 0, [P, 3, S])
        wq_raw = reg_up[:, 3 * S:3 * S + 3 * P].rearrange("p (k n) -> p k n", k=3)
        wq_hi = parts_at("wq_hi", "reg_up", 3 * S + 3 * P, [P, 3, P])
        wq_lo = parts_at("wq_lo", "reg_up", 3 * S + 6 * P, [P, 3, P])
        assert 3 * S + 9 * P <= 3 * H * QH
        wukv_sb = reg_up[:, 3 * H * QH:].rearrange("p (k n) -> p k n", k=2)
        qlat_hi = parts_at("qlat_hi", "reg_lat", 0, [P, 3, S])
        kvlatT = reg_lat[:, 3 * D:5 * D].rearrange("p (k s) -> p k s", k=2)
        g1p, A2, B2, Ga, Ba = (reg_lat[:, i * D:(i + 1) * D] for i in range(5))

        at = [0]

        def work(n):
            at[0] += n
            assert at[0] <= 11264
            return reg_work[:, at[0] - n:at[0]]

        win_sb = work(KD * ZW).rearrange("p (k n) -> p k n", k=KD)
        MOD_BUFS = 4
        zs = [work(ZW) for _ in range(2)]
        sq_junk = work(QL)
        k_rope = work(T * ROPE).rearrange("p (t r) -> p t r", t=T)
        k_rot = work(T * 2 * ROPE).rearrange("p (t r) -> p t r", t=T)
        rope_k = work(4 * T * HR).rearrange("p (a t r) -> p a t r", a=4, t=T)
        late_buf = work(2 * D)
        turn_tab = work(T * 2 * ROPE).rearrange("p (t r) -> p t r", t=T)

        def mod_w(n):
            b = n % MOD_BUFS
            if n >= KD and b < 2:
                return reg_klo[:] if b == 0 else late_buf
            return reg_up[:, b * 2 * D:(b + 1) * 2 * D]

        at[0] = 0
        work(4 * S)
        kT_hi = [parts_at(f"kT_hi{i}", "reg_work", i * S, [P, S]) for i in range(2)]
        qT_hi = [parts_at(f"qT_hi{i}", "reg_work", (2 + i) * S, [P, S]) for i in range(2)]
        kT_lo = [parts_at(f"kT_lo{i}", "reg_klo", i * S, [P, S]) for i in range(2)]
        qT_lo = [parts_at(f"qT_lo{i}", "reg_mod", i * S, [P, S]) for i in range(2)]
        qT_full = [reg_mod[:, i * S:(i + 1) * S] for i in range(2)]
        v_h = [work(T * VH).rearrange("p (t d) -> p t d", t=T) for _ in range(2)]
        k_h = work(T * NOPE).rearrange("p (t d) -> p t d", t=T)
        q_turn = work(S)
        probs = [work(S) for _ in range(2)]
        pT = [work(S).rearrange("p (b q) -> p b q", b=T) for _ in range(2)]
        at[0] = 0
        work(2 * D)
        oT_hi = [parts_at(f"oT_hi{i}", "reg_work", i * D, [P, KD, P]) for i in range(2)]
        oT_lo = [parts_at(f"oT_lo{i}", "reg_mod", i * D, [P, KD, P]) for i in range(2)]
        wo_hi = parts_at("wo_hi", "reg_up", 0, [P, KD, D])
        wo_lo = parts_at("wo_lo", "reg_x", 0, [P, KD, D])
        h2T = work(D).rearrange("p (k q) -> p k q", k=KD)
        xs = [work(D) for _ in range(2)]
        g2p = work(D)
        r_buf = [work(D) for _ in range(2)]
        h2 = [work(D) for _ in range(2)]
        at[0] = 0
        xg = [work(D) for _ in range(2)]
        xgT = [work(D).rearrange("p (k q) -> p k q", k=KD) for _ in range(2)]
        he = [work(FF) for _ in range(2)]
        heT = [work(FF).rearrange("p (k q) -> p k q", k=2) for _ in range(2)]
        assert at[0] == 5 * D
        work(D)
        sil = [work(FF) for _ in range(2)]
        y_e = [work(D) for _ in range(2)]
        assert at[0] <= 9 * D
        lng2, lnb2 = reg_lat[:, 0:D], reg_lat[:, D:2 * D]
        te_cmp = reg_lat[:, 2 * D:2 * D + E]
        place = reg_lat[:, 4 * D:4 * D + T * E].rearrange("p (t e) -> p t e", e=E)
        picked = reg_lat[:, 4 * D + T * E:4 * D + 3 * T * E].rearrange("p (a t e) -> p a t e", a=TOPK, e=E)
        hot = reg_x[:, 7 * D:7 * D + TOPK * T * E].rearrange("p (a t e) -> p a t e", a=TOPK, t=T)
        hot_in = reg_x[:, 0:TOPK * T * P].rearrange("p (a t j) -> p a t j", a=TOPK, t=T)
        hot_dv = reg_x[:, 2 * D:2 * D + TOPK * T * 2 * TILES_MAX].rearrange("p (a n j) -> p a n j", n=TOPK * T, a=2)
        over = reg_x[:, 7 * D + TOPK * T * E:7 * D + 3 * T * E].rearrange("p (e t) -> p e t", t=T)
        wgu = [reg_mod[:, 0:KD * 2 * FF].rearrange("p (k n) -> p k n", k=KD),
               reg_up[:, 0:KD * 2 * FF].rearrange("p (k n) -> p k n", k=KD)]
        wdn = [reg_mod[:, KD * 2 * FF:KD * 2 * FF + 2 * D].rearrange("p (k n) -> p k n", k=2),
               reg_up[:, KD * 2 * FF:KD * 2 * FF + 2 * D].rearrange("p (k n) -> p k n", k=2)]
        y_at = [reg_x[:, i * D:(i + 1) * D] for i in range(8)] + [reg_up[:, i * D:(i + 1) * D] for i in range(8)]
        ya, yb = y_at[0::2], y_at[1::2]

        ident = sb("ident", [P, P])
        ones = sb("ones", [P, P])
        ident_bf = sb("ident_bf", [P, P], BF16)
        causal_bf = sb("causal_bf", [P, P], BF16)
        before_bf = sb("before_bf", [P, P], BF16)
        ones_bf = sb("ones_bf", [P, P], BF16)
        iota_row = sb("iota_row", [P, P])
        iota_tiles = sb("iota_tiles", [P, T])
        row_id = sb("row_id", [P, TOPK * T])
        freq = sb("freq", [P, HR])
        c_col = sb("c_col", [P, KD])
        c_act = sb("c_act", [P, KD])
        mod_cols = sb("mod_cols", [P, 2 * KD])
        qg_col = sb("qg_col", [P, 3])
        kvg_col = sb("kvg_col", [P, 2])
        pos_i = sb("pos_i", [P, T], I32)
        pos_f = sb("pos_f", [P, T])
        ang = sb("ang", [P, T, HR])
        turns = sb("turns", [P, T, HR])
        cos_t = sb("cos_t", [P, T, HR])
        sin_t = sb("sin_t", [P, T, HR])
        ms = sb("ms", [P, T, 2])
        rms = sb("rms", [P, T, 2])
        rrms = sb("rrms", [P, T, 2])
        eps_rms = sb("eps_rms", [P, 1])
        eps_ln = sb("eps_ln", [P, 1])
        neg_max = sb("neg_max", [P, T])
        row_sum = sb("row_sum", [P, 2 * T])
        inv_sum = sb("inv_sum", [P, T])
        bn = sb("bn", [P, 2, 6])
        mv = sb("mv", [P, 2 * T, 2])
        std = sb("std", [P, 2 * T])
        rstd = sb("rstd", [P, 2 * T])
        w_rt = sb("w_rt", [P, KD, G + E])
        b_rt = sb("b_rt", [P, G + E])
        logits = sb("logits", [P, T, G + E])
        gl = sb("gl", [P, T, 8])
        g_top = sb("g_top", [P, T, 8])
        g_idx = sb("g_idx", [P, T, 8], U32)
        g_idf = sb("g_idf", [P, T])
        g_exp = sb("g_exp", [P, T, G])
        g_den = sb("g_den", [P, T])
        g_p = sb("g_p", [P, T])
        g_hot = sb("g_hot", [P, T, G])
        e_sel = sb("e_sel", [P, G, EPG])[:]
        e_in = sb("e_in", [P, T, EPG])
        e_top = sb("e_top", [P, T, 8])
        e_idx = sb("e_idx", [P, T, 8], U32)
        e_idf = sb("e_idf", [P, TOPK, T])
        e_dif = sb("e_dif", [P, T])
        e_exp = sb("e_exp", [P, T])
        e_den = sb("e_den", [P, T])
        wts = sb("wts", [P, TOPK, T])
        member = sb("member", [P, T, E], BF16)
        count = sb("count", [P, E])
        n_tiles = sb("n_tiles", [P, E])
        tile_end = sb("tile_end", [P, E])
        base = sb("base", [P, E])
        slot = sb("slot", [P, TOPK, T])
        row_f = sb("row_f", [P, LOOP_TABLE])
        pad = sb("pad", [P, LOOP_TABLE])
        slot_w = sb("slot_w", [P, LOOP_TABLE])
        past = sb("past", [P, LOOP_TABLE])
        slot_in = sb("slot_in", [P, TOPK, T])
        slot_dv = sb("slot_dv", [P, TOPK, T])
        idx_f = sb("idx_f", [P, LOOP_TABLE])
        idx_u = sb("idx_u", [P, LOOP_TABLE], U32)
        dst_u = sb("dst_u", [P, LOOP_TABLE], U32)
        idx_now = [sb(f"idx_now{i}", [P, 1], U32) for i in range(2)]
        dst_now = [sb(f"dst_now{i}", [P, 1], U32) for i in range(2)]
        te_col = sb("te_col", [P, 1])
        te_i = sb("te_i", [1, LOOP_TABLE], I32)
        rounds_f = sb("rounds_f", [1, 2])
        rounds_i = sb("rounds_i", [1, 2], I32)

        consts = sem("consts")
        ld_x = [sem(f"ld_x{i}") for i in range(2)]
        ld_small = sem("ld_small")
        ld_c = sem("ld_c")
        ld_pos = sem("ld_pos")
        ld_bmod = [sem(f"ld_bmod{i}") for i in range(2)]
        acc_zero = sem("acc_zero")
        ld_mod = [sem(f"ld_mod{i}") for i in range(MOD_BUFS)]
        mod_done = sem("mod_done")
        c_ready = sem("c_ready")
        ld_win = sem("ld_win")
        ld_up = sem("ld_up")
        ld_wo = sem("ld_wo")
        xT_done = sem("xT_done")
        xT_out = sem("xT_out")
        cols_done = sem("cols_done")
        cols_out = sem("cols_out")
        z_done = sem("z_done")
        z_out = sem("z_out")
        ms_done = sem("ms_done")
        rms_done = sem("rms_done")
        zn_done = sem("zn_done")
        znT_done = sem("znT_done")
        znT_out = sem("znT_out")
        ang_done = sem("ang_done")
        trig_done = sem("trig_done")
        krot_done = sem("krot_done")
        krT_done = sem("krT_done")
        krT_out = sem("krT_out")
        krT_lo = sem("krT_lo")
        lo_out = sem("lo_out")
        wo_split = sem("wo_split")
        wo_rest = sem("wo_rest")
        oT_rest = sem("oT_rest")
        proj_done = sem("proj_done")
        proj_out = sem("proj_out")
        ld_wq = sem("ld_wq")
        wq_split = sem("wq_split")
        wq_rest = sem("wq_rest")
        zlo_out = sem("zlo_out")
        tab_turned = sem("tab_turned")
        tab_out = sem("tab_out")
        q_turned = sem("q_turned")
        q_split = sem("q_split")
        q_rest = sem("q_rest")
        s_done = sem("s_done")
        max_done = sem("max_done")
        exp_done = sem("exp_done")
        inv_done = sem("inv_done")
        pT_done = sem("pT_done")
        pT_out = sem("pT_out")
        o_done = sem("o_done")
        o_out = sem("o_out")
        bc_done = sem("bc_done")
        bc_out = sem("bc_out")
        ld_ln = sem("ld_ln")
        ld_ln2 = sem("ld_ln2")
        ld_xs = [sem(f"ld_xs{i}") for i in range(2)]
        oT_done = sem("oT_done")
        oT_out = sem("oT_out")
        yo_done = sem("yo_done")
        yo_used = sem("yo_used")
        std_in = sem("std_in")
        std_done = sem("std_done")
        xa_done = sem("xa_done")
        h2_done = sem("h2_done")
        h2_stored = [sem(f"h2_stored{i}") for i in range(2)]
        h2T_done = sem("h2T_done")
        h2T_out = sem("h2T_out")
        lg_done = sem("lg_done")
        lg_out = sem("lg_out")
        rt_exp_in = sem("rt_exp_in")
        rt_exp = sem("rt_exp")
        member_done = sem("member_done")
        rank_done = sem("rank_done")
        place_known = sem("place_known")
        te_in = sem("te_in")
        te_turned = sem("te_turned")
        hot_done = sem("hot_done")
        hot_weighed = sem("hot_weighed")
        w_acc = sem("w_acc")
        idx_acc = sem("idx_acc")
        tiles_known = sem("tiles_known")
        table_done = sem("table_done")
        ld_gu = [sem(f"ld_gu{i}") for i in range(2)]
        ld_dn = [sem(f"ld_dn{i}") for i in range(2)]
        idx_set = sem("idx_set")
        gathered = [sem(f"gathered{i}") for i in range(2)]
        xgT_done = sem("xgT_done")
        xgT_outA = sem("xgT_outA")
        xgT_outV = sem("xgT_outV")
        hid_done = sem("hid_done")
        silu_done = sem("silu_done")
        he_done = sem("he_done")
        heT_done = sem("heT_done")
        heT_out = sem("heT_out")
        ye_done = sem("ye_done")
        ye_out = sem("ye_out")
        y_stored = [sem(f"y_stored{i}") for i in range(2)]
        y_all = sem("y_all")
        ld_y = [sem(f"ld_y{i}") for i in range(T)]
        added = sem("added")
        summed = sem("summed")
        out_done = sem("out_done")
        last_out = sem("last_out")
        stored = sem("stored")
        k_turn = sem("k_turn")
        idx_seen = sem("idx_seen")
        y_free = sem("y_free")
        rstd_done = sem("rstd_done")
        weighed = sem("weighed")
        scaled = sem("scaled")
        vec = sem("vec")
        pol = sem("pol")

        block = ctx.enter_context(nc.Block())
        MOD_STEPS = 3 * KD
        PROJ = 6

        @block.sync
        def _(sp):
            with nc.allow_non_contiguous_dma(reason="a vector of 1024 elements"):
                sp.dma_start(c_col[:], c.rearrange("o (k p) -> p (o k)", p=P)).then_inc(ld_c, 16)
            x_t = x[0].rearrange("(t p) d -> p t d", p=P)
            wm = w_mod[0].rearrange("(k p) n -> p k n", p=P)

            def load_mod(n):
                if n >= MOD_BUFS:
                    sp.wait_ge(mod_done, n - MOD_BUFS + 1)
                sec, k = n // KD, n % KD
                sp.dma_start(mod_w(n), wm[:, k, sec * 2 * D:(sec + 1) * 2 * D]).then_inc(ld_mod[n % MOD_BUFS], 16)

            for n in range(2):
                load_mod(n)
            sp.wait_ge(acc_zero, 1)
            sp.dma_start(acc[0:1, 0:2 * D], b_mod[:, 0:2 * D]).then_inc(ld_bmod[0], 16)
            for n in range(2, KD):
                load_mod(n)
            sp.dma_start(x_tok[:, 0:4, :], x_t[:, 0:4, :]).then_inc(ld_x[0], 16)
            with nc.allow_non_contiguous_dma(reason="1024 positions"):
                sp.dma_start(pos_i[:], positions.rearrange("o (t p) -> p (o t)", p=P)).then_inc(ld_pos, 16)
            sp.dma_start(win_sb, w_in[0].rearrange("(k p) n -> p k n", p=P)).then_inc(ld_win, 16)
            sp.dma_start(x_tok[:, 4:8, :], x_t[:, 4:8, :]).then_inc(ld_x[1], 16)
            sp.wait_ge(acc_zero, 2)
            sp.dma_start(acc[0:1, 2 * D:], b_mod[:, 2 * D:]).then_inc(ld_bmod[1], 16)
            with nc.allow_non_contiguous_dma(reason="two vectors of at most 1024 elements"):
                sp.dma_start(qg_col[:], q_norm_g.rearrange("o (k p) -> p (o k)", p=P)).then_inc(ld_small, 16)
                sp.dma_start(kvg_col[:], kv_norm_g.rearrange("o (k p) -> p (o k)", p=P)).then_inc(ld_small, 16)
            sp.dma_start(w_rt[:, :, 0:G], w_gr[0].rearrange("(k p) n -> p k n", p=P)).then_inc(ld_small, 16)
            sp.dma_start(w_rt[:, :, G:], w_er[0].rearrange("(k p) n -> p k n", p=P)).then_inc(ld_small, 16)
            sp.dma_start(b_rt[:, 0:G], b_gr.broadcast_to([P, G])).then_inc(ld_small, 16)
            sp.dma_start(b_rt[:, G:], b_er.broadcast_to([P, E])).then_inc(ld_small, 16)
            for n in range(KD, MOD_STEPS):
                load_mod(n)
            uq = w_uq[0].rearrange("(k p) n -> p k n", p=P)

            def load_wq(at0):
                sp.dma_start(wq_raw[:, :, 0:QH], uq[:, :, bass.ds(at0, QH)]).then_inc(ld_wq, 16)
                sp.dma_start(wq_raw[:, :, QH:QH + HR], uq[:, :, bass.ds(at0 + (NOPE + HR), HR)]).then_inc(ld_wq, 16)
                sp.dma_start(wq_raw[:, :, QH + HR:P], uq[:, :, bass.ds(at0 + NOPE, HR)]).then_inc(ld_wq, 16)

            load_wq(0)
            sp.wait_ge(mod_done, MOD_STEPS)
            sp.dma_start(wukv_sb, w_ukv[0].rearrange("(k p) n -> p k n", p=P)).then_inc(ld_up, 16)
            sp.wait_ge(xT_done, 16)
            sp.dma_start(wo_sb, w_o[0].rearrange("(k p) n -> p k n", p=P)).then_inc(ld_wo, 16)

            with sp.Fori(0, H - 1) as i:
                sp.wait_ge(wq_rest, i + 1)
                load_wq(i * QH + QH)

            sp.wait_ge(proj_done, H * PROJ)
            sp.dma_start(Ga, ln_g[0, 0:1, :].broadcast_to([P, D])).then_inc(ld_ln, 16)
            sp.dma_start(Ba, ln_b[0, 0:1, :].broadcast_to([P, D])).then_inc(ld_ln, 16)
            for t in range(T):
                if t == 0:
                    sp.wait_ge(o_done, H * T)
                if t >= 2:
                    sp.wait_ge(std_in, t - 1)
                sp.dma_start(xs[t % 2], x_t[:, t, :]).then_inc(ld_xs[t % 2], 16)
                if t >= 1:
                    sp.wait_ge(h2_done, t)
                    sp.dma_start(h2_rows[(t - 1) * P:t * P, :], h2[(t - 1) % 2]).then_inc(h2_stored[(t - 1) % 2], 16)
            sp.wait_ge(h2_done, T)
            sp.dma_start(h2_rows[(T - 1) * P:, :], h2[(T - 1) % 2]).then_inc(h2_stored[(T - 1) % 2], 16)

            sp.wait_ge(tiles_known, 1)

            def expert(j):
                return sp.value_load(te_i[0:1, bass.ds(j, 1)], min_val=0, max_val=E - 1)

            def load_gate_up(e, b):
                for w, at0 in ((w_gate, 0), (w_up, FF)):
                    sp.dma_start(wgu[b][:, :, at0:at0 + FF],
                                 w[0, bass.ds(e, 1)].rearrange("o (p k) n -> p (o k) n", p=P)).then_inc(ld_gu[b], 16)

            def load_down(e, b):
                sp.dma_start(wdn[b], w_down[0, bass.ds(e, 1)].rearrange("o (p k) n -> p (o k) n", p=P)).then_inc(ld_dn[b], 16)

            def refill(i, b, both):
                e_down = expert(i * 2 + (b + 2))
                if both:
                    e_gu = expert(i * 2 + (b + 3))
                    sp.wait_ge(hid_done, i * 2 + (b + 2))
                    load_gate_up(e_gu, 1 - b)
                sp.wait_ge(ye_done, i * 2 + (b + 1))
                load_down(e_down, b)

            for b in range(2):
                e_b = expert(b)
                load_gate_up(e_b, b)
                if b == 1:
                    sp.wait_ge(gathered[0], 16)
                load_down(e_b, b)
            e_2 = expert(2)
            rounds_less = sp.value_load(rounds_i[0:1, 1:2], min_val=T - 2, max_val=TILES_MAX // 2 - 2)
            sp.wait_ge(hid_done, 1)
            load_gate_up(e_2, 0)
            with sp.Fori(0, rounds_less) as i:
                for b in range(2):
                    refill(i, b, True)
            refill(rounds_less, 0, True)
            refill(rounds_less, 1, False)
            sp.dma_start(lng2, ln_g[0, 1:2, :].broadcast_to([P, D])).then_inc(ld_ln2, 16)
            sp.dma_start(lnb2, ln_b[0, 1:2, :].broadcast_to([P, D])).then_inc(ld_ln2, 16)

            sp.wait_ge(y_all, 1)

            for t in range(T):
                for a, dst in ((0, ya), (1, yb)):
                    sp.dma_start(dst[t], y_rows[a * S + t * P:a * S + (t + 1) * P, :]).then_inc(ld_y[t], 16)
            for t in range(T):
                if t < T - 2:
                    sp.wait_ge(out_done, t + 1)
                else:
                    sp.wait_ge(last_out, t - T + 3)
                sp.dma_start(out[0, t * P:(t + 1) * P, :], yb[t]).then_inc(stored, 16)
            sp.wait_ge(stored, 16 * T)

        @block.tensor
        def _(pe):
            def mm(o, a, b, start, stop):
                return nc.tensor.matmul(o, a, b, start=start, stop=stop, skip_group_check=True)

            pe.wait_ge(consts, 1)
            def xT_group(g):
                half, k = g // KD, g % KD
                pe.wait_ge(ld_x[half], 16)
                if g >= 4:
                    pe.wait_ge(xT_out, g - 3)
                for t in range(4):
                    ins = nc.tensor.transpose(PS[:, 4 + g % 4, t * P:(t + 1) * P],
                                              x_tok[:, half * 4 + t, k * P:(k + 1) * P], ident[:])
                ins.then_inc(xT_done, 1)

            pe.wait_ge(mod_done, KD)
            for j in range(2 * KD):
                ins = mm(PS[:, 0, j:j + 1], acc[:, j * P:(j + 1) * P], ones[:, 0:1], True, True)
            ins.then_inc(cols_done, 1)
            for g in range(KD):
                xT_group(g)

            pe.wait_ge(ld_win, 16)
            pe.wait_ge(xT_out, KD)

            def z_tile(t):
                b = 2 * (t % 2)
                if t >= 2:
                    pe.wait_ge(z_out, t - 1)
                for lo, hi in ((0, 512), (512, ZW)):
                    for k in range(KD):
                        ins = mm(PS[:, b + lo // 512, 0:hi - lo], hT[:, k, t * P:(t + 1) * P],
                                 win_sb[:, k, lo:hi], k == 0, k == KD - 1)
                ins.then_inc(z_done, 1)

            def zn_tile(t):
                pe.wait_ge(zn_done, t + 1)
                if t >= 1:
                    pe.wait_ge(znT_out, t)
                    pe.wait_ge(zlo_out, t)
                for j in range(5):
                    bank, off = (4, j) if j < 3 else (5, j - 3)
                    ins = nc.tensor.transpose(PS[:, bank, off * P:(off + 1) * P], zs[t % 2][:, j * P:(j + 1) * P], ident[:])
                ins.then_inc(znT_done, 1)

            z_tile(0)
            for g in range(KD, 2 * KD):
                xT_group(g)
            for t in range(T - 1):
                z_tile(t + 1)
                if t == 0:
                    pe.wait_ge(xT_out, 2 * KD)
                zn_tile(t)
            def mm_parts(o, a_hi, a_lo, b_hi, b_lo, start, stop):
                mm(o, a_hi, b_hi, start, False)
                mm(o, a_hi, b_lo, False, False)
                return mm(o, a_lo, b_hi, False, stop)

            def project(m, hn, hp):
                bank = proj_bank(hn, m)
                if isinstance(hn, int) and hn == 0:
                    if m < 2:
                        pe.wait_ge(znT_out, 4 + 4 * m)
                    if m == 2:
                        pe.wait_ge(wq_rest, 1)
                        pe.wait_ge(zlo_out, T)
                    if m >= 4:
                        pe.wait_ge(proj_out, m - 3)
                elif m == 0:
                    pe.wait_ge(proj_out, hn * 4)
                    pe.wait_ge(lo_out, hn * 2)
                elif m < 3:
                    pe.wait_ge(proj_out, hn * 4 + m)
                    if m == 2:
                        pe.wait_ge(wq_rest, hn + 1)
                elif m < 5:
                    pe.wait_ge(q_turned, hn * 2 + (m - 2))
                else:
                    pe.wait_ge(proj_out, hn * 4 + 3)
                    pe.wait_ge(lo_out, hn * 2 + 1)
                half = m % 2
                cols = slice(half * 512, (half + 1) * 512)
                if m < 2:
                    for t in range(4):
                        for k in range(2):
                            ins = mm(PS[:, bank, t * KVH:(t + 1) * KVH], kvlatT[:, k, (half * 4 + t) * P:(half * 4 + t + 1) * P],
                                     wukv_sb[:, k, bass.ds(hn * KVH, KVH)], k == 0, k == 1)
                elif m < 4:
                    for k in range(3):
                        ins = mm_parts(PS[:, bank, :], wq_hi[:, k, :], wq_lo[:, k, :], qlat_hi[:, k, cols], qlat_lo[:, k, cols],
                                       k == 0, k == 2)
                else:
                    pe.sem_inc(k_turn, 1)
                    for t in range(4):
                        ins = nc.tensor.transpose(PS[0:NOPE, bank, t * P:(t + 1) * P], k_h[:, half * 4 + t, :], ident[:])
                ins.then_inc(proj_done, 1)

            def scores(h, hp, i):
                b, w = 2 * (i % 2), (i + 1) * P
                if not (isinstance(h, int) and h == 0 and i < 2):
                    pe.wait_ge(exp_done, h * T + (i - 1))
                if i == 0:
                    pe.wait_ge(lo_out, h * 2 + 2)
                    pe.wait_ge(q_rest, h * 2 + 2)
                qs = slice(i * P, (i + 1) * P)
                at0, lo = score_start(i), 0
                while lo < w:
                    bank, off = b + (at0 + lo) // 512, (at0 + lo) % 512
                    hi = min(w, lo + 512 - off)
                    mm_parts(PS[:, bank, off:off + hi - lo], qT_hi[hp][:, qs], qT_lo[hp][:, qs],
                             kT_hi[hp][:, lo:hi], kT_lo[hp][:, lo:hi], True, hi < w)
                    if hi == w:
                        ins = mm(PS[:, bank, off + hi - lo - P:off + hi - lo], ident_bf[:], causal_bf[:], False, True)
                    lo = hi
                ins.then_inc(s_done, 1)

            def turn(h, i):
                pe.wait_ge(exp_done, h * T + (i + 1))
                for g in range(1 if i < 4 else 2):
                    n = group_at(i) + g
                    if not (isinstance(h, int) and h == 0 and n < 2):
                        pe.wait_ge(pT_out, h * 12 + (n - 1))
                    for k in range(4 * g, min(4 * g + 4, i + 1)):
                        ins = nc.tensor.transpose(PS[:, 4 + n % 2, (k % 4) * P:(k % 4 + 1) * P],
                                                  probs[i % 2][:, k * P:(k + 1) * P], ident[:])
                    ins.then_inc(pT_done, 1)

            def values(h, hp, i):
                pe.wait_ge(pT_out, h * 12 + (group_at(i) + (1 if i < 4 else 2)))
                if not (isinstance(h, int) and h == 0 and i == 0):
                    pe.wait_ge(o_out, h * T + i)
                for k in range(i + 1):
                    ins = mm(PS[:, 7, 0:VH], pT[i % 2][:, k, :], v_h[hp][:, k, :], k == 0, k == i)
                ins.then_inc(o_done, 1)

            def mod_row(m):
                sec, half = (2, 4, 3, 5)[m // 2], m % 2
                if m == 0:
                    pe.wait_ge(mod_done, MOD_STEPS)
                else:
                    pe.wait_ge(bc_out, m)
                mm(PS[:, 6, :], ones[:], acc[:, sec * D + half * 512:sec * D + half * 512 + 512], True, True).then_inc(bc_done, 1)

            def turn_o(t):
                pe.wait_ge(o_out, (H - 1) * T + t + 1)
                for half in range(2):
                    if t >= 1:
                        pe.wait_ge(oT_rest, 2 * t - 1 + half)
                    for k in range(4):
                        ins = nc.tensor.transpose(PS[:, half, k * P:(k + 1) * P],
                                                  o_tok[:, t, (half * 4 + k) * P:(half * 4 + k + 1) * P], ident[:])
                    ins.then_inc(oT_done, 1)

            def head(h, hp, first, nxt):
                for i in range(T):
                    scores(h, hp, i)
                    if nxt and i >= 2:
                        project(i - 2, h + 1, 1 - hp)
                    if not nxt:
                        mod_row(i)
                    if i >= 1:
                        turn(h, i - 1)
                    elif not first:
                        turn(h - 1, T - 1)
                    if i >= 2:
                        values(h, hp, i - 2)
                    elif not first:
                        values(h - 1, 1 - hp, T - 2 + i)

            pe.wait_ge(ld_up, 16)
            project(0, 0, 0)
            zn_tile(T - 1)
            pe.wait_ge(trig_done, 1)
            pe.wait_ge(z_out, T)
            for half in range(2):
                for t in range(4):
                    ins = nc.tensor.transpose(PS[0:2 * ROPE, 2 + half, t * P:(t + 1) * P], turn_tab[:, half * 4 + t, :], ident[:])
            ins.then_inc(tab_turned, 1)
            pe.wait_ge(krot_done, 1)
            for half in range(2):
                for t in range(4):
                    ins = nc.tensor.transpose(PS[0:2 * ROPE, half, t * P:(t + 1) * P], k_rot[:, half * 4 + t, :], ident[:])
            ins.then_inc(krT_done, 1)
            for m in range(1, PROJ):
                project(m, 0, 0)
            head(0, 0, True, True)
            with pe.Fori(0, (H - 2) // 2) as hh:
                for q in range(2):
                    head(hh * 2 + (1 + q), 1 - q, False, True)
            head(H - 1, 1, False, False)
            pe.wait_ge(exp_done, (H - 1) * T + T - 1)
            turn_o(0)
            turn(H - 1, T - 1)
            values(H - 1, 1, T - 2)
            values(H - 1, 1, T - 1)

            pe.wait_ge(wo_rest, KD)

            def out_proj(t, half):
                if half == 0:
                    pe.wait_ge(oT_rest, 2 * t + 2)
                    if t >= 2:
                        pe.wait_ge(yo_used, t - 1)
                cols = slice(half * 512, (half + 1) * 512)
                for k in range(KD):
                    ins = mm_parts(PS[:, 2 + 2 * (t % 2) + half, :], oT_hi[t % 2][:, k, :], oT_lo[t % 2][:, k, :],
                                   wo_hi[:, k, cols], wo_lo[:, k, cols], k == 0, k == KD - 1)
                if half == 1:
                    ins.then_inc(yo_done, 1)

            def turn_h2(t):
                pe.wait_ge(h2_done, t + 1)
                for half in range(2):
                    if t == 0 and half == 0:
                        pe.wait_ge(bc_out, 8)
                    elif t >= 1:
                        pe.wait_ge(lg_out if half == 0 else h2T_out, t if half == 0 else 2 * t)
                    for k in range(4):
                        ins = nc.tensor.transpose(PS[:, 6 + half, k * P:(k + 1) * P],
                                                  h2[t % 2][:, (half * 4 + k) * P:(half * 4 + k + 1) * P], ident[:])
                    ins.then_inc(h2T_done, 1)

            def route(t):
                pe.wait_ge(h2T_out, 2 * t + 2)
                for k in range(KD):
                    ins = mm(PS[:, 6, 0:G + E], h2T[:, k, :], w_rt[:, k, :], k == 0, k == KD - 1)
                ins.then_inc(lg_done, 1)

            for t in range(T):
                if t + 1 < T:
                    turn_o(t + 1)
                out_proj(t, 0)
                if t >= 2:
                    route(t - 2)
                out_proj(t, 1)
                if t >= 1:
                    turn_h2(t - 1)
            route(T - 2)
            turn_h2(T - 1)
            route(T - 1)

            pe.wait_ge(member_done, 1)
            for t in range(T):
                for u in range(t + 1):
                    mm(PS[:, 0, t * E:(t + 1) * E], before_bf[:] if u == t else ones_bf[:], member[:, u, :], u == 0, u == t)
            for u in range(T):
                ins = mm(PS[:, 1, 0:E], ones_bf[:], member[:, u, :], u == 0, u == T - 1)
            ins.then_inc(rank_done, 1)
            pe.wait_ge(te_in, 1)
            mm(PS[0:1, 5, 0:P], te_col[:], ident[:], True, True).then_inc(te_turned, 1)
            for n in range(TOPK * T):
                if n % 4 == 0:
                    pe.wait_ge(hot_done, n // 4 + 1)
                ins = mm(PS[:, 2, 0:TILES_MAX], hot_in[:, n // T, n % T, :], hot_dv[:, 0, n, :], n == 0, n == TOPK * T - 1)
            ins.then_inc(idx_acc, 1)
            pe.wait_ge(hot_weighed, 1)
            for n in range(TOPK * T):
                ins = mm(PS[:, 3, 0:TILES_MAX], hot_in[:, n // T, n % T, :], hot_dv[:, 1, n, :], n == 0, n == TOPK * T - 1)
            ins.then_inc(w_acc, 1)

            pe.wait_ge(table_done, 1)
            rounds = pe.value_load(rounds_i[0:1, 0:1], min_val=T - 1, max_val=TILES_MAX // 2 - 1)

            def turn_rows(i, b):
                pe.wait_ge(gathered[b], i * 16 + 16)
                if not (isinstance(i, int) and i == 0 and b == 0):
                    pe.wait_ge(xgT_outA, i * 2 + b)
                    pe.wait_ge(xgT_outV, i * 2 + b)
                rows = xg[b].rearrange("p (q k) -> p k q", k=KD)
                for half in range(2):
                    for k in range(4):
                        ins = nc.tensor.transpose(PS[:, half, k * P:(k + 1) * P], rows[:, half * 4 + k, :], ident[:])
                ins.then_inc(xgT_done, 1)

            def hidden(i, b):
                pe.wait_ge(ld_gu[b], i * 32 + 32)
                pe.wait_ge(xgT_outA, i * 2 + (b + 1))
                pe.wait_ge(xgT_outV, i * 2 + (b + 1))
                for k in range(KD):
                    ins = mm(PS[:, 2 + b, :], xgT[b][:, k, :], wgu[b][:, k, :], k == 0, k == KD - 1)
                ins.then_inc(hid_done, 1)

            def turn_hidden(i, b):
                pe.wait_ge(he_done, i * 2 + (b + 1))
                for k in range(2):
                    ins = nc.tensor.transpose(PS[:, 4, k * P:(k + 1) * P], he[b].rearrange("p (q k) -> p k q", k=2)[:, k, :], ident[:])
                ins.then_inc(heT_done, 1)

            def down(i, b):
                pe.wait_ge(heT_out, i * 2 + (b + 1))
                pe.wait_ge(ld_dn[b], i * 16 + 16)
                pe.wait_ge(ye_out, i * 2 + (b + 1))
                for half in range(2):
                    for k in range(2):
                        ins = mm(PS[:, 6 + half, :], heT[b][:, k, :], wdn[b][:, k, half * 512:(half + 1) * 512], k == 0, k == 1)
                ins.then_inc(ye_done, 1)

            turn_rows(0, 0)
            hidden(0, 0)
            turn_rows(0, 1)
            with pe.Fori(0, rounds) as i:
                for b in range(2):
                    turn_hidden(i, b)
                    hidden(i + b, 1 - b)
                    turn_rows(i + 1, b)
                    down(i, b)
            turn_hidden(rounds, 0)
            hidden(rounds, 1)
            down(rounds, 0)
            turn_hidden(rounds, 1)
            down(rounds, 1)

            pe.wait_ge(xa_done, T)
            pe.wait_ge(y_all, 1)
            for t in range(0, T, 2):
                for n, term in enumerate((xa[:, t, :], ya[t], yb[t])):
                    if n == 1:
                        pe.wait_ge(ld_y[t], 32)
                    for half in range(2):
                        ins = mm(PS[:, t + half, :], ident[:], term[:, half * 512:(half + 1) * 512], n == 0, n == 2)
                ins.then_inc(summed, 1)

        @block.scalar
        def _(act):
            act.wait_ge(ld_c, 16)
            nc.scalar.activation(c_act[:], c_col[:], ACT.Silu).then_inc(c_ready, 1)
            act.wait_ge(cols_out, 1)
            for g in range(16):
                half, k = g // KD, g % KD
                act.wait_ge(xT_done, g + 1)
                nc.scalar.activation(hT[:, k, half * 512:(half + 1) * 512], PS[:, 4 + g % 4, :], ACT.Identity,
                                     bias=mod_cols[:, k:k + 1], scale=mod_cols[:, KD + k:KD + k + 1]).then_inc(xT_out, 1)
            act.wait_ge(ang_done, 1)
            nc.scalar.activation(sin_t[:], ang[:], ACT.Sin)
            nc.scalar.activation(cos_t[:], turns[:], ACT.Sin)
            for at0, angle, sign in ((0, turns, 1.0), (HR, turns, 1.0), (2 * HR, ang, -1.0), (3 * HR, ang, 1.0)):
                ins = nc.scalar.activation(turn_tab[:, :, at0:at0 + HR], angle[:], ACT.Sin, scale=sign)
            ins.then_inc(trig_done, 1)
            act.wait_ge(ld_small, 16 * 6)
            for t in range(T):
                act.wait_ge(z_out, t + 1)
                nc.scalar.activation(sq_junk, zs[t % 2][:, 0:QL], ACT.Square, scale=QL ** -0.5, accum_out=ms[:, t, 0:1]).then_inc(ms_done, 1)
                act.wait_ge(ms_done, 2 * t + 1)
                nc.scalar.activation(sq_junk[:, 0:KVL], zs[t % 2][:, QL:QL + KVL], ACT.Square, scale=KVL ** -0.5,
                                     accum_out=ms[:, t, 1:2]).then_inc(ms_done, 1)
                act.wait_ge(ms_done, 2 * t + 2)
                nc.scalar.activation(rms[:, t, :], ms[:, t, :], ACT.Sqrt, bias=eps_rms[:]).then_inc(rms_done, 1)
                act.wait_ge(znT_done, t + 1)
                for j in range(5):
                    src = PS[:, 4, j * P:(j + 1) * P] if j < 3 else PS[:, 5, (j - 3) * P:(j - 2) * P]
                    dst = qlat_hi[:, j, t * P:(t + 1) * P] if j < 3 else kvlatT[:, j - 3, t * P:(t + 1) * P]
                    gw = qg_col[:, j:j + 1] if j < 3 else kvg_col[:, j - 3:j - 2]
                    ins = nc.scalar.activation(dst, src, ACT.Copy, scale=gw)
                ins.then_inc(znT_out, 1)
            def split_wq(n):
                act.wait_ge(ld_wq, n * 48 + 48)
                nc.scalar.activation(wq_hi[:], wq_raw, ACT.Copy).then_inc(wq_split, 1)

            def copy_out(m, hn, hp):
                half, bank = m % 2, proj_bank(hn, m)
                ts, cols = slice(half * 4, half * 4 + 4), slice(half * 512, (half + 1) * 512)
                if m in (2, 3):
                    act.wait_ge(q_turned, hn * 2 + (m - 1))
                    nc.scalar.activation(qT_hi[hp][:, cols], qT_full[hp][:, cols], ACT.Copy).then_inc(q_split, 1)
                    return
                act.wait_ge(proj_done, hn * PROJ + (m + 1))
                if m < 2:
                    src = PS[:, bank, :].rearrange("p (t d) -> p t d", t=4)
                    nc.scalar.activation(k_h[:, ts, :], src[:, :, 0:NOPE], ACT.Copy)
                    ins = nc.scalar.activation(v_h[hp][:, ts, :], src[:, :, NOPE:], ACT.Copy)
                else:
                    ins = nc.scalar.activation(kT_hi[hp][0:NOPE, cols], PS[0:NOPE, bank, :], ACT.Copy)
                ins.then_inc(proj_out, 1)

            def softmax(h, hp, i):
                act.wait_ge(max_done, h * T + (i + 1))
                if not (isinstance(h, int) and h == 0 and i < 2):
                    act.wait_ge(pT_done, h * 12 + (group_at(i - 2) + (1 if 0 <= i - 2 < 4 else 2)))
                b, w = 2 * (i % 2), (i + 1) * P
                at0 = score_start(i)
                nc.scalar.activation(probs[i % 2][:, 0:w], PS[:, b:b + 2, :].rearrange("p a n -> p (a n)")[:, at0:at0 + w], ACT.Exp,
                                     bias=neg_max[:, i:i + 1], accum_out=row_sum[:, hp * T + i:hp * T + i + 1]).then_inc(exp_done, 1)

            def head(h, hp, nxt):
                for i in range(T):
                    if nxt and i >= 6:
                        copy_out(i - 2, h + 1, 1 - hp)
                    softmax(h, hp, i)
                    if nxt and i == 0:
                        split_wq(h + 1)
                    if nxt and 2 <= i < 6:
                        copy_out(i - 2, h + 1, 1 - hp)
                    if not nxt:
                        if i == 0:
                            act.wait_ge(ld_wo, 16)
                        nc.scalar.activation(wo_hi[:, i, :], wo_sb[:, i, :], ACT.Copy).then_inc(wo_split, 1)

            split_wq(0)
            act.wait_ge(tab_turned, 1)
            for half in range(2):
                cols = slice(half * 512, (half + 1) * 512)
                ins = nc.scalar.activation(q_turn[NOPE:P, cols], PS[0:2 * ROPE, 2 + half, :], ACT.Copy, scale=SCALE)
            ins.then_inc(tab_out, 1)
            copy_out(0, 0, 0)
            act.wait_ge(krT_done, 1)
            for half in range(2):
                cols = slice(half * 512, (half + 1) * 512)
                nc.scalar.activation(kT_hi[0][NOPE:P, cols], PS[0:2 * ROPE, half, :], ACT.Copy)
                ins = nc.scalar.activation(probs[0][NOPE:P, cols], PS[0:2 * ROPE, half, :], ACT.Copy)
            ins.then_inc(krT_out, 1)
            for m in range(1, PROJ):
                copy_out(m, 0, 0)
            nc.scalar.activation(kT_hi[1][NOPE:P, :], probs[0][NOPE:P, :], ACT.Copy).then_inc(krT_out, 1)
            act.wait_ge(krT_out, 2)
            act.wait_ge(krT_lo, 1)
            head(0, 0, True)
            with act.Fori(0, (H - 2) // 2) as hh:
                for q in range(2):
                    head(hh * 2 + (1 + q), 1 - q, True)
            head(H - 1, 1, False)

            act.wait_ge(s_done, H * T)

            def oT_copy(t):
                if t >= 2:
                    act.wait_ge(yo_done, t - 1)
                for half in range(2):
                    act.wait_ge(oT_done, 2 * t + half + 1)
                    nc.scalar.activation(oT_hi[t % 2][:, half * 4:half * 4 + 4, :],
                                         PS[:, half, :].rearrange("p (k q) -> p k q", k=4), ACT.Copy).then_inc(oT_out, 1)

            def h2T_copy(t):
                act.wait_ge(std_in, t + 1)
                nc.scalar.activation(std[:, t:t + 1], mv[:, t, 1:2], ACT.Sqrt, bias=eps_ln[:]).then_inc(std_done, 1)
                for half in range(2):
                    act.wait_ge(h2T_done, 2 * t + half + 1)
                    if half == 0 and t >= 1:
                        act.wait_ge(lg_done, t)
                    nc.scalar.activation(h2T[:, half * 4:half * 4 + 4, :],
                                         PS[:, 6 + half, :].rearrange("p (k q) -> p k q", k=4), ACT.Copy).then_inc(h2T_out, 1)

            oT_copy(0)
            for t in range(T):
                if t + 1 < T:
                    oT_copy(t + 1)
                if t >= 1:
                    h2T_copy(t - 1)
            h2T_copy(T - 1)

            act.wait_ge(rt_exp_in, 1)
            nc.scalar.activation(g_exp[:], g_exp[:], ACT.Exp)
            nc.scalar.activation(e_exp[:], e_dif[:], ACT.Exp).then_inc(rt_exp, 1)

            act.wait_ge(table_done, 1)
            rounds = act.value_load(rounds_i[0:1, 0:1], min_val=T - 1, max_val=TILES_MAX // 2 - 1)

            def rows_out(i, b):
                act.wait_ge(xgT_done, i * 2 + (b + 1))
                nc.scalar.activation(xgT[b][:, 0:4, :], PS[:, 0, :].rearrange("p (k q) -> p k q", k=4), ACT.Copy).then_inc(xgT_outA, 1)

            def silu(i, b):
                act.wait_ge(hid_done, i * 2 + (b + 1))
                nc.scalar.activation(sil[b], PS[:, 2 + b, 0:FF], ACT.Silu).then_inc(silu_done, 1)

            rows_out(0, 0)
            silu(0, 0)
            rows_out(0, 1)
            with act.Fori(0, rounds) as i:
                for b in range(2):
                    silu(i + b, 1 - b)
                    rows_out(i + 1, b)
            silu(rounds, 1)

            def scale(t):
                act.wait_ge(weighed, t + 1)
                act.wait_ge(rstd_done, t + 1)
                nc.scalar.activation(ya[t], ya[t], ACT.Copy, scale=rstd[:, T + t:T + t + 1]).then_inc(scaled, 1)

            for t in range(T):
                act.wait_ge(std_in, T + t + 1)
                nc.scalar.activation(std[:, T + t:T + t + 1], mv[:, T + t, 1:2], ACT.Sqrt, bias=eps_ln[:]).then_inc(std_done, 1)
                if 1 <= t < T - 1:
                    scale(t - 1)

        @block.vector
        def _(dve):
            links = [0]

            def then(ins):
                links[0] += 1
                ins.then_inc(vec, 1)
                dve.wait_ge(vec, links[0])

            dve_ = nc.vector
            dve_.memset(acc[:, 0:2 * D], 0.0).then_inc(acc_zero, 1)
            dve_.memset(acc[:, 2 * D:], 0.0).then_inc(acc_zero, 1)
            dve_.memset(eps_rms[:], RMS_EPS)
            then(dve_.memset(eps_ln[:], LN_EPS))
            dve.wait_ge(c_ready, 1)
            dve.wait_ge(ld_bmod[0], 16)
            dve.wait_ge(acc_zero, 2)

            def mod_step(n):
                sec, k = n // KD, n % KD
                a = acc[:, sec * 2 * D:(sec + 1) * 2 * D]
                dve.wait_ge(ld_mod[n % MOD_BUFS], 16 * (n // MOD_BUFS + 1))
                if n >= 1:
                    dve.wait_ge(mod_done, n)
                dve_.scalar_tensor_tensor(out=a, in0=mod_w(n), scalar=c_act[:, k:k + 1], in1=a,
                                          op0=ALU.mult, op1=ALU.add).then_inc(mod_done, 1)

            for n in range(KD):
                mod_step(n)
            dve.wait_ge(cols_done, 1)
            dve_.tensor_copy(mod_cols[:, 0:KD], PS[:, 0, 0:KD])
            dve_.tensor_scalar(mod_cols[:, KD:], PS[:, 0, KD:2 * KD], 1.0, None, ALU.add).then_inc(cols_out, 1)

            dve.wait_ge(consts, 1)
            dve.wait_ge(ld_pos, 16)
            then(dve_.tensor_copy(pos_f[:], pos_i[:]))
            then(dve_.tensor_tensor(ang[:], pos_f[:].unsqueeze(2).broadcast_to([P, T, HR]),
                                    freq[:].unsqueeze(1).broadcast_to([P, T, HR]), ALU.mult))
            then(dve_.tensor_scalar(turns[:], ang[:], float(1.0 / TWO_PI), ROUND, ALU.mult, ALU.add))
            then(dve_.tensor_scalar(turns[:], turns[:], -ROUND, None, ALU.add))
            for part in (TWO_PI_HI, TWO_PI_MID, TWO_PI_LO):
                then(dve_.scalar_tensor_tensor(out=ang[:], in0=turns[:], scalar=-part, in1=ang[:], op0=ALU.mult, op1=ALU.add))
            then(dve_.tensor_scalar(turns[:], ang[:], float(np.pi / 2), None, ALU.add))
            then(dve_.tensor_scalar(cos_t[:], turns[:], float(np.pi), -TWO_PI, ALU.is_gt, ALU.mult))
            then(dve_.tensor_tensor(turns[:], turns[:], cos_t[:], ALU.add))
            then(dve_.tensor_scalar(turns[:], turns[:], PI_F, -PI_F, ALU.min, ALU.max))
            dve_.tensor_scalar(ang[:], ang[:], PI_F, -PI_F, ALU.min, ALU.max).then_inc(ang_done, 1)

            def latent_rest(t):
                dve.wait_ge(znT_out, t + 1)
                cols = slice(t * P, (t + 1) * P)
                for j in range(3):
                    ins = dve_.scalar_tensor_tensor(out=qlat_lo[:, j, cols], in0=PS[:, 4, j * P:(j + 1) * P], scalar=qg_col[:, j:j + 1],
                                                    in1=qlat_hi[:, j, cols].bitcast(F32), op0=ALU.mult, op1=ALU.subtract)
                ins.then_inc(zlo_out, 1)

            for t in range(T):
                dve.wait_ge(z_done, t + 1)
                if t >= 2:
                    dve.wait_ge(znT_done, t - 1)
                b = 2 * (t % 2)
                z_flat = PS[:, b:b + 2, :].rearrange("p a n -> p (a n)")
                dve_.tensor_copy(k_rope[:, t, :], z_flat[:, QL + KVL:ZW])
                dve_.tensor_copy(zs[t % 2][:, 0:QL + KVL], z_flat[:, 0:QL + KVL]).then_inc(z_out, 1)
                if t == 0:
                    dve.wait_ge(ld_bmod[1], 16)
                steps = list(range(KD + 3 * t, min(KD + 3 * t + 3, MOD_STEPS)))
                for n in steps[:1]:
                    mod_step(n)
                dve.wait_ge(rms_done, t + 1)
                then(dve_.reciprocal(rrms[:, t, :], rms[:, t, :]))
                dve_.tensor_scalar(zs[t % 2][:, 0:QL], zs[t % 2][:, 0:QL], rrms[:, t, 0:1], None, ALU.mult)
                dve_.tensor_scalar(zs[t % 2][:, QL:QL + KVL], zs[t % 2][:, QL:QL + KVL], rrms[:, t, 1:2], None,
                                   ALU.mult).then_inc(zn_done, 1)
                if t >= 1:
                    latent_rest(t - 1)
                for n in steps[1:]:
                    mod_step(n)
            latent_rest(T - 1)
            then(dve_.memset(q_turn[0:NOPE, :], SCALE))

            def row_max(h, i):
                dve.wait_ge(s_done, h * T + (i + 1))
                b, w, at0 = 2 * (i % 2), (i + 1) * P, score_start(i)
                dve_.tensor_reduce(neg_max[:, i:i + 1], PS[:, b:b + 2, :].rearrange("p a n -> p (a n)")[:, at0:at0 + w], AX.X, ALU.max,
                                   negate=True).then_inc(max_done, 1)

            def turned(h, i):
                for g in range(1 if i < 4 else 2):
                    n = group_at(i) + g
                    dve.wait_ge(pT_done, h * 12 + (n + 1))
                    if g == 0 and not (isinstance(h, int) and h == 0 and i < 2):
                        dve.wait_ge(o_done, h * T + (i - 1))
                    k0, k1 = 4 * g, min(4 * g + 4, i + 1)
                    dve_.tensor_copy(pT[i % 2][:, k0:k1, :],
                                     PS[:, 4 + n % 2, 0:(k1 - k0) * P].rearrange("p (k q) -> p k q", k=k1 - k0)).then_inc(pT_out, 1)

            def turn_q(m, hn, hp):
                dve.wait_ge(proj_done, hn * PROJ + (m + 1))
                cols = slice((m % 2) * 512, (m % 2) * 512 + 512)
                dve_.tensor_tensor(qT_full[hp][:, cols], PS[:, proj_bank(hn, m), :], q_turn[:, cols], ALU.mult).then_inc(q_turned, 1)

            def rest(m, hn, hp):
                dve.wait_ge(proj_out, hn * 4 + (m - 1))
                cols = slice((m % 2) * 512, (m % 2) * 512 + 512)
                dve_.tensor_tensor(kT_lo[hp][0:NOPE, cols], PS[0:NOPE, proj_bank(hn, m), :], kT_hi[hp][0:NOPE, cols].bitcast(F32),
                                   ALU.subtract).then_inc(lo_out, 1)

            def finish(h, hp, i):
                dve.wait_ge(exp_done, h * T + (i + 1))
                dve_.reciprocal(inv_sum[:, i:i + 1], row_sum[:, hp * T + i:hp * T + i + 1]).then_inc(inv_done, 1)
                dve.wait_ge(o_done, h * T + (i + 1))
                dve.wait_ge(inv_done, h * T + (i + 1))
                dve_.tensor_scalar(o_tok[:, i, bass.ds(h * VH, VH)], PS[:, 7, 0:VH], inv_sum[:, i:i + 1], None,
                                   ALU.mult).then_inc(o_out, 1)

            def mod_row(m):
                half = slice((m % 2) * 512, (m % 2) * 512 + 512)
                src = PS[:, 6, :]
                dve.wait_ge(bc_done, m + 1)
                if m < 2:
                    ins = dve_.tensor_scalar(g1p[:, half], src, 1.0, None, ALU.add)
                elif m < 4:
                    if m == 2:
                        dve.wait_ge(ld_ln, 32)
                    dve_.scalar_tensor_tensor(out=A2[:, half], in0=src, scalar=1.0, in1=Ga[:, half], op0=ALU.add, op1=ALU.mult)
                    ins = dve_.scalar_tensor_tensor(out=B2[:, half], in0=src, scalar=1.0, in1=Ba[:, half], op0=ALU.add, op1=ALU.mult)
                elif m < 6:
                    dve.wait_ge(bc_out, m - 1)
                    ins = dve_.tensor_tensor(B2[:, half], src, B2[:, half], ALU.add)
                else:
                    ins = dve_.tensor_scalar(g2p[:, half], src, 1.0, None, ALU.add)
                ins.then_inc(bc_out, 1)

            def head(h, hp, first, nxt):
                for i in range(T):
                    row_max(h, i)
                    if nxt and 4 <= i < 6:
                        turn_q(i - 2, h + 1, 1 - hp)
                    if nxt and i >= 6:
                        rest(i - 2, h + 1, 1 - hp)
                    if i >= 1:
                        turned(h, i - 1)
                    elif not first:
                        turned(h - 1, T - 1)
                    if i >= 2:
                        finish(h, hp, i - 2)
                    elif not first:
                        finish(h - 1, 1 - hp, T - 2 + i)
                    if not nxt:
                        mod_row(i)

            dve.wait_ge(krT_out, 1)
            dve_.tensor_tensor(kT_lo[0][NOPE:P, :], probs[0][NOPE:P, :], kT_hi[0][NOPE:P, :].bitcast(F32),
                               ALU.subtract).then_inc(krT_lo, 1)
            dve.wait_ge(tab_out, 1)
            turn_q(2, 0, 0)
            turn_q(3, 0, 0)
            rest(4, 0, 0)
            rest(5, 0, 0)
            dve.wait_ge(krT_lo, 1)
            dve_.tensor_copy(kT_lo[1][NOPE:P, :], kT_lo[0][NOPE:P, :].bitcast(F32)).then_inc(krT_lo, 1)
            head(0, 0, True, True)
            with dve.Fori(0, (H - 2) // 2) as hh:
                for q in range(2):
                    head(hh * 2 + (1 + q), 1 - q, False, True)
            def oT_rests(t):
                for half in range(2):
                    ks = slice(half * 4, half * 4 + 4)
                    dve.wait_ge(oT_out, 2 * t + half + 1)
                    if t >= 2 and half == 0:
                        dve.wait_ge(yo_done, t - 1)
                    dve_.tensor_tensor(oT_lo[t % 2][:, ks, :], PS[:, half, :].rearrange("p (k q) -> p k q", k=4),
                                       oT_hi[t % 2][:, ks, :].bitcast(F32), ALU.subtract).then_inc(oT_rest, 1)

            head(H - 1, 1, False, False)
            oT_rests(0)
            turned(H - 1, T - 1)
            finish(H - 1, 1, T - 2)
            finish(H - 1, 1, T - 1)

            dve.wait_ge(bc_out, 8)
            then(dve_.tensor_scalar(Ga, Ga, ALPHA, None, ALU.mult))
            then(dve_.tensor_scalar(Ba, Ba, ALPHA, None, ALU.mult))

            def normalise(t, r):
                dve_.bn_stats(bn[:, 0, :], r[:, 0:512])
                then(dve_.bn_stats(bn[:, 1, :], r[:, 512:D]))
                dve_.bn_aggr(mv[:, t, :], bn[:].rearrange("p a b -> p (a b)")).then_inc(std_in, 1)
                dve.wait_ge(std_done, t + 1)
                then(dve_.reciprocal(rstd[:, t:t + 1], std[:, t:t + 1]))
                then(dve_.tensor_scalar(r, r, mv[:, t, 0:1], rstd[:, t:t + 1], ALU.subtract, ALU.mult))

            def choose(t):
                dve.wait_ge(lg_done, t + 1)
                dve_.tensor_tensor(gl[:, t, 0:G], PS[:, 6, 0:G], b_rt[:, 0:G], ALU.add)
                dve_.tensor_tensor(logits[:, t, :], PS[:, 6, 0:G + E], b_rt[:], ALU.add).then_inc(lg_out, 1)
                dve.wait_ge(lg_out, t + 1)
                then(dve_.max(g_top[:, t, :], gl[:, t, :]))
                then(dve_.max_index(g_idx[:, t, :], g_top[:, t, :], gl[:, t, :]))
                then(dve_.tensor_copy(g_idf[:, t:t + 1], g_idx[:, t, 0:1]))
                then(dve_.tensor_scalar(g_hot[:, t, :], iota_row[:, 0:G], g_idf[:, t:t + 1], None, ALU.is_equal))
                then(dve_.tensor_tensor(e_sel, logits[:, t, G:].rearrange("p (g e) -> p g e", g=G),
                                        g_hot[:, t, :].unsqueeze(2).broadcast_to([P, G, EPG]), ALU.mult))
                then(dve_.tensor_reduce(e_in[:, t, :], e_sel.rearrange("p g e -> p e g"), AX.X, ALU.add))
                then(dve_.max(e_top[:, t, :], e_in[:, t, :]))
                dve_.max_index(e_idx[:, t, :], e_top[:, t, :], e_in[:, t, :])

            then(dve_.memset(gl[:], -BIG))
            for t in range(T):
                r = r_buf[t % 2]
                if t + 1 < T:
                    oT_rests(t + 1)
                if t >= 2:
                    choose(t - 2)
                dve.wait_ge(yo_done, t + 1)
                b = 2 + 2 * (t % 2)
                y = PS[:, b:b + 2, :].rearrange("p a n -> p (a n)")
                dve.wait_ge(ld_xs[t % 2], 16 * (t // 2 + 1))
                if t >= 2:
                    dve.wait_ge(xa_done, t - 1)
                dve_.tensor_tensor(r, y, g1p, ALU.mult).then_inc(yo_used, 1)
                dve.wait_ge(yo_used, t + 1)
                then(dve_.scalar_tensor_tensor(out=r, in0=xs[t % 2], scalar=ALPHA, in1=r, op0=ALU.mult, op1=ALU.add))
                normalise(t, r)
                if t >= 2:
                    dve.wait_ge(h2_stored[t % 2], 16 * (t // 2))
                    dve.wait_ge(h2T_done, 2 * (t - 1))
                then(dve_.tensor_tensor(h2[t % 2], r, A2, ALU.mult))
                dve_.tensor_tensor(h2[t % 2], h2[t % 2], B2, ALU.add).then_inc(h2_done, 1)
            choose(T - 2)
            for b in range(2):
                ins = dve_.memset(xg[b], 0.0)
            then(ins)
            choose(T - 1)

            dve.wait_ge(xa_done, T)
            then(dve_.memset(idx_f[:], 0.0))
            dve_.tensor_tensor(g_exp[:], logits[:, :, 0:G], g_top[:, :, 0:1].broadcast_to([P, T, G]), ALU.subtract)
            dve_.tensor_tensor(e_dif[:], e_top[:, :, 1], e_top[:, :, 0], ALU.subtract).then_inc(rt_exp_in, 1)
            for a in range(TOPK):
                then(dve_.tensor_copy(e_idf[:, a, :], e_idx[:, :, a]))
                then(dve_.scalar_tensor_tensor(out=e_idf[:, a, :], in0=g_idf[:], scalar=float(EPG), in1=e_idf[:, a, :],
                                               op0=ALU.mult, op1=ALU.add))
                then(dve_.tensor_tensor(hot[:, a], iota_row[:, 0:E].unsqueeze(1).broadcast_to([P, T, E]),
                                        e_idf[:, a, :].unsqueeze(2).broadcast_to([P, T, E]), ALU.is_equal))
            dve_.tensor_tensor(member[:], hot[:, 0], hot[:, 1], ALU.add).then_inc(member_done, 1)
            dve.wait_ge(rt_exp, 1)
            then(dve_.tensor_reduce(g_den[:], g_exp[:], AX.X, ALU.add))
            then(dve_.reciprocal(g_p[:], g_den[:]))
            then(dve_.tensor_scalar(e_den[:], e_exp[:], 1.0, None, ALU.add))
            then(dve_.reciprocal(e_den[:], e_den[:]))
            then(dve_.tensor_tensor(wts[:, 0, :], e_den[:], g_p[:], ALU.mult))
            then(dve_.tensor_tensor(wts[:, 1, :], wts[:, 0, :], e_exp[:], ALU.mult))
            dve.wait_ge(rank_done, 1)
            then(dve_.tensor_copy(count[:], PS[:, 1, 0:E]))
            then(dve_.tensor_tensor(over, count[:].unsqueeze(2).broadcast_to([P, E, T]),
                                    iota_tiles[:].unsqueeze(1).broadcast_to([P, E, T]), ALU.is_gt))
            then(dve_.tensor_reduce(n_tiles[:], over, AX.X, ALU.add))
            then(dve_.tensor_tensor_scan(tile_end[:], ones[:, 0:E], n_tiles[:], 0.0, ALU.mult, ALU.add))
            then(dve_.tensor_scalar(te_cmp, tile_end[:], row_id[:, 0:1], None, ALU.is_lt))
            then(dve_.tensor_reduce(te_col[:], te_cmp, AX.X, ALU.add))
            dve_.tensor_scalar(te_col[:], te_col[:], float(E - 1), None, ALU.min).then_inc(te_in, 1)
            then(dve_.tensor_scalar(rounds_f[:, 0:1], tile_end[0:1, E - 1:E], 0.5, 0.25, ALU.mult, ALU.add))
            then(dve_.tensor_scalar(rounds_f[:, 0:1], rounds_f[:, 0:1], ROUND, -ROUND - 1.0, ALU.add, ALU.add))
            then(dve_.tensor_scalar(rounds_f[:, 1:2], rounds_f[:, 0:1], -1.0, None, ALU.add))
            dve_.tensor_copy(rounds_i[:], rounds_f[:])
            dve.wait_ge(te_turned, 1)
            dve_.tensor_copy(te_i[:], PS[0:1, 5, 0:LOOP_TABLE]).then_inc(tiles_known, 1)
            then(dve_.tensor_tensor(base[:], tile_end[:], n_tiles[:], ALU.subtract))
            then(dve_.scalar_tensor_tensor(out=place, in0=base[:].unsqueeze(1).broadcast_to([P, T, E]), scalar=float(P),
                                           in1=PS[:, 0, 0:T * E].rearrange("p (t e) -> p t e", t=T), op0=ALU.mult, op1=ALU.add))
            for a in range(TOPK):
                then(dve_.tensor_tensor(picked[:, a], hot[:, a], place, ALU.mult))
            then(dve_.tensor_reduce(slot[:], picked, AX.X, ALU.add))
            then(dve_.tensor_scalar(slot_dv[:], slot[:], 1.0 / P, -0.5 + 0.5 / P, ALU.mult, ALU.add))
            then(dve_.tensor_scalar(slot_dv[:], slot_dv[:], ROUND, None, ALU.add))
            then(dve_.tensor_scalar(slot_dv[:], slot_dv[:], -ROUND, None, ALU.add))
            dve_.scalar_tensor_tensor(out=slot_in[:], in0=slot_dv[:], scalar=-float(P), in1=slot[:], op0=ALU.mult,
                                      op1=ALU.add).then_inc(place_known, 1)
            then(dve_.tensor_tensor(hot_dv[:, 1], iota_row[:, 0:TILES_MAX].unsqueeze(1).broadcast_to([P, TOPK * T, TILES_MAX]),
                                    slot_dv[:].rearrange("p a t -> p (a t)").unsqueeze(2).broadcast_to([P, TOPK * T, TILES_MAX]),
                                    ALU.is_equal))
            dve_.tensor_tensor(hot_dv[:, 0], hot_dv[:, 1],
                               row_id[:].unsqueeze(2).broadcast_to([P, TOPK * T, TILES_MAX]), ALU.mult)
            dve.wait_ge(place_known, 1)
            for n in range(0, TOPK * T, 4):
                a, ts = n // T, slice(n % T, n % T + 4)
                dve_.tensor_tensor(hot_in[:, a, ts, :], iota_row[:].unsqueeze(1).broadcast_to([P, 4, P]),
                                   slot_in[:, a, ts].unsqueeze(2).broadcast_to([P, 4, P]), ALU.is_equal).then_inc(hot_done, 1)
            dve_.tensor_tensor(hot_dv[:, 1], hot_dv[:, 1],
                               wts[:].rearrange("p a t -> p (a t)").unsqueeze(2).broadcast_to([P, TOPK * T, TILES_MAX]),
                               ALU.mult).then_inc(hot_weighed, 1)
            dve.wait_ge(idx_acc, 1)
            then(dve_.tensor_copy(idx_f[:, 0:TILES_MAX], PS[:, 2, 0:TILES_MAX]))
            then(dve_.tensor_scalar(pad[:], idx_f[:], 0.0, 4.0 * S, ALU.is_equal, ALU.mult))
            then(dve_.scalar_tensor_tensor(out=row_f[:], in0=idx_f[:], scalar=-1.0, in1=pad[:], op0=ALU.add, op1=ALU.add))
            then(dve_.tensor_copy(dst_u[:], row_f[:]))
            then(dve_.tensor_scalar(past[:], row_f[:], float(S) - 0.5, -float(S), ALU.is_gt, ALU.mult))
            then(dve_.tensor_tensor(row_f[:], row_f[:], past[:], ALU.add))
            dve_.tensor_copy(idx_u[:], row_f[:]).then_inc(table_done, 1)
            dve.wait_ge(w_acc, 1)
            then(dve_.tensor_copy(slot_w[:, 0:TILES_MAX], PS[:, 3, 0:TILES_MAX]))

            dve.wait_ge(table_done, 1)
            rounds = dve.value_load(rounds_i[0:1, 0:1], min_val=T - 1, max_val=TILES_MAX // 2 - 1)

            def rows_out(i, b):
                dve.wait_ge(xgT_done, i * 2 + (b + 1))
                dve_.tensor_copy(xgT[b][:, 4:8, :], PS[:, 1, :].rearrange("p (k q) -> p k q", k=4)).then_inc(xgT_outV, 1)

            def gated(i, b):
                dve.wait_ge(silu_done, i * 2 + (b + 1))
                dve_.tensor_tensor(he[b], PS[:, 2 + b, FF:], sil[b], ALU.mult).then_inc(he_done, 1)

            def hidden_out(i, b):
                dve.wait_ge(heT_done, i * 2 + (b + 1))
                dve_.tensor_copy(heT[b], PS[:, 4, 0:2 * P].rearrange("p (k q) -> p k q", k=2)).then_inc(heT_out, 1)

            def result_out(i, b):
                dve.wait_ge(ye_done, i * 2 + (b + 1))
                dve.wait_ge(y_free, i * 2 + (b + 1))
                dve_.scalar_tensor_tensor(out=y_e[b], in0=PS[:, 6:8, :].rearrange("p a n -> p (a n)"),
                                          scalar=slot_w[:, bass.ds(i * 2 + b, 1)], in1=g2p, op0=ALU.mult, op1=ALU.mult).then_inc(ye_out, 1)

            dve.sem_inc(ye_out, 1)
            rows_out(0, 0)
            gated(0, 0)
            rows_out(0, 1)
            with dve.Fori(0, rounds) as i:
                for b in range(2):
                    hidden_out(i, b)
                    gated(i + b, 1 - b)
                    rows_out(i + 1, b)
                    result_out(i, b)
            hidden_out(rounds, 0)
            gated(rounds, 1)
            result_out(rounds, 0)
            hidden_out(rounds, 1)
            result_out(rounds, 1)

            dve.wait_ge(ld_ln2, 32)

            def residual(t):
                if t % 2 == 0:
                    dve.wait_ge(summed, t // 2 + 1)
                    r = PS[:, t:t + 2, :].rearrange("p a n -> p (a n)")
                else:
                    dve.wait_ge(added, t // 2 + 1)
                    r = ya[t]
                    then(dve_.tensor_tensor(r, r, xa[:, t, :], ALU.add))
                dve_.bn_stats(bn[:, 0, :], r[:, 0:512])
                then(dve_.bn_stats(bn[:, 1, :], r[:, 512:D]))
                dve_.bn_aggr(mv[:, T + t, :], bn[:].rearrange("p a b -> p (a b)")).then_inc(std_in, 1)
                dve.wait_ge(std_in, T + t + 1)
                dve_.scalar_tensor_tensor(out=ya[t], in0=r, scalar=mv[:, T + t, 0:1], in1=lng2,
                                          op0=ALU.subtract, op1=ALU.mult).then_inc(weighed, 1)

            def invert(t):
                dve.wait_ge(std_done, T + t + 1)
                dve_.reciprocal(rstd[:, T + t:T + t + 1], std[:, T + t:T + t + 1]).then_inc(rstd_done, 1)

            for t in range(T):
                residual(t)
                if t >= 1:
                    invert(t - 1)
            for t in range(T - 2, T):
                if t == T - 1:
                    invert(t)
                dve.wait_ge(rstd_done, t + 1)
                dve.wait_ge(weighed, t + 1)
                dve_.scalar_tensor_tensor(out=yb[t], in0=ya[t], scalar=rstd[:, T + t:T + t + 1], in1=lnb2,
                                          op0=ALU.mult, op1=ALU.add).then_inc(last_out, 1)

        @block.gpsimd
        def _(pool):
            links = [0]

            def then(ins):
                links[0] += 1
                ins.then_inc(pol, 1)
                pool.wait_ge(pol, links[0])

            g_ = nc.gpsimd
            g_.memset(ident[:], 0.0)
            g_.memset(ones[:], 1.0)
            g_.memset(causal_bf[:], 0.0)
            g_.memset(ident_bf[:], 0.0)
            then(g_.memset(ones_bf[:], 1.0))
            for m in (ident, ident_bf):
                then(g_.affine_select(out=m[:], in_=m[:], compare_op=ALU.not_equal, fill=1.0, base=0,
                                      pattern=[[-1, P]], channel_multiplier=1))
            then(g_.affine_select(out=causal_bf[:], in_=causal_bf[:], compare_op=ALU.is_ge, fill=-BIG, base=0,
                                  pattern=[[-1, P]], channel_multiplier=1))
            then(g_.affine_select(out=before_bf[:], in_=ones_bf[:], compare_op=ALU.is_gt, fill=0.0, base=0,
                                  pattern=[[1, P]], channel_multiplier=-1))
            then(g_.iota(iota_row[:], [[1, P]], base=0, channel_multiplier=0, allow_small_or_imprecise_dtypes=True))
            then(g_.iota(iota_tiles[:], [[P, T]], base=0, channel_multiplier=0, allow_small_or_imprecise_dtypes=True))
            then(g_.iota(row_id[:], [[P, TOPK * T]], base=1, channel_multiplier=1, allow_small_or_imprecise_dtypes=True))
            for r in range(HR):
                ins = g_.memset(freq[:, r:r + 1], float(inv_freq[r]))
            then(ins)
            pool.sem_inc(consts, 1)

            pool.wait_ge(trig_done, 1)
            pool.wait_ge(z_out, T)
            x1, x2 = k_rope[:, :, 0:HR], k_rope[:, :, HR:ROPE]
            g_.tensor_tensor(rope_k[:, 0], x1, cos_t[:], ALU.mult)
            g_.tensor_tensor(rope_k[:, 1], x2, sin_t[:], ALU.mult)
            g_.tensor_tensor(rope_k[:, 2], x1, sin_t[:], ALU.mult)
            then(g_.tensor_tensor(rope_k[:, 3], x2, cos_t[:], ALU.mult))
            for at0 in (0, ROPE):
                g_.tensor_tensor(k_rot[:, :, at0:at0 + HR], rope_k[:, 0], rope_k[:, 1], ALU.subtract)
                ins = g_.tensor_tensor(k_rot[:, :, at0 + HR:at0 + ROPE], rope_k[:, 2], rope_k[:, 3], ALU.add)
            ins.then_inc(krot_done, 1)

            with pool.Fori(0, H // 2) as hh:
                for hp in range(2):
                    pool.wait_ge(wq_split, hh * 2 + (hp + 1))
                    g_.tensor_tensor(wq_lo[:], wq_raw, wq_hi[:].bitcast(F32), ALU.subtract).then_inc(wq_rest, 1)
                    for half in range(2):
                        pool.wait_ge(q_split, hh * 4 + (2 * hp + half + 1))
                        cols = slice(half * 512, (half + 1) * 512)
                        g_.tensor_tensor(qT_lo[hp][:, cols], qT_full[hp][:, cols], qT_hi[hp][:, cols].bitcast(F32),
                                         ALU.subtract).then_inc(q_rest, 1)

            for k in range(KD):
                pool.wait_ge(wo_split, k + 1)
                g_.tensor_tensor(wo_lo[:, k, :], wo_sb[:, k, :], wo_hi[:, k, :].bitcast(F32), ALU.subtract).then_inc(wo_rest, 1)

            for t in range(T):
                pool.wait_ge(h2_done, t + 1)
                pool.wait_ge(oT_done, 2 * t + 2)
                then(g_.tensor_tensor(xa[:, t, :], r_buf[t % 2], Ga, ALU.mult))
                g_.tensor_tensor(xa[:, t, :], xa[:, t, :], Ba, ALU.add).then_inc(xa_done, 1)

            pool.wait_ge(xa_done, T)
            pool.wait_ge(h2_stored[0], 16 * (T // 2))
            pool.wait_ge(h2_stored[1], 16 * (T // 2))
            pool.wait_ge(h2T_done, 2 * T)
            pool.wait_ge(table_done, 1)
            rounds = pool.value_load(rounds_i[0:1, 0:1], min_val=T - 1, max_val=TILES_MAX // 2 - 1)
            rows_all = pool.snap(rounds * 16 + 32)
            y_both = pool.snap(rounds * 16 + 16)

            def gather(b):
                g_.indirect_dma_start(xg[b], None, h2_rows, bass.IndirectOffsetOnAxis(idx_now[b][:, 0:1], 0),
                                      bounds_check=S - 1, oob_is_err=False).then_inc(gathered[b], 16)

            def scatter(i, c, ahead):
                n, b = i * 2 + c, c % 2
                if ahead:
                    pool.wait_ge(xgT_done, n + 2)
                    g_.tensor_copy(idx_now[1 - b][:], idx_u[:, bass.ds(n + 3, 1)])
                g_.tensor_copy(dst_now[b][:], dst_u[:, bass.ds(n, 1)]).then_inc(idx_set, 1)
                pool.wait_ge(idx_set, n + 2)
                if ahead:
                    pool.sem_inc(idx_seen, 1)
                    gather(1 - b)
                pool.wait_ge(ye_out, n + 2)
                pool.sem_inc(idx_seen, 1)
                g_.indirect_dma_start(y_rows, bass.IndirectOffsetOnAxis(dst_now[b][:, 0:1], 0), y_e[b], None,
                                      bounds_check=TOPK * S - 1, oob_is_err=False).then_inc(y_stored[b], 16)
                if c >= 1:
                    pool.wait_ge(y_stored[1 - b], i * 16 + 16)
                    pool.sem_inc(y_free, 1)

            pool.sem_inc(y_free, 2)
            g_.tensor_copy(idx_now[0][:], idx_u[:, 0:1])
            g_.tensor_copy(idx_now[1][:], idx_u[:, 1:2]).then_inc(idx_set, 1)
            pool.wait_ge(idx_set, 1)
            gather(0)
            gather(1)
            pool.wait_ge(xgT_done, 1)
            then(g_.tensor_copy(idx_now[0][:], idx_u[:, 2:3]))
            gather(0)
            scatter(0, 0, True)
            with pool.Fori(0, rounds) as i:
                for c in (1, 2):
                    scatter(i, c, True)
            scatter(rounds, 1, False)
            pool.wait_ge(y_stored[1], y_both)
            pool.wait_ge(gathered[0], rows_all)
            pool.wait_ge(gathered[1], rows_all)
            pool.sem_inc(y_all, 1)

            def add_bias(t):
                pool.wait_ge(scaled, t + 1)
                g_.tensor_tensor(yb[t], ya[t], lnb2, ALU.add).then_inc(out_done, 1)

            pool.wait_ge(ld_ln2, 32)
            for t in range(1, T, 2):
                pool.wait_ge(ld_y[t], 32)
                g_.tensor_tensor(ya[t], ya[t], yb[t], ALU.add).then_inc(added, 1)
                for u in range(max(0, t - 3), t - 1):
                    add_bias(u)


def proj_bank(h, m):
    return (6, 7, 4, 5)[m % 4] if isinstance(h, int) and h == 0 else 6


def score_start(i):
    return P if i == 4 else 0


def group_at(i):
    return sum(1 if j < 4 else 2 for j in range(i)) if i >= 0 else -sum(1 if j % T < 4 else 2 for j in range(i, 0))


_INS = ["x", "c", "positions", "w_mod", "b_mod", "ln_g", "ln_b", "w_in", "q_norm_g", "kv_norm_g", "w_uq", "w_ukv", "w_o",
        "w_group_router", "b_group_router", "w_expert_router", "b_expert_router", "w_gate", "w_up", "w_down"]


def kernel(**inputs):
    import concourse.bacc as _bacc
    from concourse.bass_utils import run_bass_kernel_spmd as _run

    nc = _bacc.Bacc("TRN2", target_bir_lowering=False, num_devices=1)
    arrays, args = {}, []
    for name in _INS:
        a = np.ascontiguousarray(inputs[name])
        arrays[f"in_{name}_dram"] = a
        args.append(nc.dram_tensor(f"in_{name}_dram", a.shape, mybir.dt.from_np(a.dtype), kind="ExternalInput").ap())
    args.append(nc.dram_tensor("out_dram", (1, S, D), F32, kind="ExternalOutput").ap())
    build_trunk(nc, *args)
    r = _run(nc, [arrays], core_ids=[0])
    return r.results[0]["out_dram"]
```
